# Optimizing a Trainium2 kernel written in Bass

```python
import jax, jax.numpy as jnp
from jax import lax
import numpy as np

D_MODEL = 1024
BATCH = 1
SEQ = 512
DEPTH = 1

CHUNK = 64
POOL_WIDTH = 1024
POOL_WINDOWS = (2, 4, 8, 16)
POOL_GROUPS = len(POOL_WINDOWS)
POOL_GROUP_WIDTH = POOL_WIDTH // POOL_GROUPS
HGRN_WIDTH = 1024
HGRN_EXPAND = 128
HGRN_HEADS = HGRN_WIDTH // HGRN_EXPAND
HGRN_HEAD_V = HGRN_WIDTH // HGRN_HEADS
MIX_WIDTH = POOL_WIDTH + HGRN_WIDTH
IN_WIDTH = 2 * POOL_WIDTH + 4 * HGRN_WIDTH
EPS = 1e-6


def rms_norm(x, w):
    xf = x.astype(jnp.float32)
    xf = xf * lax.rsqrt(jnp.mean(xf * xf, axis=-1, keepdims=True) + EPS)
    return xf * w.astype(jnp.float32)

def multiscale_pool(u, pool_w, pool_scale):
    B, S, _ = u.shape
    cs = jnp.cumsum(u, axis=1)
    count = jnp.arange(1, S + 1, dtype=jnp.float32)[None, :, None]
    outs = []
    for g, w in enumerate(POOL_WINDOWS):
        lo, hi = g * POOL_GROUP_WIDTH, (g + 1) * POOL_GROUP_WIDTH
        cs_g = cs[..., lo:hi]
        prev = jnp.pad(cs_g, ((0, 0), (w, 0), (0, 0)))[:, :S]
        mean = (cs_g - prev) / jnp.minimum(count, float(w))
        outs.append(mean - u[..., lo:hi])
    d = jnp.stack(outs, axis=2)
    y = jnp.einsum('bsgc,gcd->bsgd', d, pool_w.astype(jnp.float32))
    return y.reshape(B, S, POOL_WIDTH) * pool_scale.astype(jnp.float32)

def _to_chunks(t):
    B, S, H, D = t.shape
    return t.reshape(B, S // CHUNK, CHUNK, H, D).transpose(1, 0, 3, 2, 4)

def hgrn2_chunkwise(q, log_f, k, v):
    B, S, H, dk = q.shape
    dv = v.shape[-1]
    causal = jnp.tril(jnp.ones((CHUNK, CHUNK), dtype=bool))[:, :, None]

    def step(state, xs):
        qc, lfc, kc, vc = xs
        b = jnp.cumsum(lfc, axis=2)
        o_inter = jnp.einsum('bhtk,bhkv->bhtv', qc * jnp.exp(b), state)
        diff = b[:, :, :, None, :] - b[:, :, None, :, :]
        decay = jnp.exp(jnp.where(causal, diff, -jnp.inf))
        attn = jnp.einsum('bhtk,bhsk,bhtsk->bhts', qc, kc, decay)
        o_intra = jnp.einsum('bhts,bhsv->bhtv', attn, vc)
        b_last = b[:, :, -1, :]
        k_dec = kc * jnp.exp(b_last[:, :, None, :] - b)
        new_state = jnp.exp(b_last)[..., None] * state + jnp.einsum('bhsk,bhsv->bhkv', k_dec, vc)
        return new_state, o_inter + o_intra

    state0 = jnp.zeros((B, H, dk, dv), jnp.float32)
    _, o = lax.scan(step, state0, (_to_chunks(q), _to_chunks(log_f), _to_chunks(k), _to_chunks(v)))
    return o.transpose(1, 0, 3, 2, 4).reshape(B, S, H, dv)

def first_inputs(seed: int = 0) -> dict:
    key = jax.random.key(seed)
    ks = jax.random.split(key, 12)
    f32 = jnp.float32
    x = jax.random.normal(ks[0], (BATCH, SEQ, D_MODEL), f32)
    c = jax.random.normal(ks[1], (BATCH, D_MODEL), f32)
    norm_pre_w = 1.0 + 0.05 * jax.random.normal(ks[2], (DEPTH, D_MODEL), f32)
    ada_w = 0.5 * D_MODEL ** -0.5 * jax.random.normal(ks[3], (DEPTH, D_MODEL, 3 * D_MODEL), f32)
    ada_b = 0.01 * jax.random.normal(ks[4], (DEPTH, 3 * D_MODEL), f32)
    w_in = D_MODEL ** -0.5 * jax.random.normal(ks[5], (DEPTH, D_MODEL, IN_WIDTH), f32)
    pool_w = POOL_GROUP_WIDTH ** -0.5 * jax.random.normal(
        ks[6], (DEPTH, POOL_GROUPS, POOL_GROUP_WIDTH, POOL_GROUP_WIDTH), f32)
    pool_scale = 1.0 + 0.05 * jax.random.normal(ks[7], (DEPTH, POOL_WIDTH), f32)
    hgrn_lower_bounds = 0.5 * jax.random.normal(ks[8], (DEPTH, HGRN_WIDTH), f32)
    hgrn_norm_w = 1.0 + 0.05 * jax.random.normal(ks[9], (DEPTH, HGRN_HEAD_V), f32)
    w_out = MIX_WIDTH ** -0.5 * jax.random.normal(ks[10], (DEPTH, MIX_WIDTH, D_MODEL), f32)
    norm_post_w = 1.0 + 0.05 * jax.random.normal(ks[11], (DEPTH, D_MODEL), f32)
    return {"x": x, "c": c, "norm_pre_w": norm_pre_w, "ada_w": ada_w, "ada_b": ada_b,
            "w_in": w_in, "pool_w": pool_w, "pool_scale": pool_scale,
            "hgrn_lower_bounds": hgrn_lower_bounds, "hgrn_norm_w": hgrn_norm_w,
            "w_out": w_out, "norm_post_w": norm_post_w}

def first_block(x, c, norm_pre_w, ada_w, ada_b, w_in, pool_w, pool_scale,
              hgrn_lower_bounds, hgrn_norm_w, w_out, norm_post_w):
    B, S, D = x.shape
    f32 = jnp.float32
    lb_sm = jax.nn.softmax(hgrn_lower_bounds.astype(f32), axis=0)
    lower_bounds = jnp.cumsum(lb_sm, axis=0) - lb_sm[0]
    silu_c = jax.nn.silu(c.astype(f32))
    h_res = x.astype(f32)
    for l in range(DEPTH):
        mod = silu_c @ ada_w[l].astype(f32) + ada_b[l].astype(f32)
        shift, scale, gate = jnp.split(mod[:, None, :], 3, axis=-1)
        h = rms_norm(h_res, norm_pre_w[l]) * (1.0 + scale) + shift
        z = h @ w_in[l].astype(f32)
        u_pool, g_pool, q, f_pre, i_in, g_h = jnp.split(
            z, np.cumsum([POOL_WIDTH, POOL_WIDTH, HGRN_WIDTH, HGRN_WIDTH, HGRN_WIDTH]), axis=-1)
        pool_out = multiscale_pool(u_pool, pool_w[l], pool_scale[l]) * jax.nn.silu(g_pool)
        lb = lower_bounds[l]
        f = lb + (1.0 - lb) * jax.nn.sigmoid(f_pre)
        log_f = jnp.log(f)
        k = 1.0 - f
        heads = lambda t, d: t.reshape(B, S, HGRN_HEADS, d)
        o = hgrn2_chunkwise(heads(q, HGRN_EXPAND), heads(log_f, HGRN_EXPAND),
                            heads(k, HGRN_EXPAND), heads(i_in, HGRN_HEAD_V))
        o = rms_norm(o, hgrn_norm_w[l]) * jax.nn.silu(heads(g_h, HGRN_HEAD_V))
        hgrn_out = o.reshape(B, S, HGRN_WIDTH)
        y = jnp.concatenate([pool_out, hgrn_out], axis=-1) @ w_out[l].astype(f32)
        h_res = h_res + gate * rms_norm(y, norm_post_w[l])
    return h_res.astype(x.dtype)


N_BRANCH = 4
BRANCH_WIDTH = 512
Q_BLOCK = 128
GM_GROUPS = 4
GM_CHUNK = 128
GM_GROUP_DIM = BRANCH_WIDTH // GM_GROUPS
DSA_HEADS = 4
DSA_HEAD_DIM = BRANCH_WIDTH // DSA_HEADS
DSA_LATENT = 128
IDX_HEADS = 4
IDX_DIM = 64
TOPK_MAX = 256
CONV_WIDTH = 3
FOX_HEADS = 4
FOX_HEAD_DIM = BRANCH_WIDTH // FOX_HEADS

W = BRANCH_WIDTH
IN_SPLITS = (
    W, W, W,
    W, DSA_LATENT, IDX_HEADS * IDX_DIM, IDX_DIM, IDX_HEADS, W,
    W, W, W, W,
    W, W, W, FOX_HEADS, W,
    N_BRANCH * D_MODEL,
)
IN_WIDTH_2 = sum(IN_SPLITS)


def rms_norm_2(x, g):
    xf = x.astype(jnp.float32)
    y = xf * lax.rsqrt(jnp.mean(xf * xf, axis=-1, keepdims=True) + EPS)
    return (y * g.astype(jnp.float32)).astype(x.dtype)

def layer_norm(x, g, b):
    xf = x.astype(jnp.float32)
    mu = jnp.mean(xf, axis=-1, keepdims=True)
    var = jnp.mean(jnp.square(xf - mu), axis=-1, keepdims=True)
    y = (xf - mu) * lax.rsqrt(var + EPS)
    return (y * g.astype(jnp.float32) + b.astype(jnp.float32)).astype(x.dtype)

def to_blocks(a):
    b, s = a.shape[0], a.shape[1]
    return jnp.moveaxis(a.reshape(b, s // Q_BLOCK, Q_BLOCK, *a.shape[2:]), 1, 0)

def from_blocks(a):
    nb, b = a.shape[0], a.shape[1]
    return jnp.moveaxis(a, 0, 1).reshape(b, nb * Q_BLOCK, a.shape[-1])

def chunked_spatial_gating(u, v, ln_g, ln_b, w_s, b_s):
    bsz, s, _ = v.shape
    v = layer_norm(v, ln_g, ln_b)
    vc = v.reshape(bsz, s // GM_CHUNK, GM_CHUNK, GM_GROUPS, GM_GROUP_DIM)
    mask = jnp.tril(jnp.ones((GM_CHUNK, GM_CHUNK), dtype=bool))
    w = jnp.where(mask[None], w_s, jnp.zeros_like(w_s))
    mixed = jnp.einsum('gts,bcsge->bctge', w, vc) + jnp.transpose(b_s)[None, None, :, :, None]
    return u * mixed.reshape(bsz, s, W)

def dsa_attention(q, c_kv, q_idx, k_idx, w_idx, kv_g, w_uk, w_uv):
    bsz, s, _ = q.shape
    k_sel = min(TOPK_MAX, s // 4)
    c = rms_norm_2(c_kv, kv_g)
    qh = q.reshape(bsz, s, DSA_HEADS, DSA_HEAD_DIM)
    q_lat = jnp.einsum('bshd,hld->bshl', qh, w_uk)
    qi = q_idx.reshape(bsz, s, IDX_HEADS, IDX_DIM)
    wi = w_idx * (IDX_HEADS ** -0.5)
    key_pos = jnp.arange(s)
    gather = jax.vmap(lambda cb, ib: cb[ib])

    def block(args):
        qlb, qib, wib, blk = args
        pos_q = blk * Q_BLOCK + jnp.arange(Q_BLOCK)
        dots = jnp.einsum('bqhd,bsd->bqhs', qib, k_idx).astype(jnp.float32) * (IDX_DIM ** -0.5)
        score = jnp.einsum('bqh,bqhs->bqs', wib.astype(jnp.float32), jax.nn.relu(dots))
        causal = key_pos[None, :] <= pos_q[:, None]
        score = jnp.where(causal[None], score, -jnp.inf)
        _, idx = lax.top_k(score, k_sel)
        valid = idx <= pos_q[None, :, None]
        c_sel = gather(c, idx)
        logits = jnp.einsum('bqhl,bqkl->bqhk', qlb, c_sel).astype(jnp.float32) * (DSA_HEAD_DIM ** -0.5)
        logits = jnp.where(valid[:, :, None, :], logits, -jnp.inf)
        p = jax.nn.softmax(logits, axis=-1).astype(c.dtype)
        o_lat = jnp.einsum('bqhk,bqkl->bqhl', p, c_sel)
        o = jnp.einsum('bqhl,hld->bqhd', o_lat, w_uv)
        return o.reshape(bsz, Q_BLOCK, W)

    nb = s // Q_BLOCK
    out = lax.map(block, (to_blocks(q_lat), to_blocks(qi), to_blocks(wi), jnp.arange(nb)))
    return from_blocks(out)

def short_gated_conv(b_gate, c_gate, x_in, conv_w):
    s = x_in.shape[1]
    y = c_gate * x_in
    yp = jnp.pad(y, ((0, 0), (CONV_WIDTH - 1, 0), (0, 0)))
    conv = conv_w[0] * yp[:, 0:s]
    for j in range(1, CONV_WIDTH):
        conv = conv + conv_w[j] * yp[:, j:j + s]
    return b_gate * conv

def forgetting_attention(q, k, v, f_logit, b_f):
    bsz, s, _ = q.shape
    qh = q.reshape(bsz, s, FOX_HEADS, FOX_HEAD_DIM)
    kh = k.reshape(bsz, s, FOX_HEADS, FOX_HEAD_DIM)
    vh = v.reshape(bsz, s, FOX_HEADS, FOX_HEAD_DIM)
    cum = jnp.cumsum(jax.nn.log_sigmoid((f_logit + b_f).astype(jnp.float32)), axis=1)
    cum_k = jnp.transpose(cum, (0, 2, 1))
    key_pos = jnp.arange(s)

    def block(args):
        qb, cq, blk = args
        pos_q = blk * Q_BLOCK + jnp.arange(Q_BLOCK)
        logits = jnp.einsum('bqhd,bshd->bhqs', qb, kh).astype(jnp.float32) * (FOX_HEAD_DIM ** -0.5)
        logits = logits + jnp.transpose(cq, (0, 2, 1))[..., None] - cum_k[:, :, None, :]
        logits = jnp.where((key_pos[None, :] <= pos_q[:, None])[None, None], logits, -jnp.inf)
        p = jax.nn.softmax(logits, axis=-1).astype(vh.dtype)
        o = jnp.einsum('bhqs,bshd->bqhd', p, vh)
        return o.reshape(bsz, Q_BLOCK, W)

    nb = s // Q_BLOCK
    out = lax.map(block, (to_blocks(qh), to_blocks(cum), jnp.arange(nb)))
    return from_blocks(out)

def hybrid_layer(x, norm_g, w_in, gm_ln_g, gm_ln_b, gm_w_s, gm_b_s, dsa_kv_g, dsa_w_uk, dsa_w_uv,
                 conv_w, fox_b_f, w_branch, w_out):
    bsz, s, d = x.shape
    h = rms_norm_2(x, norm_g)
    proj = h @ w_in
    points = [int(p) for p in np.cumsum(np.array(IN_SPLITS))[:-1]]
    (a_u, a_v, a_z,
     b_q, b_c, b_qi, b_ki, b_wi, b_z,
     c_b, c_c, c_x, c_z,
     d_q, d_k, d_v, d_f, d_z,
     gates) = jnp.split(proj, points, axis=-1)
    y_a = chunked_spatial_gating(a_u, a_v, gm_ln_g, gm_ln_b, gm_w_s, gm_b_s) * jax.nn.silu(a_z)
    y_b = dsa_attention(b_q, b_c, b_qi, b_ki, b_wi, dsa_kv_g, dsa_w_uk, dsa_w_uv) * jax.nn.silu(b_z)
    y_c = short_gated_conv(c_b, c_c, c_x, conv_w) * jax.nn.silu(c_z)
    y_d = forgetting_attention(d_q, d_k, d_v, d_f, fox_b_f) * jax.nn.silu(d_z)
    ys = jnp.stack([y_a, y_b, y_c, y_d], axis=0)
    branch_d = jnp.einsum('nbsw,nwd->bsnd', ys, w_branch)
    g = jax.nn.sigmoid(gates.reshape(bsz, s, N_BRANCH, d))
    merged = jnp.sum(g * branch_d, axis=2)
    return x + merged @ w_out

def second_inputs(seed: int = 0) -> dict:
    key = jax.random.key(seed)
    ks = jax.random.split(key, 16)
    f32 = jnp.float32
    nrm = lambda k, shp, sc: jax.random.normal(k, shp, f32) * sc
    return {
        'x': nrm(ks[0], (BATCH, SEQ, D_MODEL), 1.0),
        'norm_g': 1.0 + nrm(ks[1], (DEPTH, D_MODEL), 0.05),
        'w_in': nrm(ks[2], (DEPTH, D_MODEL, IN_WIDTH_2), D_MODEL ** -0.5),
        'gm_ln_g': 1.0 + nrm(ks[3], (DEPTH, W), 0.05),
        'gm_ln_b': nrm(ks[4], (DEPTH, W), 0.02),
        'gm_w_s': nrm(ks[5], (DEPTH, GM_GROUPS, GM_CHUNK, GM_CHUNK), GM_CHUNK ** -0.5),
        'gm_b_s': 1.0 + nrm(ks[6], (DEPTH, GM_GROUPS, GM_CHUNK), 0.1),
        'dsa_kv_g': 1.0 + nrm(ks[7], (DEPTH, DSA_LATENT), 0.05),
        'dsa_w_uk': nrm(ks[8], (DEPTH, DSA_HEADS, DSA_LATENT, DSA_HEAD_DIM), DSA_LATENT ** -0.5),
        'dsa_w_uv': nrm(ks[9], (DEPTH, DSA_HEADS, DSA_LATENT, DSA_HEAD_DIM), DSA_LATENT ** -0.5),
        'conv_w': nrm(ks[10], (DEPTH, CONV_WIDTH, W), CONV_WIDTH ** -0.5),
        'fox_b_f': jax.random.uniform(ks[11], (DEPTH, FOX_HEADS), f32, minval=1.0, maxval=4.0),
        'w_branch': nrm(ks[12], (DEPTH, N_BRANCH, W, D_MODEL), W ** -0.5),
        'w_out': nrm(ks[13], (DEPTH, D_MODEL, D_MODEL), 0.5 * D_MODEL ** -0.5),
        'final_g': 1.0 + nrm(ks[14], (D_MODEL,), 0.05),
    }

def second_block(x, norm_g, w_in, gm_ln_g, gm_ln_b, gm_w_s, gm_b_s, dsa_kv_g, dsa_w_uk, dsa_w_uv,
              conv_w, fox_b_f, w_branch, w_out, final_g):
    h = x
    for l in range(DEPTH):
        h = hybrid_layer(h, norm_g[l], w_in[l], gm_ln_g[l], gm_ln_b[l], gm_w_s[l], gm_b_s[l],
                         dsa_kv_g[l], dsa_w_uk[l], dsa_w_uv[l], conv_w[l], fox_b_f[l],
                         w_branch[l], w_out[l])
    return rms_norm_2(h, final_g)


def setup_inputs(seed=0):
    out = dict(first_inputs(seed))
    for name, value in second_inputs(seed + 1).items():
        if name != "x":
            out[name + "_2"] = value
    return out


def reference(
    x, c, norm_pre_w, ada_w, ada_b, w_in, pool_w, pool_scale, hgrn_lower_bounds, hgrn_norm_w,
    w_out, norm_post_w, norm_g_2, w_in_2, gm_ln_g_2, gm_ln_b_2, gm_w_s_2, gm_b_s_2, dsa_kv_g_2,
    dsa_w_uk_2, dsa_w_uv_2, conv_w_2, fox_b_f_2, w_branch_2, w_out_2, final_g_2,
):
    x = first_block(
        x, c, norm_pre_w, ada_w, ada_b, w_in, pool_w, pool_scale, hgrn_lower_bounds,
        hgrn_norm_w, w_out, norm_post_w,
    )
    return second_block(
        x, norm_g_2, w_in_2, gm_ln_g_2, gm_ln_b_2, gm_w_s_2, gm_b_s_2, dsa_kv_g_2, dsa_w_uk_2,
        dsa_w_uv_2, conv_w_2, fox_b_f_2, w_branch_2, w_out_2, final_g_2,
    )


_drawn_inputs = setup_inputs


def setup_inputs(seed=0):
    import zlib

    import numpy as np

    out = dict(_drawn_inputs(seed))
    spreads = {}
    factors = {'ada_b': 4.162,
     'pool_scale': 5.148,
     'hgrn_norm_w': 4.024,
     'norm_post_w': 3.37,
     'gm_ln_g_2': 21.889,
     'gm_ln_b_2': 51.127,
     'gm_b_s_2': 10.353,
     'dsa_kv_g_2': 8.0,
     'fox_b_f_2': 29.96}
    for name, (base, spread) in spreads.items():
        noise = np.random.default_rng([zlib.crc32(name.encode()), seed]).standard_normal(out[name].shape)
        drawn = base * np.exp(spread * noise) if base else spread * noise
        out[name] = __import__('jax').numpy.asarray(drawn.astype(out[name].dtype))
    for name, factor in factors.items():
        out[name] = (out[name] * factor).astype(out[name].dtype)
    return out
```

```python
import numpy as np
import concourse.bass as bass
from concourse import mybir
from contextlib import ExitStack

P = 128
S = 512
TT = S // P
D = 1024
KT = D // P
W = 512
HEADS = 8
C = 64
NC = S // C
EPS = 1e-6
U = 1024
RING = 4
SPLITS = 4
AHEAD = SPLITS - 1
NEG = -1.0e30
OUTSIDE = -3.0e38
TAKEN = -3.3e38
SIDE = 128 + 256 + 64 + 4 + 4

ORDER = [("ada", j) for j in range(16)]
ORDER += [("f", j) for j in range(8)] + [("q", j) for j in range(8)]
for g in range(4):
    ORDER += [("u", 2 * g), ("u", 2 * g + 1), ("gp", 2 * g), ("gp", 2 * g + 1),
              ("gate_ada", 2 * g), ("gate_ada", 2 * g + 1), ("pw", g)]
ORDER += [("i", j) for j in range(8)] + [("gh", j) for j in range(8)]
ORDER += [("wo", j) for j in range(16)]
for kind in ("bs", "bq", "av", "au", "az"):
    ORDER += [(kind, j) for j in range(4)]
for j in range(4):
    ORDER += [("cc", j), ("cx", j), ("cb", j), ("cz", j)]
for kind in ("dq", "dk", "dv", "bz", "dz"):
    ORDER += [(kind, j) for j in range(4)]
for j in range(KT):
    ORDER += [("ga", 4 * j), ("ga", 4 * j + 1), ("br", 2 * j), ("ga", 4 * j + 2), ("ga", 4 * j + 3), ("br", 2 * j + 1)]
ORDER += [("w2", j) for j in range(8)]
ADA = ("ada", "gate_ada")
UNIT = {u: n for n, u in enumerate(ORDER)}
USED = [u for u in ORDER if u[0] not in ADA]
STEP = {u: k for k, u in enumerate(USED)}
WIDTH = {"pw": 512, "bs": 2 * SIDE}
TOKEN_UNITS = {"i": 4, "wo": 8, "bs": 4, "av": 4, "dv": 4, "w2": 4}
GATES = ("gp", "gh", "az", "bz", "cz", "dz")
PANELS = ("f", "q", "u", "gp", "gh", "bq", "au", "az", "bz", "cc", "cx", "cb", "cz", "dq", "dk", "dz", "ga")
PAIRS = ("pw", "br")
BY_DVE = ("gp", "gh", "pw", "av", "az", "bz", "cz", "dz", "cx", "cb", "br", "w2")

GATE_ORDER = [u for u in USED if u[0] in GATES]

RESULT = {}
FREED = []
_freed = {"act": 0, "dve": 0}
for _kind, _j in USED:
    _per = TOKEN_UNITS.get(_kind, 1)
    if _j % _per:
        continue
    RESULT[_kind, _j // _per] = len(FREED)
    for _ in range(TT if _kind in TOKEN_UNITS else 2 if _kind in PAIRS else 1):
        _by = "dve" if _kind in BY_DVE or (_kind, _j) == ("wo", 8) else "act"
        _freed[_by] += 1
        FREED.append((_by, _freed[_by]))

LEVELS = [32, 16, 8, 4, 2, 1, 0]
NL = len(LEVELS)
LEVEL_AT = {u: m for m, u in enumerate([u for u in USED if u[0] in ("u", "gp", "pw", "i")])}
assert len(LEVEL_AT) == 4 * NL
HEAD_AT = {u: n for n, u in enumerate([("gh", j) for j in range(8)] + [("wo", 0)])}


SLOT0 = STEP["av", 0]
SPARSE = TT * 4
SCORES_AT = {t: [] for t in range(-8, 200)}
for _s in range(2 * SPARSE):
    SCORES_AT[1 + _s + _s // 4 if _s < SPARSE else 38 + (_s - SPARSE) // 2].append(_s)
SLOT_OF = {_s: _t for _t, _l in SCORES_AT.items() for _s in _l}
TURN_AT = {t: SCORES_AT.get(t - 1, []) for t in range(-7, 200)}
SUM_AT = {t: SCORES_AT.get(t - 2, []) for t in range(-6, 200)}
UP_AT = {SLOT_OF[4 * q + 3] + 3: q for q in range(TT)}
BANK2 = []
for _t in range(0, 60):
    BANK2 += [("turn", _s) for _s in TURN_AT[_t]] + ([("up", UP_AT[_t])] if _t in UP_AT else [])
ROUNDS = 128 // 8
TOPK_STEP = 3
MIXED_AT = {7 + g: g for g in range(4)}
FORGET_AT, CUM_AT = 21, 24


FINAL = [("a", j) for j in range(4)] + [("c", j) for j in range(4)] + [("b", j) for j in range(4)] + \
    [("d", j) for j in range(4)]
D_FINAL_AT = SLOT0 + max(t for t, l in SUM_AT.items() if l) + 1


def finals_at(k):
    return 4 if k == D_FINAL_AT else int(k > 0 and USED[k - 1][0] in ("az", "bz", "cz"))


def topk_rounds(slot):
    first = slot * TOPK_STEP
    return [(1 + i // ROUNDS, i % ROUNDS) for i in range(max(first, 0), first + TOPK_STEP) if i < 3 * ROUNDS]


def pair_levels(m):
    return m + 1 - (m + 1) // NL


PAR = {}
_at = 0
for _name, _n in (("c", 8), ("ada_b", 16), ("pre_w", 8), ("pool_scale", 8), ("lb", 8), ("nw", 1),
                  ("norm_g", 8), ("conv_w", 12)):
    PAR[_name] = slice(_at, _at + _n)
    _at += _n
NPAR = _at


def program(nc, dram, out):
    f32, f32r, bf16, i32 = mybir.dt.float32, mybir.dt.float32r, mybir.dt.bfloat16, mybir.dt.int32
    ALU, ACT, AX = mybir.AluOpType, mybir.ActivationFunctionType, mybir.AxisListType
    with ExitStack() as ctx:
        top = [16512]

        def at(name, offset, shape, dt=f32):
            return nc.alloc_sbuf_tensor_at(name, shape, dt, offset=offset)

        def take(nbytes):
            top[0] += nbytes
            return top[0] - nbytes

        def fixed(name, shape, dt=f32):
            nbytes = int(np.prod(shape[1:])) * (2 if dt == bf16 else 4)
            return at(name, take(-(-nbytes // 32) * 32), shape, dt)

        ident = fixed("ident", [P, P])
        ones = fixed("ones", [P, P])
        R_0 = take(4096)
        level_mask = at("level_mask", R_0, [P, NL, C], i32)
        chunk_keep = at("chunk_keep", R_0 + 1792, [P, S])
        inv_count = at("inv_count", R_0 + 3840, [P, 16])
        ident16 = fixed("ident16", [P, P], bf16)
        causal16 = fixed("causal16", [P, P], bf16)
        kv_row = fixed("kv_row", [P, P])
        pick = fixed("pick", [36, 8], f32r)
        par = fixed("par", [P, NPAR])
        small = fixed("small", [P, 384])
        R_GP = take(4096)
        gate_post = at("gate_post", R_GP, [P, D])
        raw = fixed("raw", [P, RING, U])
        w_hi = fixed("w_hi", [P, SPLITS, U], f32r)
        w_lo = fixed("w_lo", [P, SPLITS, U], f32r)
        R_HT = take(32768)
        R_B, R_K, R_Q, R_V, R_MP = (take(16384) for _ in range(5))
        R_G = take(4096)
        R_X = take(8192)
        R_ATT = take(8192)
        R_H = top[0]
        assert R_H + 13824 <= nc.sbuf_usable_end, (R_H, nc.sbuf_usable_end)

        silu_c, ss, rstd, mod, scale_a, low_b, one_low, tmp8 = (
            small[:, a:a + n] for a, n in ((0, 8), (8, 8), (16, 8), (24, 16), (40, 8), (48, 8), (56, 8), (64, 8)))
        b_end = small[:, 72:88].rearrange("p (s c) -> p s c", s=2)
        ss_y, rstd_y = small[:, 88:100], small[:, 100:104]

        _c = [104]

        def cols(n):
            _c[0] += n
            assert _c[0] <= 384
            return small[:, _c[0] - n:_c[0]]

        ss_h, rstd_h, ss_kv, rstd_kv, ss_o, rstd_o = (cols(n) for n in (4, 4, 4, 4, 8, 8))
        top_max, top_neg, row_sum, row_inv = cols(32), cols(32), cols(32), cols(32)
        bn, bn_mean, rstd_v, cum_q, idx_w, top8, bf_col, pick_f = (cols(n) for n in (24, 8, 4, 16, 16, 8, 1, 8))

        x_in = at("x_in", R_V, [P, TT, D])
        ada_acc = at("ada_acc", R_MP, [P, 2 * D])
        hT_full = at("hT_full", R_Q, [P, KT, S])
        hT_hi = at("hT_hi", R_HT, [P, KT, S], f32r)
        hT_lo = at("hT_lo", R_HT + 16384, [P, KT, S], f32r)
        junk = at("junk", R_X, [P, D])
        idx = at("idx", R_X + 4096, [P, 2, C], i32)
        later = at("later", R_X + 4608, [P, C])
        b_cum = at("b_cum", R_B, [P, HEADS, S])
        keys = at("keys", R_K, [P, HEADS, S])
        queries = at("queries", R_Q, [P, HEADS, S])
        values = at("values", R_V, [P, TT, D])
        attn = at("attn", R_ATT, [P, HEADS, S // 2])
        xq = at("xq", R_X, [P, 2, 2 * S])
        u_pad = at("u_pad", R_V, [P, 2, 16 + S])
        sums = [at("sums0", R_V + 4224, [P, 2, 16 + S]), at("sums1", R_V + 8448, [P, 2, 16 + S])]
        d_hi = at("d_hi", R_H, [P, 2, S], f32r)
        d_lo = at("d_lo", R_H + 4096, [P, 2, S], f32r)
        silu_out = at("silu_out", R_G, [P, 2, S])
        silu_e = at("silu_e", R_H + 11776, [P, S])
        mix_pool = at("mix_pool", R_MP, [P, KT, S])
        e_b = at("e_b", R_X, [P, S])
        k_dec = at("k_dec", R_X + 2048, [P, S])
        k_decT = at("k_decT", R_X + 4096, [P, TT, P])
        q_dec = at("q_dec", R_H, [P, 2, S])
        o_sb = at("o_sb", R_H + 4096, [P, S])
        o_sq = at("o_sq", R_H + 6144, [P, S])
        states = at("states", R_H + 8192, [P, NC - 1, P])
        mixh_hi = at("mixh_hi", R_B, [P, HEADS, S], f32r)
        mixh_lo = at("mixh_lo", R_K, [P, HEADS, S], f32r)
        mixp_hi = at("mixp_hi", R_HT, [P, KT, S], f32r)
        mixp_lo = at("mixp_lo", R_HT + 16384, [P, KT, S], f32r)
        y_sb = at("y_sb", R_Q, [P, TT, D])
        x_again = at("x_again", R_V, [P, TT, D])
        x2 = at("x2", R_B, [P, TT, D])
        gate_row = at("gate_row", R_MP, [P, D])
        post_row = at("post_row", R_MP + 4096, [P, D])
        h2_full = at("h2_full", R_MP + 8192, [P, 2, S])
        M = R_G
        side_tok = at("side_tok", M, [P, TT, SIDE])
        lat_q = at("lat_q", M + 8192, [P, 4, S])
        probs = at("probs", M + 16384, [P, 2, S])
        probsT = at("probsT", M + 20480, [P, 2, S])
        latT = at("latT", M + 24576, [P, S])
        lat = at("lat", M + 26624, [P, TT, P])
        lat_out = at("lat_out", M + 28672, [P, S])
        sel16 = at("sel16", M + 30720, [P, 3, S], bf16)
        w_up = at("w_up", R_GP, [P, 2, 4, P])
        idx_qT = at("idx_qT", R_MP, [P, 2, S])
        idx_kT = at("idx_kT", R_MP + 4096, [P, S])
        score = at("score", R_MP + 6144, [P, 3, S])
        relu = at("relu", R_MP + 12288, [P, 2, S])
        key_twice = at("key_twice", R_MP + 14336, [P, TT, P])
        v_norm = at("v_norm", R_V, [P, TT, S])
        ln_rows = at("ln_rows", R_V + 8192, [P, 2, S])
        mixT = at("mixT", R_V + 12288, [P, 4, P])
        mix_b = at("mix_b", R_V + 14336, [P, 4, P])
        c_gate = at("c_gate", R_MP, [P, S])
        conv_in = at("conv_in", R_MP + 2048, [P, 2 + S])
        conv = at("conv", R_MP + 12288, [P, S])
        fox_q, fox_k = at("fox_q", M, [P, 4, S]), at("fox_k", M + 8192, [P, 4, S])
        fox_v = at("fox_v", R_MP + 8192, [P, TT, S])
        forget = at("forget", M + 24576, [4, 2, S])
        forget_r = at("forget_r", M + 32768, [36, S], f32r)
        z_d = at("z_d", M + 24576, [P, 4, S])
        silu_e2 = at("silu_e2", R_0, [P, S])
        y_tmp = at("y_tmp", R_0 + 2048, [P, S])
        y_tmp2 = at("mixed", R_MP + 14336, [P, S])[:, :]
        y_hi = {n: at(f"y{n}_hi", r, [P, 4, S], f32r) for n, r in zip("abcd", (R_K, R_Q, R_V, R_MP))}
        y_lo = {n: at(f"y{n}_lo", r + 8192, [P, 4, S], f32r) for n, r in zip("abcd", (R_K, R_Q, R_V, R_MP))}
        y_raw = {n: at(f"y{n}_raw", r, [P, 4, S]) for n, r in zip("abcd", (R_K, R_Q, R_V, R_MP))}
        sig = at("sig", R_GP, [P, 2, S])
        merged = at("merged", R_0, [P, S])
        merged_part = at("merged_part", R_0 + 2048, [P, S])
        m_hi, m_lo = at("m_hi", M, [P, KT, S], f32r), at("m_lo", M + 16384, [P, KT, S], f32r)
        final_row = at("final_row", R_K, [P, D])
        assert M + 34816 <= nc.sbuf_usable_end, (M, nc.sbuf_usable_end)

        acc = [ctx.enter_context(nc.psum_tensor(f"acc{n}", [P, S], f32)) for n in range(4)]
        side = [ctx.enter_context(nc.psum_tensor(f"side{n}", [P, S], f32)) for n in range(4)]

        def sem(name):
            return ctx.enter_context(nc.semaphore(name))

        raw_in = [sem(f"raw_in{n}") for n in range(RING)]
        x_here, par_here, rows_here, x_again_here = sem("x_here"), sem("par_here"), sem("rows_here"), sem("x_again_here")
        stored = sem("stored")
        hi_made, lo_made = sem("hi_made"), sem("lo_made")
        ada_summed = sem("ada_summed")
        unit_used = sem("unit_used")
        freed = {"act": sem("freed_act"), "dve": sem("freed_dve")}
        act_chain, dve_chain, pool_chain = sem("act_chain"), sem("dve_chain"), sem("pool_chain")
        consts = sem("consts")
        c_exp, lb_exp, lb_diff = sem("c_exp"), sem("lb_exp"), sem("lb_diff")
        x_normed, xT_made, xT_copied = sem("x_normed"), sem("xT_made"), sem("xT_copied")
        mod_summed, h_full, h_hi, h_lo = sem("mod_summed"), sem("h_full"), sem("h_hi"), sem("h_lo")
        f_made, log_made, b_made = sem("f_made"), sem("log_made"), sem("b_made")
        sum_made, d_made, d_hi_made, d_lo_made = sem("sum_made"), sem("d_made"), sem("d_hi_made"), sem("d_lo_made")
        silu_exp, silu_bound, silu_sig = sem("silu_exp"), sem("silu_bound"), sem("silu_sig")
        f_bound, f_sig = sem("f_bound"), sem("f_sig")
        level_diff, level_exp, level_x = sem("level_diff"), sem("level_exp"), sem("level_x")
        scores_made, level_copied = sem("scores_made"), sem("level_copied")
        decay_diff, decay_exp, prep_made = sem("decay_diff"), sem("decay_exp"), sem("prep_made")
        kT_made, kT_copied, outer_made, states_made = sem("kT_made"), sem("kT_copied"), sem("outer_made"), sem("states_made")
        even_made = sem("even_made")
        o_made, o_squared, ms_made, o_rstd = sem("o_made"), sem("o_squared"), sem("ms_made"), sem("o_rstd")
        o_final, mixh_hi_made, mixh_made = sem("o_final"), sem("mixh_hi_made"), sem("mixh_made")
        mixp_hi_made, mixp_made = sem("mixp_hi_made"), sem("mixp_made")
        gate_summed, gate_made = sem("gate_summed"), sem("gate_made")
        y_squared, y_total, y_rstd, x2_made = sem("y_squared"), sem("y_total"), sem("y_rstd"), sem("x2_made")

        h2_squared, x2_normed, x2T_made, h2_full_made, h2_hi_made, h2_made = (
            sem(n) for n in ("h2_squared", "x2_normed", "x2T_made", "h2_full_made", "h2_hi_made", "h2_made"))
        small_rows, up_here, spatial_here, masked = sem("small_rows"), sem("up_here"), sem("spatial_here"), sem("masked")
        lat_rstd, lat_made, idxT_made, idxT_copied = sem("lat_rstd"), sem("lat_made"), sem("idxT_made"), sem("idxT_copied")
        dots_made, relu_made, cut_made = sem("dots_made"), sem("relu_made"), sem("cut_made")
        relu_used, sel_made = sem("relu_used"), sem("sel_made")
        latq_made, latq_copied = sem("latq_made"), sem("latq_copied")
        logits_made, max_made, exp_made, probs_made = sem("logits_made"), sem("max_made"), sem("exp_made"), sem("probs_made")
        turned, bank2_read, summed, bank3_read = (
            sem(n) for n in ("turned", "bank2_read", "summed", "bank3_read"))
        bn_made, bn_rstd, v_made, mixed_made, mixed_read = (
            sem(n) for n in ("bn_made", "bn_rstd", "v_made", "mixed_made", "mixed_read"))
        conv_freed = sem("conv_freed")
        y_final, y_hi_made, y_made = sem("y_final"), sem("y_hi_made"), sem("y_made")
        fgt_made, fgt_abs, fgt_ln, fgt_sum, fgt_hi, fgt_ready = (
            sem(n) for n in ("fgt_made", "fgt_abs", "fgt_ln", "fgt_sum", "fgt_hi", "fgt_ready"))
        cum_made, cum_read, pick_made = sem("cum_made"), sem("cum_read"), sem("pick_made")
        sig_made, m_sum, m_hi_made, m_made = sem("sig_made"), sem("m_sum"), sem("m_hi_made"), sem("m_made")
        h_sq, h_tot, h_rstd, out_made, final_here = (
            sem(n) for n in ("h_sq", "h_tot", "h_rstd", "out_made", "final_here"))

        def wait_freed(eng, result):
            by, n = FREED[result]
            eng.wait_ge(freed[by], n)

        def gate_e(n):
            return silu_e[:, :] if n < 16 else silu_e2[:, :]

        def level_view(tile, half):
            return tile.rearrange("p (n w) -> p n w", w=2 * half)

        block = ctx.enter_context(nc.Block())

        @block.sync
        def _(sp):
            sp.dma_start(x_in[:, :, :], dram["x"].rearrange("(t p) d -> p t d", p=P)).then_inc(x_here, 16)
            for n, (kind, j) in enumerate(ORDER):
                if n >= RING:
                    last = ORDER[n - RING]
                    if last[0] in ADA:
                        sp.wait_ge(ada_summed, last[1] + 1 + 16 * (last[0] == "gate_ada"))
                    else:
                        sp.wait_ge(lo_made, STEP[last] + 1)
                if kind == "ada":
                    src = dram["ada_w"][(j // 2) * P:(j // 2 + 1) * P, (j % 2) * D:(j % 2 + 1) * D]
                elif kind == "gate_ada":
                    src = dram["ada_w"][j * P:(j + 1) * P, 2 * D:3 * D]
                else:
                    src = dram[kind][j, :, :]
                width = WIDTH.get(kind, U)
                sp.dma_start(raw[:, n % RING, 0:width], src).then_inc(raw_in[n % RING], 16)
            out_tiles = out.rearrange("(t p) d -> p t d", p=P)
            for t in range(TT):
                sp.wait_ge(out_made, t + 1)
                sp.dma_start(out_tiles[:, t, :], x2[:, t, :]).then_inc(stored, 16)
            sp.wait_ge(stored, 16 * TT)

        @block.gpsimd
        def _(pool):
            done = [0]

            def then(ins):
                done[0] += 1
                ins.then_inc(pool_chain, 1)
                pool.wait_ge(pool_chain, done[0])

            then(nc.gpsimd.memset(ident[:, :], 0.0))
            nc.gpsimd.affine_select(out=ident[:, :], in_=ident[:, :], compare_op=ALU.not_equal, fill=1.0, base=0,
                                    pattern=[[-1, P]], channel_multiplier=1).then_inc(consts, 1)
            nc.gpsimd.memset(ones[:, :], 1.0).then_inc(consts, 1)
            nc.gpsimd.iota(idx[:, 0, :], pattern=[[1, C]], base=0, channel_multiplier=0).then_inc(consts, 1)
            nc.gpsimd.iota(idx[:, 1, :], pattern=[[0, C]], base=0, channel_multiplier=1).then_inc(consts, 1)
            then(nc.gpsimd.memset(chunk_keep[:, :], 1.0))
            nc.gpsimd.memset(chunk_keep[:, :].rearrange("p (c t) -> p c t", t=C)[:, :, 0:1], 0.0).then_inc(consts, 1)
            nc.gpsimd.memset(attn[:, :, :], 0.0).then_inc(consts, 1)
            then(nc.gpsimd.memset(causal16[:, :], 0.0))
            nc.gpsimd.affine_select(out=causal16[:, :], in_=causal16[:, :], compare_op=ALU.is_ge, fill=NEG, base=0,
                                    pattern=[[-1, P]], channel_multiplier=1).then_inc(consts, 1)
            then(nc.gpsimd.memset(pick_f[0:36, :], 0.0))
            for base in (0, -32):
                then(nc.gpsimd.affine_select(out=pick_f[0:36, 0:4], in_=pick_f[0:36, 0:4], compare_op=ALU.not_equal,
                                             fill=1.0, base=base, pattern=[[-1, 4]], channel_multiplier=1))
            nc.gpsimd.memset(pick_f[0:36, 4:8], 0.0).then_inc(consts, 1)
            pool.dma_start(kv_row[:, :], dram["kv_g"].partition_broadcast(P)).then_inc(small_rows, 16)
            pool.dma_start(bf_col[0:4, :], dram["b_f"]).then_inc(small_rows, 16)
            pool.wait_ge(h_lo, KT)
            then(nc.gpsimd.memset(u_pad[:, :, 0:16], 0.0))
            for g in range(4):
                wait_freed(pool, RESULT["u", 2 * g + 1])
                if g:
                    pool.wait_ge(d_lo_made, g)
                src, reach = u_pad, 0
                for r in range(g + 1):
                    dst, shift = sums[r % 2], 1 << r
                    reach += shift
                    ins = nc.gpsimd.tensor_tensor(out=dst[:, :, reach:], in0=src[:, :, reach:],
                                                  in1=src[:, :, reach - shift:16 + S - shift], op=ALU.add)
                    if r < g:
                        then(ins)
                    else:
                        ins.then_inc(sum_made, 1)
                    src = dst
            pool.wait_ge(mixp_made, KT)
            pool.dma_start(gate_row[:, :], dram["gate_b"].partition_broadcast(P)).then_inc(rows_here, 16)
            pool.dma_start(post_row[:, :], dram["post_w"].partition_broadcast(P)).then_inc(rows_here, 16)
            pool.wait_ge(o_made, HEADS)
            pool.dma_start(x_again[:, :, :], dram["x"].rearrange("(t p) d -> p t d", p=P)).then_inc(x_again_here, 16)
            pool.wait_ge(x2_made, TT)
            for o, name in enumerate(("w_uk", "w_uv")):
                pool.dma_start(w_up[:, o, :, :], dram[name]).then_inc(up_here, 16)
            pool.dma_start(ln_rows[:, 0, :], dram["ln_g"].partition_broadcast(P)).then_inc(spatial_here, 16)
            pool.dma_start(ln_rows[:, 1, :], dram["ln_b"].partition_broadcast(P)).then_inc(spatial_here, 16)
            pool.dma_start(mix_b[:, :, :].rearrange("p g t -> p (g t)"), dram["b_s"].partition_broadcast(P))\
                .then_inc(spatial_here, 16)
            pool.dma_start(mixT[:, :, :], dram["w_s"]).then_inc(spatial_here, 16)
            pool.wait_ge(spatial_here, 64)
            nc.gpsimd.affine_select(out=mixT[:, :, :], in_=mixT[:, :, :], compare_op=ALU.is_ge, fill=0.0, base=0,
                                    pattern=[[0, 4], [1, P]], channel_multiplier=-1).then_inc(masked, 1)
            for t in range(1, TT):
                pool.wait_ge(relu_used, 4 * t)
                diagonal = score[:, t - 1, t * P:(t + 1) * P]
                nc.gpsimd.affine_select(out=diagonal, in_=diagonal, compare_op=ALU.is_ge, fill=OUTSIDE, base=0,
                                        pattern=[[-1, P]], channel_multiplier=1).then_inc(cut_made, 1)
            pool.wait_ge(unit_used, STEP["br", 2 * KT - 1] + 1)
            pool.dma_start(final_row[:, :], dram["final_g"].partition_broadcast(P)).then_inc(final_here, 16)

        @block.scalar
        def _(act):
            done = [0]

            def then(ins):
                done[0] += 1
                ins.then_inc(act_chain, 1)
                act.wait_ge(act_chain, done[0])

            def split_hi(k):
                kind, j = USED[k]
                n, width = UNIT[kind, j], WIDTH.get(kind, U)
                act.wait_ge(raw_in[n % RING], 16 * (n // RING + 1))
                if k >= SPLITS:
                    act.wait_ge(unit_used, k - SPLITS + 1)
                nc.scalar.activation(w_hi[:, k % SPLITS, 0:width], raw[:, n % RING, 0:width], ACT.Copy)\
                    .then_inc(hi_made, 1)

            def exp_level(m):
                if m < 4 * NL and LEVELS[m % NL]:
                    act.wait_ge(level_diff, pair_levels(m))
                    nc.scalar.activation(xq[:, m % 2, :], xq[:, m % 2, :], ACT.Exp).then_inc(level_exp, 1)

            def exp_decays(n):
                act.wait_ge(decay_diff, n + 1)
                nc.scalar.activation(e_b[:, :], b_cum[:, n, :], ACT.Exp).then_inc(decay_exp, 1)
                nc.scalar.activation(k_dec[:, :], k_dec[:, :], ACT.Exp).then_inc(decay_exp, 1)

            act.preload_act_table_set("natural_log_exp_and_others")
            act.dma_start(par[:, :], dram["par"]).then_inc(par_here, 16)
            act.wait_ge(par_here, 16)
            nc.scalar.activation(tmp8, par[:, PAR["c"]], ACT.Exp, scale=-1.0).then_inc(c_exp, 1)
            act.wait_ge(lb_diff, 1)
            nc.scalar.activation(one_low, low_b, ACT.Exp).then_inc(lb_exp, 1)
            act.wait_ge(x_here, 16)
            for t in range(TT):
                then(nc.scalar.activation(junk[:, :], x_in[:, t, :], ACT.Square, accum_out=ss[:, t:t + 1]))
                then(nc.scalar.activation(rstd[:, t:t + 1], ss[:, t:t + 1], ACT.Ln, scale=1.0 / D, bias=EPS))
                then(nc.scalar.activation(rstd[:, t:t + 1], rstd[:, t:t + 1], ACT.Exp, scale=-0.5))
                nc.scalar.activation(x_in[:, t, :], x_in[:, t, :], ACT.Copy, scale=rstd[:, t:t + 1]).then_inc(x_normed, 1)
            for kt in range(KT):
                act.wait_ge(xT_made, kt + 1)
                nc.scalar.activation(hT_full[:, kt, :], (acc + side)[kt][:, :], ACT.Copy).then_inc(xT_copied, 1)
            split_hi(0)
            for kt in range(KT):
                act.wait_ge(h_full, kt + 1)
                nc.scalar.activation(hT_hi[:, kt, :], hT_full[:, kt, :], ACT.Copy).then_inc(h_hi, 1)
            for k in range(1, AHEAD):
                split_hi(k)

            def copy_out(dst, result, by, **more):
                nc.scalar.activation(dst, acc[result % 4][:, :], ACT.Copy, **more).then_inc(by, 1)

            def enter_second_block():
                for t in range(TT):
                    act.wait_ge(x2_made, t + 1)
                    then(nc.scalar.activation(y_sb[:, t, :], x2[:, t, :], ACT.Square, accum_out=ss_h[:, t:t + 1]))
                    then(nc.scalar.activation(rstd_h[:, t:t + 1], ss_h[:, t:t + 1], ACT.Ln, scale=1.0 / D, bias=EPS))
                    then(nc.scalar.activation(rstd_h[:, t:t + 1], rstd_h[:, t:t + 1], ACT.Exp, scale=-0.5))
                    nc.scalar.activation(y_sb[:, t, :], x2[:, t, :], ACT.Copy, scale=rstd_h[:, t:t + 1])\
                        .then_inc(x2_normed, 1)
                for n in range(2 * TT):
                    act.wait_ge(h2_full_made, n + 1)
                    t, half = n // 2, n % 2
                    nc.scalar.activation(hT_hi[:, 4 * half:4 * half + 4, t * P:(t + 1) * P],
                                         h2_full[:, n % 2, :].rearrange("p (k s) -> p k s", s=P), ACT.Copy)\
                        .then_inc(h2_hi_made, 1)

            def side_slot(slot):
                for s in TURN_AT.get(slot, []):
                    n, w = BANK2.index(("turn", s)), (s // 4 % TT + 1) * P
                    act.wait_ge(turned, n + 1)
                    if s >= 2:
                        act.wait_ge(summed, s - 1)
                    nc.scalar.activation(probsT[:, s % 2, 0:w], side[2][:, 0:w], ACT.Copy).then_inc(bank2_read, 1)
                for s in SUM_AT.get(slot, []):
                    if s % 4 == 3:
                        q = s // 4
                        act.wait_ge(summed, s + 1)
                        if s < SPARSE:
                            if q:
                                act.wait_ge(turned, BANK2.index(("up", q - 1)) + 1)
                            nc.scalar.activation(lat_out[:, :], side[3][:, :], ACT.Copy).then_inc(bank3_read, 1)
                        else:
                            tok = slice((q % TT) * P, (q % TT + 1) * P)
                            nc.scalar.activation(y_raw["d"][:, :, tok], side[3][:, :].rearrange("p (h s) -> p h s", s=P),
                                                 ACT.Copy).then_inc(bank3_read, 1)
                if slot in UP_AT:
                    q = UP_AT[slot]
                    n = BANK2.index(("up", q))
                    act.wait_ge(turned, n + 1)
                    nc.scalar.activation(y_raw["b"][:, :, q * P:(q + 1) * P],
                                         side[2][:, :].rearrange("p (h s) -> p h s", s=P), ACT.Copy).then_inc(bank2_read, 1)
                for s in SCORES_AT.get(slot, []):
                    w = (s // 4 % TT + 1) * P
                    act.wait_ge(max_made, s + 1)
                    if s >= 2:
                        act.wait_ge(turned, BANK2.index(("turn", s - 2)) + 1)
                    nc.scalar.activation(probs[:, s % 2, 0:w], side[s % 2][:, 0:w], ACT.Exp, bias=top_neg[:, s:s + 1],
                                         accum_out=row_sum[:, s:s + 1]).then_inc(exp_made, 1)

            gates = 0
            finals = [0]
            before = None
            for k, (kind, j) in enumerate(USED):
                if k + AHEAD < len(USED):
                    split_hi(k + AHEAD)
                if before in GATES:
                    act.wait_ge(silu_bound, gates)
                    then(nc.scalar.activation(gate_e(gates - 1), gate_e(gates - 1), ACT.Ln))
                    nc.scalar.activation(gate_e(gates - 1), gate_e(gates - 1), ACT.Exp, scale=-1.0).then_inc(silu_sig, 1)
                before = kind
                m = LEVEL_AT.get((kind, j))
                if m is not None:
                    exp_level(m + 1)
                if k - 1 in range(HEADS):
                    act.wait_ge(f_bound, k)
                    then(nc.scalar.activation(b_cum[:, k - 1, :], b_cum[:, k - 1, :], ACT.Ln))
                    nc.scalar.activation(b_cum[:, k - 1, :], b_cum[:, k - 1, :], ACT.Exp, scale=-1.0).then_inc(f_sig, 1)
                if k - 2 in range(HEADS):
                    act.wait_ge(f_made, k - 1)
                    nc.scalar.activation(b_cum[:, k - 2, :], b_cum[:, k - 2, :], ACT.Ln).then_inc(log_made, 1)
                act.wait_ge(unit_used, k + 1)
                if kind == "f":
                    nc.scalar.activation(b_cum[:, j, :], acc[RESULT[kind, j] % 4][:, :], ACT.Exp, scale=-1.0)\
                        .then_inc(freed["act"], 1)
                if kind == "q":
                    nc.scalar.activation(queries[:, j, :], acc[RESULT[kind, j] % 4][:, :], ACT.Copy)\
                        .then_inc(freed["act"], 1)
                    if j == 7:
                        exp_level(0)
                if kind == "u":
                    if j >= 2:
                        act.wait_ge(d_lo_made, j // 2)
                    nc.scalar.activation(u_pad[:, j % 2, 16:], acc[RESULT[kind, j] % 4][:, :], ACT.Copy)\
                        .then_inc(freed["act"], 1)
                if kind in GATES:
                    if gates:
                        wait_freed(act, RESULT[GATE_ORDER[gates - 1]])
                    nc.scalar.activation(gate_e(gates), acc[RESULT[kind, j] % 4][:, :], ACT.Exp, scale=-1.0)\
                        .then_inc(silu_exp, 1)
                    gates += 1
                if (kind, j % 2) == ("gp", 0):
                    g = j // 2
                    act.wait_ge(d_made, g + 1)
                    if g:
                        act.wait_ge(unit_used, STEP["pw", g - 1] + 1)
                    nc.scalar.activation(d_hi[:, :, :], sums[(g + 1) % 2][:, :, 0:S], ACT.Copy).then_inc(d_hi_made, 1)
                if (kind, j % 4) == ("i", 3):
                    for t in range(TT):
                        r = RESULT["i", j // 4] + t
                        nc.scalar.activation(values[:, t, (j // 4) * S:(j // 4 + 1) * S], acc[r % 4][:, :], ACT.Copy)\
                            .then_inc(freed["act"], 1)
                if (kind, j) == ("i", 7):
                    exp_decays(0)
                n = HEAD_AT.get((kind, j))
                if n is not None and n < HEADS:
                    act.wait_ge(kT_made, n + 1)
                    nc.scalar.activation(k_decT[:, :, :], side[0][:, :].rearrange("p (t k) -> p t k", t=TT), ACT.Copy)\
                        .then_inc(kT_copied, 1)
                if n:
                    act.wait_ge(o_made, n)
                    if n >= 2:
                        act.wait_ge(mixh_made, n - 1)
                    nc.scalar.activation(o_sq[:, :], side[3][:, :], ACT.Square)
                    nc.scalar.activation(o_sb[:, :], side[3][:, :], ACT.Copy).then_inc(o_squared, 1)
                if n is not None and n + 1 < HEADS:
                    exp_decays(n + 1)
                if n:
                    act.wait_ge(ms_made, n)
                    then(nc.scalar.activation(o_sq[:, :], side[0][:, :], ACT.Ln, scale=1.0 / P, bias=EPS))
                    nc.scalar.activation(o_sq[:, :], o_sq[:, :], ACT.Exp, scale=-0.5).then_inc(o_rstd, 1)
                    act.wait_ge(o_final, n)
                    nc.scalar.activation(mixh_hi[:, n - 1, :], o_sb[:, :], ACT.Copy).then_inc(mixh_hi_made, 1)
                if (kind, j) == ("gh", 7):
                    for kt in range(KT):
                        nc.scalar.activation(mixp_hi[:, kt, :], mix_pool[:, kt, :], ACT.Copy).then_inc(mixp_hi_made, 1)
                if (kind, j) == ("wo", 7):
                    for t in range(TT):
                        r = RESULT["wo", 0] + t
                        nc.scalar.activation(y_sb[:, t, S:D], acc[r % 4][:, :], ACT.Square, accum_out=ss_y[:, t:t + 1])
                        nc.scalar.activation(y_sb[:, t, 0:S], acc[r % 4][:, :], ACT.Copy).then_inc(freed["act"], 1)
                if (kind, j) == ("wo", 15):
                    wait_freed(act, RESULT["wo", 0] + TT - 1)
                    for t in range(TT):
                        r = RESULT["wo", 1] + t
                        nc.scalar.activation(y_sb[:, t, S:D], acc[r % 4][:, :], ACT.Square, accum_out=ss_y[:, 4 + t:5 + t])\
                            .then_inc(y_squared, 1)
                    for t in range(TT):
                        act.wait_ge(y_total, t + 1)
                        then(nc.scalar.activation(rstd_y[:, t:t + 1], ss_y[:, 8 + t:9 + t], ACT.Ln, scale=1.0 / D, bias=EPS))
                        nc.scalar.activation(rstd_y[:, t:t + 1], rstd_y[:, t:t + 1], ACT.Exp, scale=-0.5)\
                            .then_inc(y_rstd, 1)
                    enter_second_block()
                r = RESULT.get((kind, j))
                if (kind, j) == ("bs", 3):
                    for t in range(TT):
                        nc.scalar.activation(side_tok[:, t, :], acc[(RESULT["bs", 0] + t) % 4][:, 0:SIDE], ACT.Copy)\
                            .then_inc(freed["act"], 1)
                    wait_freed(act, RESULT["bs", 0] + 3)
                    for t in range(TT):
                        then(nc.scalar.activation(lat[:, t, :], side_tok[:, t, 0:P], ACT.Square,
                                                  accum_out=ss_kv[:, t:t + 1]))
                    then(nc.scalar.activation(rstd_kv, ss_kv, ACT.Ln, scale=1.0 / P, bias=EPS))
                    nc.scalar.activation(rstd_kv, rstd_kv, ACT.Exp, scale=-0.5).then_inc(lat_rstd, 1)
                if kind == "bq":
                    copy_out(lat_q[:, j, :], r, freed["act"])
                    if j == 0:
                        act.wait_ge(idxT_made, 1)
                        for n, dst in enumerate((latT[:, :], idx_qT[:, 0, :], idx_qT[:, 1, :], idx_kT[:, :])):
                            nc.scalar.activation(dst, side[n][:, :], ACT.Copy).then_inc(idxT_copied, 1)
                    else:
                        for h in range(4):
                            n = 4 * (j - 1) + h
                            act.wait_ge(dots_made, n + 1)
                            if n >= 2:
                                act.wait_ge(relu_used, n - 1)
                            w = (j + 1) * P
                            nc.scalar.activation(relu[:, n % 2, 0:w], side[h][:, 0:w], ACT.Relu, scale=0.125)\
                                .then_inc(relu_made, 1)
                if (kind, j) == ("av", 0):
                    act.wait_ge(latq_made, 1)
                    for h in range(4):
                        nc.scalar.activation(lat_q[:, h, :], side[h][:, :], ACT.Copy, scale=float(P) ** -0.5)\
                            .then_inc(latq_copied, 1)
                if (kind, j) == ("av", 3):
                    act.wait_ge(bn_made, 1)
                    then(nc.scalar.activation(rstd_v, bn_mean.rearrange("p (t m) -> p t m", m=2)[:, :, 1], ACT.Ln, bias=EPS))
                    nc.scalar.activation(rstd_v, rstd_v, ACT.Exp, scale=-0.5).then_inc(bn_rstd, 1)
                if kind == "au":
                    copy_out(y_raw["a"][:, j, :], r, freed["act"])
                if kind == "cc":
                    if j:
                        wait_freed(act, RESULT["cx", j - 1])
                    copy_out(c_gate[:, :], r, freed["act"])
                if kind == "dq":
                    copy_out(fox_q[:, j, :], r, freed["act"], scale=float(P) ** -0.5)
                if kind == "dk":
                    copy_out(fox_k[:, j, :], r, freed["act"])
                if (kind, j) == ("dv", 3):
                    for t in range(TT):
                        copy_out(fox_v[:, t, :], RESULT["dv", 0] + t, freed["act"])
                for _ in range(finals_at(k)):
                    act.wait_ge(y_final, finals[0] + 1)
                    name, kt = FINAL[finals[0]]
                    nc.scalar.activation(y_hi[name][:, kt, :], y_tmp[:, :], ACT.Copy).then_inc(y_hi_made, 1)
                    finals[0] += 1
                slot = k - SLOT0
                side_slot(slot)
                if slot == FORGET_AT:
                    act.wait_ge(fgt_abs, 1)
                    then(nc.scalar.activation(forget[:, 1, :], forget[:, 1, :], ACT.Exp, scale=-1.0))
                    nc.scalar.activation(forget[:, 1, :], forget[:, 1, :], ACT.Ln, bias=1.0).then_inc(fgt_ln, 1)
                    act.wait_ge(fgt_sum, 1)
                    nc.scalar.activation(forget_r[0:4, :], forget[:, 0, :], ACT.Copy, scale=-1.0).then_inc(fgt_hi, 1)
                if kind == "ga":
                    if j >= 2:
                        wait_freed(act, RESULT["br", (j - 2) // 2] + j % 2)
                    nc.scalar.activation(sig[:, j % 2, :], acc[r % 4][:, :], ACT.Sigmoid).then_inc(freed["act"], 1)
                if kind == "br" and j % 2:
                    act.wait_ge(m_sum, j // 2 + 1)
                    nc.scalar.activation(m_hi[:, j // 2, :], merged[:, :], ACT.Copy).then_inc(m_hi_made, 1)
                if (kind, j) == ("w2", 3) or (kind, j) == ("w2", 7):
                    half = j // 4
                    for t in range(TT):
                        wait_freed(act, RESULT["w2", half] + t)
                        nc.scalar.activation(y_sb[:, t, half * S:(half + 1) * S], x2[:, t, half * S:(half + 1) * S],
                                             ACT.Square, accum_out=ss_o[:, 4 * half + t:4 * half + t + 1]).then_inc(h_sq, 1)
                        if half:
                            act.wait_ge(h_tot, t + 1)
                            then(nc.scalar.activation(rstd_o[:, t:t + 1], rstd_o[:, 4 + t:5 + t], ACT.Ln, scale=1.0 / D,
                                                      bias=EPS))
                            nc.scalar.activation(rstd_o[:, t:t + 1], rstd_o[:, t:t + 1], ACT.Exp, scale=-0.5)\
                                .then_inc(h_rstd, 1)

        @block.vector
        def _(dve):
            done = [0]

            def then(ins):
                done[0] += 1
                ins.then_inc(dve_chain, 1)
                dve.wait_ge(dve_chain, done[0])

            def add_ada(kind, j):
                n = UNIT[kind, j]
                dve.wait_ge(raw_in[n % RING], 16 * (n // RING + 1))
                kt, dst = (j // 2, ada_acc[:, (j % 2) * D:(j % 2 + 1) * D]) if kind == "ada" else (j, gate_post[:, :])
                first = kt == 0
                if not first:
                    dve.wait_ge(ada_summed, j - 1 if kind == "ada" else 16 + j)
                if first:
                    nc.vector.tensor_scalar(dst, raw[:, n % RING, :], silu_c[:, kt:kt + 1], None, ALU.mult)\
                        .then_inc(ada_summed, 1)
                else:
                    nc.vector.scalar_tensor_tensor(out=dst, in0=raw[:, n % RING, :], scalar=silu_c[:, kt:kt + 1], in1=dst,
                                                   op0=ALU.mult, op1=ALU.add).then_inc(ada_summed, 1)

            def split_lo(k):
                kind, j = USED[k]
                n, width = UNIT[kind, j], WIDTH.get(kind, U)
                before = n - 1
                while before >= 0 and ORDER[before][0] == "gate_ada":
                    before -= 1
                for u in ORDER[before + 1:n]:
                    add_ada(*u)
                dve.wait_ge(hi_made, k + 1)
                nc.vector.tensor_tensor(out=w_lo[:, k % SPLITS, 0:width], in0=raw[:, n % RING, 0:width],
                                        in1=w_hi[:, k % SPLITS, 0:width].bitcast(f32), op=ALU.subtract).then_inc(lo_made, 1)

            def diff_level(m):
                half = LEVELS[m % NL] if m < 4 * NL else 0
                if not half:
                    return
                g = m // NL
                if m >= 2:
                    dve.wait_ge(scores_made, m - 1)
                x = level_view(xq[:, m % 2, :], half)
                b = level_view(b_cum[:, 2 * g:2 * g + 2, :].rearrange("p h s -> p (h s)"), half)
                middle = b[:, :, half - 1:half].broadcast_to([P, S // half, half])
                nc.vector.tensor_tensor(out=x[:, :, half:], in0=b[:, :, half:], in1=middle, op=ALU.subtract)
                nc.vector.tensor_tensor(out=x[:, :, :half], in0=middle, in1=b[:, :, :half], op=ALU.subtract)\
                    .then_inc(level_diff, 1)

            def scale_level(m):
                half = LEVELS[m % NL]
                if not half:
                    return
                g = m // NL
                dve.wait_ge(level_exp, pair_levels(m))
                x = level_view(xq[:, m % 2, :], half)
                q = level_view(queries[:, 2 * g:2 * g + 2, :].rearrange("p h s -> p (h s)"), half)
                kk = level_view(keys[:, 2 * g:2 * g + 2, :].rearrange("p h s -> p (h s)"), half)
                nc.vector.tensor_tensor(out=x[:, :, half:], in0=x[:, :, half:], in1=q[:, :, half:], op=ALU.mult)
                nc.vector.tensor_tensor(out=x[:, :, :half], in0=x[:, :, :half], in1=kk[:, :, :half], op=ALU.mult)\
                    .then_inc(level_x, 1)

            def copy_level(m):
                dve.wait_ge(scores_made, m + 1)
                g = m // NL
                if m:
                    dve.wait_ge(level_copied, m)
                nc.vector.copy_predicated(attn[:, 2 * g:2 * g + 2, :].rearrange("p h (t s) -> p (h t) s", s=C),
                                          level_mask[:, m % NL, :].unsqueeze(1).broadcast_to([P, 2 * TT, C]),
                                          side[m % 2][:, :].rearrange("p (n s) -> p n s", s=C)).then_inc(level_copied, 1)

            def bound_gate(n):
                dve.wait_ge(silu_exp, n + 1)
                nc.vector.tensor_scalar(gate_e(n), gate_e(n), 1.0, 1.0e19, ALU.add, ALU.min).then_inc(silu_bound, 1)

            def finish_gate(n, result, dst):
                dve.wait_ge(silu_sig, n + 1)
                ins = nc.vector.tensor_tensor(out=dst, in0=acc[result % 4][:, :], in1=gate_e(n), op=ALU.mult)
                ins.then_inc(freed["dve"], 1)

            def log_sum(j):
                dve.wait_ge(log_made, j + 1)
                nc.vector.tensor_tensor_scan(out=b_cum[:, j, :], data0=chunk_keep[:, :], data1=b_cum[:, j, :], initial=0.0,
                                             op0=ALU.mult, op1=ALU.add).then_inc(b_made, 1)

            def prepare_head(n):
                b = b_cum[:, n, :].rearrange("p (c t) -> p c t", t=C)
                if n:
                    dve.wait_ge(kT_made, n)
                else:
                    dve.wait_ge(scores_made, 4 * NL)
                nc.vector.tensor_tensor(out=k_dec[:, :].rearrange("p (c t) -> p c t", t=C),
                                        in0=b[:, :, C - 1:C].broadcast_to([P, NC, C]), in1=b, op=ALU.subtract)\
                    .then_inc(decay_diff, 1)
                dve.wait_ge(decay_exp, 2 * n + 1)
                nc.vector.tensor_copy(b_end[:, n % 2, :], e_b[:, :].rearrange("p (c t) -> p c t", t=C)[:, :, C - 1])
                if n >= 2:
                    dve.wait_ge(o_made, n - 1)
                nc.vector.tensor_tensor(out=q_dec[:, n % 2, :], in0=e_b[:, :], in1=queries[:, n, :], op=ALU.mult)
                dve.wait_ge(decay_exp, 2 * n + 2)
                nc.vector.tensor_tensor(out=k_dec[:, :], in0=k_dec[:, :], in1=keys[:, n, :], op=ALU.mult)\
                    .then_inc(prep_made, 1)

            def chain_states(n):
                dve.wait_ge(outer_made, n + 1)
                if n:
                    dve.wait_ge(o_made, n)
                then(nc.vector.tensor_copy(states[:, 0, :], side[1][:, 0:P]))
                for c in range(1, NC - 1):
                    ins = nc.vector.scalar_tensor_tensor(
                        out=states[:, c, :], in0=states[:, c - 1, :], scalar=b_end[:, n % 2, c:c + 1],
                        in1=side[1 + c % 2][:, (c // 2) * P:(c // 2 + 1) * P], op0=ALU.mult, op1=ALU.add)
                    if c < NC - 2:
                        then(ins)
                    else:
                        ins.then_inc(states_made, 1)

            def finish_head(n):
                dve.wait_ge(o_rstd, n + 1)
                then(nc.vector.tensor_tensor(out=o_sb[:, :], in0=o_sb[:, :], in1=o_sq[:, :], op=ALU.mult))
                nc.vector.scalar_tensor_tensor(out=o_sb[:, :], in0=o_sb[:, :], scalar=par[:, PAR["nw"]],
                                               in1=silu_out[:, n % 2, :], op0=ALU.mult, op1=ALU.mult).then_inc(o_final, 1)
                dve.wait_ge(o_final, n + 1)
                dve.wait_ge(mixh_hi_made, n + 1)
                nc.vector.tensor_tensor(out=mixh_lo[:, n, :], in0=o_sb[:, :], in1=mixh_hi[:, n, :].bitcast(f32),
                                        op=ALU.subtract).then_inc(mixh_made, 1)

            def end_tile(gate, raws):
                name, kt = FINAL[finals[0]]
                if finals[0]:
                    dve.wait_ge(y_made, finals[0])
                nc.vector.tensor_tensor(out=y_tmp[:, :], in0=gate, in1=raws[name][:, kt, :], op=ALU.mult).then_inc(y_final, 1)
                finals[0] += 1
                dve.wait_ge(y_final, finals[0])
                dve.wait_ge(y_hi_made, finals[0])
                nc.vector.tensor_tensor(out=y_lo[name][:, kt, :], in0=y_tmp[:, :], in1=y_hi[name][:, kt, :].bitcast(f32),
                                        op=ALU.subtract).then_inc(y_made, 1)

            def enter_second_block():
                for n in range(2 * TT):
                    t, half = n // 2, n % 2
                    dve.wait_ge(x2T_made, n + 1)
                    if n >= 2:
                        dve.wait_ge(h2_made, n - 1)
                    gain = par[:, PAR["norm_g"]][:, 4 * half:4 * half + 4].unsqueeze(2).broadcast_to([P, 4, P])
                    nc.vector.tensor_tensor(out=h2_full[:, n % 2, :].rearrange("p (k s) -> p k s", s=P),
                                            in0=side[n % 4][:, :].rearrange("p (k s) -> p k s", s=P), in1=gain,
                                            op=ALU.mult).then_inc(h2_full_made, 1)
                    dve.wait_ge(h2_full_made, n + 1)
                    dve.wait_ge(h2_hi_made, n + 1)
                    tiles = (slice(None), slice(4 * half, 4 * half + 4), slice(t * P, (t + 1) * P))
                    nc.vector.tensor_tensor(out=hT_lo[tiles], in0=h2_full[:, n % 2, :].rearrange("p (k s) -> p k s", s=P),
                                            in1=hT_hi[tiles].bitcast(f32), op=ALU.subtract).then_inc(h2_made, 1)

            def side_slot(slot):
                for s in SCORES_AT.get(slot, []):
                    w = (s // 4 % TT + 1) * P
                    dve.wait_ge(logits_made, s + 1)
                    col = slice(s, s + 1)
                    if s < SPARSE:
                        nc.vector.tensor_reduce(out=top_neg[:, col], in_=side[s % 2][:, 0:w], axis=AX.X, op=ALU.max,
                                                negate=True).then_inc(max_made, 1)
                    else:
                        cq = cum_q[:, s - SPARSE:s - SPARSE + 1]
                        then(nc.vector.tensor_reduce(out=top_max[:, col], in_=side[s % 2][:, 0:w], axis=AX.X, op=ALU.max))
                        then(nc.vector.tensor_tensor(out=top_max[:, col], in0=top_max[:, col], in1=cq, op=ALU.add))
                        nc.vector.tensor_tensor(out=top_neg[:, col], in0=cq, in1=top_max[:, col], op=ALU.subtract)\
                            .then_inc(max_made, 1)
                for s in SCORES_AT.get(slot, []):
                    w = (s // 4 % TT + 1) * P
                    dve.wait_ge(exp_made, s + 1)
                    then(nc.vector.reciprocal(row_inv[:, s:s + 1], row_sum[:, s:s + 1]))
                    nc.vector.tensor_scalar(probs[:, s % 2, 0:w], probs[:, s % 2, 0:w], row_inv[:, s:s + 1], None, ALU.mult)\
                        .then_inc(probs_made, 1)

            def topk_round(t, r):
                w = (t + 1) * P
                sc = score[:, t - 1, 0:w]
                if r == 0:
                    dve.wait_ge(cut_made, t)
                then(nc.vector.max(top8, sc))
                then(nc.vector.match_replace(sc, top8, sc, TAKEN))
                if r == ROUNDS - 1:
                    nc.vector.tensor_scalar(sel16[:, t - 1, 0:w], sc, (OUTSIDE + TAKEN) / 2, NEG, ALU.is_gt, ALU.mult)\
                        .then_inc(sel_made, 1)

            dve.wait_ge(consts, 8)
            nc.vector.tensor_copy(ident16[:, :], ident[:, :])
            nc.vector.tensor_copy(pick[:, :], pick_f[0:36, :]).then_inc(pick_made, 1)
            then(nc.vector.tensor_scalar(idx[:, 1, :], idx[:, 1, :], C - 1, None, ALU.bitwise_and))
            then(nc.vector.tensor_tensor(out=later[:, :], in0=idx[:, 0, :], in1=idx[:, 1, :], op=ALU.is_gt))
            then(nc.vector.tensor_tensor(out=idx[:, 0, :], in0=idx[:, 0, :], in1=idx[:, 1, :], op=ALU.bitwise_xor))
            nc.vector.tensor_scalar(level_mask[:, NL - 1, :], idx[:, 0, :], 0, None, ALU.is_equal)
            then(nc.vector.tensor_tensor(out=later[:, :], in0=idx[:, 0, :], in1=later[:, :], op=ALU.mult))
            for l, half in enumerate(LEVELS[:-1]):
                then(nc.vector.tensor_scalar(junk[:, 0:C], later[:, :], float(half), None, ALU.is_ge))
                then(nc.vector.scalar_tensor_tensor(out=level_mask[:, l, :], in0=later[:, :], scalar=float(2 * half),
                                                    in1=junk[:, 0:C], op0=ALU.is_lt, op1=ALU.mult))
            for r in range(16):
                nc.vector.memset(inv_count[:, r:r + 1], 1.0 / (r + 1))
            dve.wait_ge(par_here, 16)
            nc.vector.tensor_tensor(out=low_b, in0=par[:, PAR["lb"]], in1=par[:, PAR["lb"]], op=ALU.subtract)\
                .then_inc(lb_diff, 1)
            dve.wait_ge(c_exp, 1)
            then(nc.vector.tensor_scalar(tmp8, tmp8, 1.0, None, ALU.add))
            then(nc.vector.reciprocal(tmp8, tmp8))
            then(nc.vector.tensor_tensor(out=silu_c, in0=tmp8, in1=par[:, PAR["c"]], op=ALU.mult))
            dve.wait_ge(lb_exp, 1)
            then(nc.vector.reciprocal(tmp8, one_low))
            then(nc.vector.tensor_tensor(out=one_low, in0=one_low, in1=tmp8, op=ALU.mult))
            then(nc.vector.tensor_tensor(out=low_b, in0=one_low, in1=one_low, op=ALU.subtract))
            then(nc.vector.tensor_scalar(one_low, low_b, -1.0, 1.0, ALU.mult, ALU.add))
            for j in range(16):
                add_ada("ada", j)
            dve.wait_ge(mod_summed, 1)
            then(nc.vector.tensor_tensor(out=mod, in0=side[0][:, 0:16], in1=par[:, PAR["ada_b"]], op=ALU.add))
            then(nc.vector.scalar_tensor_tensor(out=scale_a, in0=mod[:, 8:16], scalar=1.0, in1=par[:, PAR["pre_w"]],
                                                op0=ALU.add, op1=ALU.mult))
            for kt in range(KT):
                dve.wait_ge(xT_copied, kt + 1)
                nc.vector.tensor_scalar(hT_full[:, kt, :], hT_full[:, kt, :], scale_a[:, kt:kt + 1], mod[:, kt:kt + 1],
                                        ALU.mult, ALU.add).then_inc(h_full, 1)
            split_lo(0)
            for kt in range(KT):
                dve.wait_ge(h_full, kt + 1)
                dve.wait_ge(h_hi, kt + 1)
                nc.vector.tensor_tensor(out=hT_lo[:, kt, :], in0=hT_full[:, kt, :], in1=hT_hi[:, kt, :].bitcast(f32),
                                        op=ALU.subtract).then_inc(h_lo, 1)
            for k in range(1, AHEAD):
                split_lo(k)

            gates = 0
            finals = [0]
            before = (None, 0)
            for k, (kind, j) in enumerate(USED):
                if k + AHEAD < len(USED):
                    split_lo(k + AHEAD)
                if before[0] in ("gp", "gh"):
                    finish_gate(gates - 1, RESULT[before], silu_out[:, before[1] % 2, :])
                if before[0] == "dz":
                    finish_gate(gates - 1, RESULT[before], z_d[:, before[1], :])
                if before[0] in ("az", "bz", "cz"):
                    if finals[0]:
                        dve.wait_ge(y_made, finals[0])
                    finish_gate(gates - 1, RESULT[before], y_tmp[:, :])
                    dve.wait_ge(freed["dve"], FREED[RESULT[before]][1])
                    end_tile(y_tmp[:, :], y_raw)
                if k == D_FINAL_AT:
                    dve.wait_ge(bank3_read, 2 * TT)
                    for h in range(4):
                        end_tile(z_d[:, h, :], y_raw)
                before = (kind, j)
                m = LEVEL_AT.get((kind, j))
                if m is not None:
                    scale_level(m)
                    diff_level(m + 1)
                    if m:
                        copy_level(m - 1)
                if k - 2 in range(HEADS):
                    log_sum(k - 2)
                if k - 1 in range(HEADS):
                    h = k - 1
                    dve.wait_ge(f_sig, h + 1)
                    then(nc.vector.tensor_scalar(b_cum[:, h, :], b_cum[:, h, :], one_low[:, h:h + 1], low_b[:, h:h + 1],
                                                 ALU.mult, ALU.add))
                    nc.vector.tensor_scalar(keys[:, h, :], b_cum[:, h, :], -1.0, 1.0, ALU.mult, ALU.add).then_inc(f_made, 1)
                if kind == "f":
                    wait_freed(dve, RESULT[kind, j])
                    nc.vector.tensor_scalar(b_cum[:, j, :], b_cum[:, j, :], 1.0, 1.0e19, ALU.add, ALU.min).then_inc(f_bound, 1)
                if (kind, j) == ("q", 7):
                    wait_freed(dve, RESULT["q", 7])
                    dve.wait_ge(b_made, HEADS)
                    dve.wait_ge(f_made, HEADS)
                    diff_level(0)
                if (kind, j % 2) == ("gp", 0):
                    g, w = j // 2, 2 << (j // 2)
                    total, diff = sums[g % 2], sums[(g + 1) % 2][:, :, 0:S]
                    dve.wait_ge(sum_made, g + 1)
                    then(nc.vector.scalar_tensor_tensor(out=diff, in0=total[:, :, 16:], scalar=1.0 / w,
                                                        in1=u_pad[:, :, 16:], op0=ALU.mult, op1=ALU.subtract))
                    then(nc.vector.tensor_tensor(out=diff[:, :, 0:w - 1], in0=total[:, :, 16:15 + w],
                                                 in1=inv_count[:, 0:w - 1].unsqueeze(1).broadcast_to([P, 2, w - 1]),
                                                 op=ALU.mult))
                    nc.vector.tensor_tensor(out=diff[:, :, 0:w - 1], in0=diff[:, :, 0:w - 1],
                                            in1=u_pad[:, :, 16:15 + w], op=ALU.subtract).then_inc(d_made, 1)
                if kind in GATES:
                    bound_gate(gates)
                    gates += 1
                if (kind, j % 2) == ("gp", 0):
                    dve.wait_ge(d_hi_made, g + 1)
                    dve.wait_ge(d_made, g + 1)
                    nc.vector.tensor_tensor(out=d_lo[:, :, :], in0=diff, in1=d_hi[:, :, :].bitcast(f32),
                                            op=ALU.subtract).then_inc(d_lo_made, 1)
                if kind == "pw":
                    dve.wait_ge(unit_used, k + 1)
                    wait_freed(dve, RESULT["gp", 2 * j + 1])
                    for o in range(2):
                        r = RESULT["pw", j] + o
                        nc.vector.scalar_tensor_tensor(out=mix_pool[:, 2 * j + o, :], in0=acc[r % 4][:, :],
                                                       scalar=par[:, PAR["pool_scale"]][:, 2 * j + o:2 * j + o + 1],
                                                       in1=silu_out[:, o, :], op0=ALU.mult, op1=ALU.mult)\
                            .then_inc(freed["dve"], 1)
                if (kind, j) == ("i", 7):
                    copy_level(4 * NL - 1)
                    prepare_head(0)
                n = HEAD_AT.get((kind, j))
                if n is not None:
                    if n + 1 < HEADS:
                        prepare_head(n + 1)
                    if n < HEADS:
                        chain_states(n)
                    if n:
                        finish_head(n - 1)
                if (kind, j) == ("gh", 7):
                    for kt in range(KT):
                        dve.wait_ge(mixp_hi_made, kt + 1)
                        nc.vector.tensor_tensor(out=mixp_lo[:, kt, :], in0=mix_pool[:, kt, :],
                                                in1=mixp_hi[:, kt, :].bitcast(f32), op=ALU.subtract).then_inc(mixp_made, 1)
                if (kind, j) == ("wo", 10):
                    dve.wait_ge(gate_summed, 2)
                    dve.wait_ge(rows_here, 32)
                    for o in range(2):
                        half = slice(o * S, (o + 1) * S)
                        then(nc.vector.tensor_tensor(out=gate_row[:, half], in0=side[1 + o][:, :], in1=gate_row[:, half],
                                                     op=ALU.add))
                        then(nc.vector.tensor_tensor(out=gate_post[:, half], in0=gate_row[:, half], in1=post_row[:, half],
                                                     op=ALU.mult))
                if (kind, j) == ("wo", 15):
                    dve.wait_ge(x_again_here, 16)
                    for t in range(TT):
                        dve.wait_ge(y_squared, t + 1)
                        nc.vector.tensor_tensor(out=ss_y[:, 8 + t:9 + t], in0=ss_y[:, t:t + 1], in1=ss_y[:, 4 + t:5 + t],
                                                op=ALU.add).then_inc(y_total, 1)
                    for t in range(TT):
                        r = RESULT["wo", 1] + t
                        dve.wait_ge(y_rstd, t + 1)
                        nc.vector.scalar_tensor_tensor(out=x2[:, t, 0:S], in0=y_sb[:, t, 0:S], scalar=rstd_y[:, t:t + 1],
                                                       in1=gate_post[:, 0:S], op0=ALU.mult, op1=ALU.mult)
                        ins = nc.vector.scalar_tensor_tensor(out=x2[:, t, S:D], in0=acc[r % 4][:, :],
                                                             scalar=rstd_y[:, t:t + 1], in1=gate_post[:, S:D],
                                                             op0=ALU.mult, op1=ALU.mult)
                        ins.then_inc(freed["dve"], 1)
                        dve.wait_ge(freed["dve"], FREED[r][1])
                        nc.vector.tensor_tensor(out=x2[:, t, :], in0=x2[:, t, :], in1=x_again[:, t, :], op=ALU.add)\
                            .then_inc(x2_made, 1)
                    enter_second_block()
                r = RESULT.get((kind, j))
                if (kind, j) == ("bs", 3):
                    dve.wait_ge(small_rows, 32)
                    dve.wait_ge(lat_rstd, 1)
                    for twice in range(2):
                        then(nc.vector.tensor_copy(key_twice[:, :, 64 * twice:64 * twice + 64], side_tok[:, :, 384:448]))
                    for t in range(TT):
                        ins = nc.vector.scalar_tensor_tensor(out=lat[:, t, :], in0=side_tok[:, t, 0:P],
                                                             scalar=rstd_kv[:, t:t + 1], in1=kv_row[:, :],
                                                             op0=ALU.mult, op1=ALU.mult)
                        ins.then_inc(lat_made, 1)
                    then(nc.vector.tensor_scalar(idx_w.rearrange("p (t h) -> p t h", h=4), side_tok[:, :, 448:452], 0.5,
                                                 None, ALU.mult))
                if kind == "bq" and j:
                    w = (j + 1) * P
                    for h in range(4):
                        n = 4 * (j - 1) + h
                        dve.wait_ge(relu_made, n + 1)
                        if h:
                            dve.wait_ge(relu_used, n)
                        weight = idx_w[:, 4 * j + h:4 * j + h + 1]
                        sc = score[:, j - 1, 0:w]
                        if h == 0:
                            ins = nc.vector.tensor_scalar(sc, relu[:, n % 2, 0:w], weight, None, ALU.mult)
                        else:
                            ins = nc.vector.scalar_tensor_tensor(out=sc, in0=relu[:, n % 2, 0:w], scalar=weight, in1=sc,
                                                                 op0=ALU.mult, op1=ALU.add)
                        ins.then_inc(relu_used, 1)
                if (kind, j) == ("av", 3):
                    for t in range(TT):
                        dve.wait_ge(unit_used, k + 1)
                        then(nc.vector.bn_stats(bn[:, 6 * t:6 * t + 6], acc[(RESULT["av", 0] + t) % 4][:, :]))
                    for t in range(TT):
                        ins = nc.vector.bn_aggr(bn_mean[:, 2 * t:2 * t + 2], bn[:, 6 * t:6 * t + 6])
                    ins.then_inc(bn_made, 1)
                    dve.wait_ge(bn_made, 1)
                    dve.wait_ge(bn_rstd, 1)
                    dve.wait_ge(spatial_here, 64)
                    for t in range(TT):
                        r = RESULT["av", 0] + t
                        nc.vector.tensor_scalar(v_norm[:, t, :], acc[r % 4][:, :], bn_mean[:, 2 * t:2 * t + 1],
                                                rstd_v[:, t:t + 1], ALU.subtract, ALU.mult).then_inc(freed["dve"], 1)
                    for t in range(TT):
                        wait_freed(dve, RESULT["av", 0] + t)
                        then(nc.vector.tensor_tensor(out=v_norm[:, t, :], in0=v_norm[:, t, :], in1=ln_rows[:, 0, :],
                                                     op=ALU.mult))
                        nc.vector.tensor_tensor(out=v_norm[:, t, :], in0=v_norm[:, t, :], in1=ln_rows[:, 1, :],
                                                op=ALU.add).then_inc(v_made, 1)
                if kind == "cx":
                    wait_freed(dve, RESULT["cc", j])
                    dve.wait_ge(unit_used, k + 1)
                    if j == 0:
                        then(nc.vector.memset(conv_in[:, 0:2], 0.0))
                    nc.vector.tensor_tensor(out=conv_in[:, 2:], in0=acc[r % 4][:, :], in1=c_gate[:, :], op=ALU.mult)\
                        .then_inc(freed["dve"], 1)
                    wait_freed(dve, r)
                    taps = par[:, PAR["conv_w"]]
                    then(nc.vector.tensor_scalar(conv[:, :], conv_in[:, 0:S], taps[:, j:j + 1], None, ALU.mult))
                    for tap in (1, 2):
                        then(nc.vector.scalar_tensor_tensor(out=conv[:, :], in0=conv_in[:, tap:tap + S],
                                                            scalar=taps[:, 4 * tap + j:4 * tap + j + 1], in1=conv[:, :],
                                                            op0=ALU.mult, op1=ALU.add))
                if kind == "cb":
                    dve.wait_ge(unit_used, k + 1)
                    nc.vector.tensor_tensor(out=y_raw["c"][:, j, :], in0=acc[r % 4][:, :], in1=conv[:, :], op=ALU.mult)\
                        .then_inc(freed["dve"], 1)
                slot = k - SLOT0
                side_slot(slot)
                if slot in MIXED_AT:
                    g = MIXED_AT[slot]
                    dve.wait_ge(mixed_made, g + 1)
                    wait_freed(dve, RESULT["au", g])
                    nc.vector.tensor_tensor(out=y_tmp2.rearrange("p (c t) -> p c t", t=P),
                                            in0=side[g % 2][:, :].rearrange("p (c t) -> p c t", t=P),
                                            in1=mix_b[:, g, :].unsqueeze(1).broadcast_to([P, TT, P]), op=ALU.add)\
                        .then_inc(mixed_read, 1)
                    dve.wait_ge(mixed_read, g + 1)
                    then(nc.vector.tensor_tensor(out=y_raw["a"][:, g, :], in0=y_raw["a"][:, g, :], in1=y_tmp2, op=ALU.mult))
                if slot == FORGET_AT:
                    dve.wait_ge(fgt_made, 1)
                    then(nc.vector.memset(forget_r[:, :].bitcast(f32), 0.0))
                    then(nc.vector.tensor_scalar(forget[:, 0, :], side[0][0:4, :], bf_col[0:4, :], None, ALU.add))
                    then(nc.vector.tensor_scalar(forget[:, 1, :], forget[:, 0, :], -1.0, None, ALU.mult))
                    nc.vector.tensor_tensor(out=forget[:, 1, :], in0=forget[:, 0, :], in1=forget[:, 1, :], op=ALU.max)\
                        .then_inc(fgt_abs, 1)
                    dve.wait_ge(fgt_abs, 1)
                    then(nc.vector.tensor_scalar(forget[:, 0, :], forget[:, 0, :], 0.0, None, ALU.min))
                    dve.wait_ge(fgt_ln, 1)
                    then(nc.vector.tensor_tensor(out=forget[:, 0, :], in0=forget[:, 0, :], in1=forget[:, 1, :],
                                                 op=ALU.subtract))
                    then(nc.vector.memset(forget[:, 1, :], 1.0))
                    nc.vector.tensor_tensor_scan(out=forget[:, 0, :], data0=forget[:, 1, :], data1=forget[:, 0, :],
                                                 initial=0.0, op0=ALU.mult, op1=ALU.add).then_inc(fgt_sum, 1)
                    dve.wait_ge(fgt_sum, 1)
                    dve.wait_ge(fgt_hi, 1)
                    then(nc.vector.tensor_tensor(out=forget[:, 1, :], in0=forget[:, 0, :],
                                                 in1=forget_r[0:4, :].bitcast(f32), op=ALU.add))
                    nc.vector.tensor_scalar(forget_r[32:36, :], forget[:, 1, :], -1.0, None, ALU.mult).then_inc(fgt_ready, 1)
                if slot == CUM_AT:
                    dve.wait_ge(cum_made, 1)
                    nc.vector.tensor_copy(cum_q, side[1][:, 0:16]).then_inc(cum_read, 1)
                for t, rr in topk_rounds(slot):
                    topk_round(t, rr)
                if kind == "br":
                    dve.wait_ge(unit_used, k + 1)
                    for o in range(2):
                        g = 2 * j + o
                        wait_freed(dve, RESULT["ga", g])
                        first = g % 4 == 0
                        if first and j >= 2:
                            dve.wait_ge(m_made, j // 2)
                        dst = merged[:, :] if first else merged_part[:, :]
                        nc.vector.tensor_tensor(out=dst, in0=acc[(r + o) % 4][:, :], in1=sig[:, g % 2, :], op=ALU.mult)\
                            .then_inc(freed["dve"], 1)
                        wait_freed(dve, r + o)
                        if not first:
                            ins = nc.vector.tensor_tensor(out=merged[:, :], in0=merged[:, :], in1=merged_part[:, :],
                                                          op=ALU.add)
                            if g % 4 == 3:
                                ins.then_inc(m_sum, 1)
                            else:
                                then(ins)
                    if j % 2:
                        dve.wait_ge(m_sum, j // 2 + 1)
                        dve.wait_ge(m_hi_made, j // 2 + 1)
                        nc.vector.tensor_tensor(out=m_lo[:, j // 2, :], in0=merged[:, :],
                                                in1=m_hi[:, j // 2, :].bitcast(f32), op=ALU.subtract).then_inc(m_made, 1)
                if (kind, j) == ("w2", 3) or (kind, j) == ("w2", 7):
                    half = j // 4
                    dve.wait_ge(unit_used, k + 1)
                    cols_ = slice(half * S, (half + 1) * S)
                    for t in range(TT):
                        r = RESULT["w2", half] + t
                        nc.vector.tensor_tensor(out=x2[:, t, cols_], in0=acc[r % 4][:, :], in1=x2[:, t, cols_],
                                                op=ALU.add).then_inc(freed["dve"], 1)
                    if half:
                        for t in range(TT):
                            dve.wait_ge(h_sq, 5 + t)
                            nc.vector.tensor_tensor(out=rstd_o[:, 4 + t:5 + t], in0=ss_o[:, t:t + 1],
                                                    in1=ss_o[:, 4 + t:5 + t], op=ALU.add).then_inc(h_tot, 1)
                        dve.wait_ge(final_here, 16)
                        for t in range(TT):
                            dve.wait_ge(h_rstd, t + 1)
                            nc.vector.scalar_tensor_tensor(out=x2[:, t, :], in0=x2[:, t, :], scalar=rstd_o[:, t:t + 1],
                                                           in1=final_row[:, :], op0=ALU.mult, op1=ALU.mult)\
                                .then_inc(out_made, 1)

        @block.tensor
        def _(pe):
            def weights(k):
                pe.wait_ge(lo_made, k + 1)
                return w_hi[:, k % SPLITS, :], w_lo[:, k % SPLITS, :]

            def bank(result):
                if result >= 4:
                    wait_freed(pe, result - 4)
                return acc[result % 4]

            def product(ps, w, x, first, last):
                nc.tensor.matmul(ps, w[0], x[0], start=first, stop=False)
                nc.tensor.matmul(ps, w[0], x[1], start=False, stop=False)
                return nc.tensor.matmul(ps, w[1], x[0], start=False, stop=last)

            def panel(k, kind, j, x, tiles, ready=None):
                hi, lo = weights(k)
                ps = bank(RESULT[kind, j])
                for kt in range(tiles):
                    if ready is not None:
                        pe.wait_ge(ready, kt + 1)
                    cols = slice(kt * P, (kt + 1) * P)
                    ins = product(ps[:, :], (hi[:, cols], lo[:, cols]), (x[0][:, kt, :], x[1][:, kt, :]),
                                  kt == 0, kt == tiles - 1)
                ins.then_inc(unit_used, 1)

            def token_unit(k, kind, j, source, width):
                hi, lo = weights(k)
                per = TOKEN_UNITS[kind]
                for t in range(TT):
                    r = RESULT[kind, j // per] + t
                    ps = bank(r) if j % per == 0 else acc[r % 4]
                    for a in range(2):
                        x = source(2 * (j % per) + a)
                        tok = slice(t * P, (t + 1) * P)
                        cols = slice(a * width, (a + 1) * width)
                        ins = product(ps[:, 0:width], (x[0][:, tok], x[1][:, tok]), (hi[:, cols], lo[:, cols]),
                                      j % per == 0 and a == 0, j % per == per - 1 and a == 1)
                ins.then_inc(unit_used, 1)

            def level_scores(m):
                g = m // NL
                if LEVELS[m % NL]:
                    pe.wait_ge(level_x, pair_levels(m))
                if m >= 2:
                    pe.wait_ge(level_copied, m - 1)
                for h in range(2):
                    for c in range(NC):
                        cols = slice(h * S + c * C, h * S + (c + 1) * C)
                        if LEVELS[m % NL]:
                            left = right = xq[:, m % 2, cols]
                        else:
                            left, right = (t[:, 2 * g + h, c * C:(c + 1) * C] for t in (keys, queries))
                        p0, n0 = (c % 2) * C, h * (S // 2) + (c // 2) * C
                        ins = nc.tensor.matmul(side[m % 2][p0:p0 + C, n0:n0 + C], left, right, start=True, stop=True)
                ins.then_inc(scores_made, 1)

            def transpose_keys(n):
                pe.wait_ge(prep_made, n + 1)
                if n >= 2:
                    pe.wait_ge(o_rstd, n - 1)
                elif n == 0:
                    pe.wait_ge(level_copied, 4 * NL)
                for t in range(TT):
                    ins = nc.tensor.transpose(side[0][:, t * P:(t + 1) * P], k_dec[:, t * P:(t + 1) * P], ident[:, :])
                ins.then_inc(kT_made, 1)

            def outer_products(n):
                pe.wait_ge(kT_copied, n + 1)
                if n:
                    pe.wait_ge(states_made, n)
                for c in range(NC - 1):
                    rows = slice((c % 2) * C, (c % 2 + 1) * C)
                    ins = nc.tensor.matmul(side[1 + c % 2][:, (c // 2) * P:(c // 2 + 1) * P], k_decT[rows, c // 2, :],
                                           values[rows, c // 2, n * P:(n + 1) * P], start=True, stop=True)
                ins.then_inc(outer_made, 1)

            def head_output(n):
                pe.wait_ge(states_made, n + 1)
                if n:
                    pe.wait_ge(o_squared, n)
                for c in range(1, NC):
                    cols = slice(c * C, (c + 1) * C)
                    nc.tensor.matmul(side[3][:, cols], states[:, c - 1, :], q_dec[:, n % 2, cols],
                                     start=(c == 1), stop=False)
                for parity in range(2):
                    if parity:
                        even.then_inc(even_made, 1)
                        pe.wait_ge(even_made, n + 1)
                    rows = slice(parity * C, (parity + 1) * C)
                    for c in range(parity, NC, 2):
                        ins = nc.tensor.matmul(side[3][:, c * C:(c + 1) * C], values[rows, c // 2, n * P:(n + 1) * P],
                                               attn[rows, n, (c // 2) * C:(c // 2 + 1) * C], start=False,
                                               stop=(c == NC - 1))
                    even = ins
                ins.then_inc(o_made, 1)

            def head_mean_squares(n):
                pe.wait_ge(o_squared, n + 1)
                nc.tensor.matmul(side[0][:, :], ones[:, :], o_sq[:, :], start=True, stop=True).then_inc(ms_made, 1)

            def enter_second_block():
                for n in range(2 * TT):
                    t, half = n // 2, n % 2
                    pe.wait_ge(x2_normed, t + 1)
                    if n >= 4:
                        pe.wait_ge(h2_full_made, n - 3)
                    for i in range(4):
                        ins = nc.tensor.transpose(side[n % 4][:, i * P:(i + 1) * P],
                                                  y_sb[:, t, (4 * half + i) * P:(4 * half + i + 1) * P], ident[:, :])
                    ins.then_inc(x2T_made, 1)
                pe.wait_ge(h2_made, 2 * TT)

            def turn(s):
                n = BANK2.index(("turn", s))
                pe.wait_ge(probs_made, s + 1)
                if n:
                    pe.wait_ge(bank2_read, n)
                for b in range(s // 4 % TT + 1):
                    ins = nc.tensor.transpose(side[2][:, b * P:(b + 1) * P], probs[:, s % 2, b * P:(b + 1) * P], ident[:, :])
                ins.then_inc(turned, 1)

            def sum_values(s):
                n = BANK2.index(("turn", s))
                pe.wait_ge(bank2_read, n + 1)
                h, blocks = s % 4, s // 4 % TT + 1
                if h == 0 and s:
                    pe.wait_ge(bank3_read, s // 4)
                if s == SPARSE:
                    wait_freed(pe, RESULT["dv", 0] + 3)
                for b in range(blocks):
                    v = lat[:, b, :] if s < SPARSE else fox_v[:, b, h * P:(h + 1) * P]
                    ins = nc.tensor.matmul(side[3][:, h * P:(h + 1) * P], v, probsT[:, s % 2, b * P:(b + 1) * P],
                                           start=(b == 0), stop=(b == blocks - 1))
                ins.then_inc(summed, 1)

            def logits(s):
                q, h = s // 4 % TT, s % 4
                w = (q + 1) * P
                ps = side[s % 2]
                tok = slice(q * P, (q + 1) * P)
                if s >= 2:
                    pe.wait_ge(exp_made, s - 1)
                if s < SPARSE:
                    if s == 0:
                        pe.wait_ge(latq_copied, 4)
                    if q:
                        pe.wait_ge(sel_made, q)
                    nc.tensor.matmul(ps[:, 0:w], lat_q[:, h, tok], latT[:, 0:w], start=True, stop=False)
                    bias = sel16[:, q - 1, 0:w] if q else causal16[:, :]
                    ins = nc.tensor.matmul(ps[:, 0:w], ident16[:, :], bias, start=False, stop=True)
                else:
                    if s == SPARSE:
                        wait_freed(pe, RESULT["dk", 3])
                        pe.wait_ge(fgt_ready, 1)
                        pe.wait_ge(cum_read, 1)
                    nc.tensor.matmul(ps[:, 0:w], fox_q[:, h, tok], fox_k[:, h, 0:w], start=True, stop=False)
                    nc.tensor.matmul(ps[:, 0:w], pick[:, h:h + 1].broadcast_to([36, P]), forget_r[:, 0:w],
                                     start=False, stop=False)
                    ins = nc.tensor.matmul(ps[:, w - P:w], ident16[:, :], causal16[:, :], start=False, stop=True)
                ins.then_inc(logits_made, 1)

            def side_slot(slot):
                turns, sums_ = TURN_AT.get(slot, []), SUM_AT.get(slot, [])
                for i in range(max(len(turns), len(sums_))):
                    if i < len(turns):
                        turn(turns[i])
                    if i < len(sums_):
                        sum_values(sums_[i])
                if slot in UP_AT:
                    q = UP_AT[slot]
                    n = BANK2.index(("up", q))
                    pe.wait_ge(bank2_read, n)
                    pe.wait_ge(bank3_read, q + 1)
                    for h in range(4):
                        ins = nc.tensor.matmul(side[2][:, h * P:(h + 1) * P], w_up[:, 1, h, :],
                                               lat_out[:, h * P:(h + 1) * P], start=True, stop=True)
                    ins.then_inc(turned, 1)
                for s in SCORES_AT.get(slot, []):
                    if 6 <= s <= 9:
                        pe.wait_ge(mixed_read, s - 5)
                    logits(s)
                if slot in MIXED_AT:
                    g = MIXED_AT[slot]
                    pe.wait_ge(v_made, TT)
                    pe.wait_ge(masked, 1)
                    pe.wait_ge(exp_made, 5 + g)
                    for t in range(TT):
                        ins = nc.tensor.matmul(side[g % 2][:, t * P:(t + 1) * P], v_norm[:, t, g * P:(g + 1) * P],
                                               mixT[:, g, :], start=True, stop=True)
                    ins.then_inc(mixed_made, 1)

            pe.wait_ge(consts, 2)
            for t in range(TT):
                pe.wait_ge(x_normed, t + 1)
                for kt in range(KT):
                    ins = nc.tensor.transpose((acc + side)[kt][:, t * P:(t + 1) * P], x_in[:, t, kt * P:(kt + 1) * P],
                                              ident[:, :])
                    if t == TT - 1:
                        ins.then_inc(xT_made, 1)
            pe.wait_ge(ada_summed, 16)
            pe.wait_ge(xT_copied, KT)
            for o in range(16):
                ins = nc.tensor.matmul(side[0][:, o:o + 1], ada_acc[:, o * P:(o + 1) * P], ones[:, 0:1],
                                       start=True, stop=True)
            ins.then_inc(mod_summed, 1)

            for k, (kind, j) in enumerate(USED):
                if (kind, j) == ("bs", 0):
                    enter_second_block()
                if kind in PANELS:
                    panel(k, kind, j, (hT_hi, hT_lo), KT, h_lo if k == 0 else None)
                if kind in ("i", "bs", "av", "dv"):
                    token_unit(k, kind, j, lambda kt: (hT_hi[:, kt, :], hT_lo[:, kt, :]), SIDE if kind == "bs" else S)
                if kind == "br":
                    hi, lo = weights(k)
                    for o in range(2):
                        name = "abcd"[2 * (j % 2) + o]
                        pe.wait_ge(y_made, 1 + FINAL.index((name, 3)))
                        ps = bank(RESULT[kind, j] + o)
                        for kt in range(4):
                            cols = slice((4 * o + kt) * P, (4 * o + kt + 1) * P)
                            ins = product(ps[:, :], (hi[:, cols], lo[:, cols]),
                                          (y_hi[name][:, kt, :], y_lo[name][:, kt, :]), kt == 0, kt == 3)
                    ins.then_inc(unit_used, 1)
                if kind == "w2":
                    pe.wait_ge(m_made, 2 * (j % 4) + 2)
                    token_unit(k, kind, j, lambda kt: (m_hi[:, kt, :], m_lo[:, kt, :]), S)
                if kind == "pw":
                    pe.wait_ge(d_lo_made, j + 1)
                    hi, lo = weights(k)
                    for o in range(2):
                        ps = bank(RESULT[kind, j] + o)
                        for a in range(2):
                            cols = slice(a * 256 + o * P, a * 256 + (o + 1) * P)
                            ins = product(ps[:, :], (hi[:, cols], lo[:, cols]), (d_hi[:, a, :], d_lo[:, a, :]),
                                          a == 0, a == 1)
                    ins.then_inc(unit_used, 1)
                if kind == "wo":
                    ktp = j % 8
                    if ktp < 4:
                        pe.wait_ge(mixp_made, 2 * ktp + 2)
                    else:
                        pe.wait_ge(mixh_made, 2 * ktp - 6)
                    token_unit(k, kind, j, lambda kt: (mixp_hi[:, kt, :], mixp_lo[:, kt, :]) if kt < KT else
                               (mixh_hi[:, kt - KT, :], mixh_lo[:, kt - KT, :]), S)
                if (kind, j) in LEVEL_AT:
                    level_scores(LEVEL_AT[kind, j])
                n = HEAD_AT.get((kind, j))
                if n is not None:
                    if n < HEADS:
                        transpose_keys(n)
                    if n:
                        head_output(n - 1)
                    if n < HEADS:
                        outer_products(n)
                    if n:
                        head_mean_squares(n - 1)
                if (kind, j) == ("wo", 8):
                    pe.wait_ge(ada_summed, 24)
                    for o in range(2):
                        nc.tensor.matmul(side[1 + o][:, :], ones[:, :], gate_post[:, o * S:(o + 1) * S],
                                         start=True, stop=True).then_inc(gate_summed, 1)
                if (kind, j) == ("bq", 0):
                    pe.wait_ge(lat_made, TT)
                    for t in range(TT):
                        for n, src in enumerate((lat[:, t, :], side_tok[:, t, P:2 * P], side_tok[:, t, 2 * P:3 * P],
                                                 key_twice[:, t, :])):
                            ins = nc.tensor.transpose(side[n][:, t * P:(t + 1) * P], src, ident[:, :])
                    ins.then_inc(idxT_made, 1)
                if kind == "bq" and j:
                    pe.wait_ge(idxT_copied, 4)
                    w = (j + 1) * P
                    for h in range(4):
                        if j > 1:
                            pe.wait_ge(relu_made, 4 * (j - 2) + h + 1)
                        rows = slice((h % 2) * 64, (h % 2 + 1) * 64)
                        nc.tensor.matmul(side[h][:, 0:w], idx_qT[rows, h // 2, j * P:(j + 1) * P], idx_kT[rows, 0:w],
                                         start=True, stop=True).then_inc(dots_made, 1)
                if (kind, j) == ("av", 0):
                    wait_freed(pe, RESULT["bq", 3])
                    pe.wait_ge(up_here, 32)
                    pe.wait_ge(relu_made, 12)
                    for h in range(4):
                        ins = nc.tensor.matmul(side[h][:, :], w_up[:, 0, h, :], lat_q[:, h, :], start=True, stop=True)
                    ins.then_inc(latq_made, 1)
                slot = k - SLOT0
                side_slot(slot)
                if slot == FORGET_AT:
                    pe.wait_ge(exp_made, SPARSE)
                    for t in range(TT):
                        ins = nc.tensor.transpose(side[0][0:4, t * P:(t + 1) * P], side_tok[:, t, 452:456], ident[:, :])
                    ins.then_inc(fgt_made, 1)
                if slot == CUM_AT:
                    pe.wait_ge(fgt_sum, 1)
                    for t in range(TT):
                        ins = nc.tensor.transpose(side[1][:, 4 * t:4 * t + 4], forget[:, 0, t * P:(t + 1) * P],
                                                  ident[0:4, 0:4])
                    ins.then_inc(cum_made, 1)


def kernel(**inputs):
    import numpy as _np
    import concourse.bacc as _bacc
    from concourse import mybir as _mybir
    from concourse.bass_utils import run_bass_kernel_spmd as _run

    def panels(w):
        k, n = w.shape
        return w.reshape(k // 128, 128, n // 128, 128).transpose(2, 1, 0, 3).reshape(n // 128, 128, k)

    def strips(w, n):
        k, total = w.shape
        return w.reshape(k // 256, 2, 128, total // n, n).transpose(3, 0, 2, 1, 4).reshape(-1, 128, 2 * n)

    def columns(v):
        return v.reshape(-1, 128).T

    a = {k: _np.asarray(v) for k, v in inputs.items()}
    w = a["w_in"][0]
    sec = {name: w[:, i * 1024:(i + 1) * 1024] for i, name in enumerate(("u", "gp", "q", "f", "i", "gh"))}
    arrays = {
        "x": a["x"][0],
        "ada_w": a["ada_w"][0],
        "par": _np.concatenate([
            columns(a["c"]), columns(a["ada_b"][0, :2048]), columns(a["norm_pre_w"]), columns(a["pool_scale"]),
            columns(a["hgrn_lower_bounds"]), columns(a["hgrn_norm_w"]), columns(a["norm_g_2"]),
            columns(a["conv_w_2"][0])], axis=1),
        "gate_b": a["ada_b"][0, 2048:],
        "post_w": a["norm_post_w"][0],
        "pw": a["pool_w"][0].reshape(4, 2, 128, 256).transpose(0, 2, 1, 3).reshape(4, 128, 512),
        "i": strips(sec["i"], 512),
        "wo": strips(a["w_out"][0], 512),
    }
    for name in ("f", "q", "u", "gp", "gh"):
        arrays[name] = panels(sec[name])
    w = a["w_in_2"][0]
    starts = _np.cumsum([0, 512, 512, 512, 512, 128 + 256 + 64 + 4, 512, 512, 512, 512, 512, 512, 512, 512, 4, 512, 4096])
    names = ("au", "av", "az", "bq", "side", "bz", "cb", "cc", "cx", "cz", "dq", "dk", "dv", "df", "dz", "ga")
    sec = {name: w[:, starts[i]:starts[i + 1]] for i, name in enumerate(names)}
    for name in ("au", "az", "bq", "bz", "cb", "cc", "cx", "cz", "dq", "dk", "dz"):
        arrays[name] = panels(sec[name])
    for name in ("av", "dv"):
        arrays[name] = strips(sec[name], 512)
    arrays["bs"] = strips(_np.concatenate([sec["side"], sec["df"]], axis=1), 456)
    arrays["ga"] = panels(sec["ga"]).reshape(4, 8, 128, 1024).transpose(1, 0, 2, 3).reshape(32, 128, 1024)
    arrays["br"] = a["w_branch_2"][0].reshape(2, 2, 4, 128, 8, 128).transpose(4, 0, 3, 1, 2, 5).reshape(16, 128, 1024)
    arrays["w2"] = strips(a["w_out_2"][0], 512)
    arrays["kv_g"] = a["dsa_kv_g_2"][0]
    arrays["b_f"] = a["fox_b_f_2"].reshape(4, 1)
    arrays["w_uk"] = a["dsa_w_uk_2"][0].transpose(2, 0, 1)
    arrays["w_uv"] = a["dsa_w_uv_2"][0].transpose(1, 0, 2)
    arrays["w_s"] = a["gm_w_s_2"][0].transpose(2, 0, 1)
    arrays["b_s"] = a["gm_b_s_2"][0].reshape(-1)
    arrays["ln_g"], arrays["ln_b"] = a["gm_ln_g_2"][0], a["gm_ln_b_2"][0]
    arrays["final_g"] = a["final_g_2"]
    nc = _bacc.Bacc("TRN2", target_bir_lowering=False, num_devices=1)
    feeds, dram = {}, {}
    for name, v in arrays.items():
        v = _np.ascontiguousarray(v)
        feeds[f"in_{name}"] = v
        dram[name] = nc.dram_tensor(f"in_{name}", v.shape, _mybir.dt.from_np(v.dtype), kind="ExternalInput").ap()
    out = nc.dram_tensor("out", (512, 1024), _mybir.dt.float32, kind="ExternalOutput").ap()
    program(nc, dram, out)
    r = _run(nc, [feeds], core_ids=[0])
    return r.results[0]["out"].reshape(1, 512, 1024)
```

```python
import numpy as np
import concourse.bass as bass
from concourse import mybir
from contextlib import ExitStack

P = 128
S = 512
TT = S // P
D = 1024
KT = D // P
W = 512
HEADS = 8
C = 64
NC = S // C
EPS = 1e-6
U = 1024
RING = 4
SPLITS = 4
AHEAD = SPLITS - 1
NEG = -1.0e30
OUTSIDE = -3.0e38
TAKEN = -3.3e38
SIDE = 128 + 256 + 64 + 4 + 4

ORDER = [("ada", j) for j in range(16)]
ORDER += [("f", j) for j in range(8)] + [("q", j) for j in range(8)]
for g in range(4):
    ORDER += [("u", 2 * g), ("u", 2 * g + 1), ("gp", 2 * g), ("gp", 2 * g + 1),
              ("gate_ada", 2 * g), ("gate_ada", 2 * g + 1), ("pw", g)]
ORDER += [("i", j) for j in range(8)] + [("gh", j) for j in range(8)]
ORDER += [("wo", j) for j in range(16)]
for kind in ("bs", "bq", "av", "au", "az"):
    ORDER += [(kind, j) for j in range(4)]
for j in range(4):
    ORDER += [("cc", j), ("cx", j), ("cb", j), ("cz", j)]
for kind in ("dq", "dk", "dv", "bz", "dz"):
    ORDER += [(kind, j) for j in range(4)]
for j in range(KT):
    ORDER += [("ga", 4 * j), ("ga", 4 * j + 1), ("br", 2 * j), ("ga", 4 * j + 2), ("ga", 4 * j + 3), ("br", 2 * j + 1)]
ORDER += [("w2", j) for j in range(8)]
ADA = ("ada", "gate_ada")
UNIT = {u: n for n, u in enumerate(ORDER)}
USED = [u for u in ORDER if u[0] not in ADA]
STEP = {u: k for k, u in enumerate(USED)}
WIDTH = {"pw": 512, "bs": 2 * SIDE}
TOKEN_UNITS = {"i": 4, "wo": 8, "bs": 4, "av": 4, "dv": 4, "w2": 4}
GATES = ("gp", "gh", "az", "bz", "cz", "dz")
PANELS = ("f", "q", "u", "gp", "gh", "bq", "au", "az", "bz", "cc", "cx", "cb", "cz", "dq", "dk", "dz", "ga")
PAIRS = ("pw", "br")
BY_DVE = ("gp", "gh", "pw", "av", "az", "bz", "cz", "dz", "cx", "cb", "br", "w2")

GATE_ORDER = [u for u in USED if u[0] in GATES]

RESULT = {}
FREED = []
_freed = {"act": 0, "dve": 0}
for _kind, _j in USED:
    _per = TOKEN_UNITS.get(_kind, 1)
    if _j % _per:
        continue
    RESULT[_kind, _j // _per] = len(FREED)
    for _ in range(TT if _kind in TOKEN_UNITS else 2 if _kind in PAIRS else 1):
        _by = "dve" if _kind in BY_DVE or (_kind, _j) == ("wo", 8) else "act"
        _freed[_by] += 1
        FREED.append((_by, _freed[_by]))

LEVELS = [32, 16, 8, 4, 2, 1, 0]
NL = len(LEVELS)
LEVEL_AT = {u: m for m, u in enumerate([u for u in USED if u[0] in ("u", "gp", "pw", "i")])}
assert len(LEVEL_AT) == 4 * NL
HEAD_AT = {u: n for n, u in enumerate([("gh", j) for j in range(8)] + [("wo", 0)])}


SLOT0 = STEP["av", 0]
SPARSE = TT * 4
SCORES_AT = {t: [] for t in range(-8, 200)}
for _s in range(2 * SPARSE):
    SCORES_AT[1 + _s + _s // 4 if _s < SPARSE else 38 + (_s - SPARSE) // 2].append(_s)
SLOT_OF = {_s: _t for _t, _l in SCORES_AT.items() for _s in _l}
TURN_AT = {t: SCORES_AT.get(t - 1, []) for t in range(-7, 200)}
SUM_AT = {t: SCORES_AT.get(t - 2, []) for t in range(-6, 200)}
UP_AT = {SLOT_OF[4 * q + 3] + 3: q for q in range(TT)}
BANK2 = []
for _t in range(0, 60):
    BANK2 += [("turn", _s) for _s in TURN_AT[_t]] + ([("up", UP_AT[_t])] if _t in UP_AT else [])
ROUNDS = 128 // 8
TOPK_STEP = 3
MIXED_AT = {7 + g: g for g in range(4)}
FORGET_AT, CUM_AT = 21, 24


FINAL = [("a", j) for j in range(4)] + [("c", j) for j in range(4)] + [("b", j) for j in range(4)] + \
    [("d", j) for j in range(4)]
D_FINAL_AT = SLOT0 + max(t for t, l in SUM_AT.items() if l) + 1


TOGETHER = {("wo", 15): 2, ("bs", 2): 3, ("w2", 7): 2}
EARLIER = {(kind, j - i) for (kind, j), n in TOGETHER.items() for i in range(1, n)}


def finals_at(k):
    return 4 if k == D_FINAL_AT else int(k > 0 and USED[k - 1][0] in ("az", "bz", "cz"))


def topk_rounds(slot):
    first = slot * TOPK_STEP
    return [(1 + i // ROUNDS, i % ROUNDS) for i in range(max(first, 0), first + TOPK_STEP) if i < 3 * ROUNDS]


DIFF_BY_DVE = (0, 3, 8, 18, 19)


def pair_levels(m):
    return m + 1 - (m + 1) // NL


PAR = {}
_at = 0
for _name, _n in (("c", 8), ("ada_b", 16), ("pre_w", 8), ("pool_scale", 8), ("lb", 8), ("nw", 1),
                  ("conv_w", 12)):
    PAR[_name] = slice(_at, _at + _n)
    _at += _n
NPAR = _at


def program(nc, dram, out):
    f32, f32r, bf16, i32 = mybir.dt.float32, mybir.dt.float32r, mybir.dt.bfloat16, mybir.dt.int32
    ALU, ACT, AX = mybir.AluOpType, mybir.ActivationFunctionType, mybir.AxisListType
    with ExitStack() as ctx:
        top = [16512]

        def at(name, offset, shape, dt=f32):
            return nc.alloc_sbuf_tensor_at(name, shape, dt, offset=offset)

        def take(nbytes):
            top[0] += nbytes
            return top[0] - nbytes

        def fixed(name, shape, dt=f32):
            nbytes = int(np.prod(shape[1:])) * (2 if dt == bf16 else 4)
            return at(name, take(-(-nbytes // 32) * 32), shape, dt)

        ident = fixed("ident", [P, P])
        ones = fixed("ones", [P, P])
        R_0 = take(4096)
        level_mask = at("level_mask", R_0, [P, NL, C], i32)
        chunk_keep = at("chunk_keep", R_0 + 1792, [P, S])
        inv_count = at("inv_count", R_0 + 3840, [P, 16])
        ident16 = fixed("ident16", [P, P], bf16)
        causal16 = fixed("causal16", [P, P], bf16)
        kv_row = fixed("kv_row", [P, P])
        pick = fixed("pick", [36, 8], f32r)
        par = fixed("par", [P, NPAR])
        small = fixed("small", [P, 384])
        R_GP = take(4096)
        gate_post = at("gate_post", R_GP, [P, D])
        raw = fixed("raw", [P, RING, U])
        w_hi = fixed("w_hi", [P, SPLITS, U], f32r)
        w_lo = fixed("w_lo", [P, SPLITS, U], f32r)
        R_HT = take(32768)
        R_B, R_K, R_Q, R_V, R_MP = (take(16384) for _ in range(5))
        R_G = take(4096)
        R_X = take(8192)
        R_ATT = take(8192)
        R_H = top[0]
        assert R_H + 13824 <= nc.sbuf_usable_end, (R_H, nc.sbuf_usable_end)

        silu_c, ss, rstd, mod, scale_a, low_b, one_low, tmp8 = (
            small[:, a:a + n] for a, n in ((0, 8), (8, 8), (16, 8), (24, 16), (40, 8), (48, 8), (56, 8), (64, 8)))
        b_end = small[:, 72:88].rearrange("p (s c) -> p s c", s=2)
        ss_y, rstd_y = small[:, 88:100], small[:, 100:104]

        _c = [104]

        def cols(n):
            _c[0] += n
            assert _c[0] <= 384
            return small[:, _c[0] - n:_c[0]]

        ss_h, rstd_h, ss_kv, rstd_kv, ss_o, rstd_o = (cols(n) for n in (4, 4, 4, 4, 8, 8))
        top_max, top_neg, row_sum, row_inv = cols(32), cols(32), cols(32), cols(32)
        bn, bn_mean, rstd_v, cum_q, idx_w, top8, bf_col, pick_f = (cols(n) for n in (24, 8, 4, 16, 16, 8, 1, 8))

        x_in = at("x_in", R_V, [P, TT, D])
        ada_acc = at("ada_acc", R_MP, [P, 2 * D])
        hT_full = at("hT_full", R_Q, [P, KT, S])
        hT_hi = at("hT_hi", R_HT, [P, KT, S], f32r)
        hT_lo = at("hT_lo", R_HT + 16384, [P, KT, S], f32r)
        junk = at("junk", R_X, [P, D])
        idx = at("idx", R_X + 4096, [P, 2, C], i32)
        later = at("later", R_X + 4608, [P, C])
        b_cum = at("b_cum", R_B, [P, HEADS, S])
        keys = at("keys", R_K, [P, HEADS, S])
        queries = at("queries", R_Q, [P, HEADS, S])
        values = at("values", R_V, [P, TT, D])
        attn = at("attn", R_ATT, [P, HEADS, S // 2])
        xq = at("xq", R_X, [P, 2, 2 * S])
        u_pad = at("u_pad", R_V, [P, 2, 16 + S])
        sums = [at("sums0", R_V + 4224, [P, 2, 16 + S]), at("sums1", R_V + 8448, [P, 2, 16 + S])]
        d_hi = at("d_hi", R_H, [P, 2, S], f32r)
        d_lo = at("d_lo", R_H + 4096, [P, 2, S], f32r)
        silu_out = at("silu_out", R_G, [P, 2, S])
        silu_e = at("silu_e", R_H + 11776, [P, S])
        mix_pool = at("mix_pool", R_MP, [P, KT, S])
        e_b = at("e_b", R_X, [P, S])
        k_dec = at("k_dec", R_X + 2048, [P, S])
        k_decT = at("k_decT", R_X + 4096, [P, TT, P])
        q_dec = at("q_dec", R_H, [P, 2, S])
        o_sb = at("o_sb", R_H + 4096, [P, S])
        o_sq = at("o_sq", R_H + 6144, [P, S])
        states = at("states", R_H + 8192, [P, NC - 1, P])
        mixh_hi = at("mixh_hi", R_B, [P, HEADS, S], f32r)
        mixh_lo = at("mixh_lo", R_K, [P, HEADS, S], f32r)
        mixp_hi = at("mixp_hi", R_Q, [P, KT, S], f32r)
        mixp_lo = at("mixp_lo", R_MP, [P, KT, S], f32r)
        y_left = at("y_left", R_ATT, [P, TT, S])
        x_again = at("x_again", R_V, [P, TT, D])
        x2 = at("x2", R_B, [P, TT, D])
        gate_row = at("gate_row", R_HT + 16384, [P, D])
        post_row = at("post_row", R_HT + 20480, [P, D])
        norm_row = at("norm_row", R_H, [P, D])
        x2_gain = at("x2_gain", R_Q, [P, TT, D])
        y_squares = at("y_squares", R_X, [P, TT, S])
        x2_squares = at("x2_squares", R_MP, [P, D])
        diag = at("diag", R_H + 4096, [P, TT, P])
        M = R_G
        side_tok = at("side_tok", M, [P, TT, SIDE])
        lat_q = at("lat_q", M + 8192, [P, 4, S])
        probs = at("probs", M + 16384, [P, 2, S])
        probsT = at("probsT", M + 20480, [P, 2, S])
        latT = at("latT", M + 24576, [P, S])
        lat = at("lat", M + 26624, [P, TT, P])
        lat_out = at("lat_out", M + 28672, [P, S])
        sel16 = at("sel16", M + 30720, [P, 3, S], bf16)
        w_up = at("w_up", R_GP, [P, 2, 4, P])
        idx_qT = at("idx_qT", R_MP, [P, 2, S])
        idx_kT = at("idx_kT", R_MP + 4096, [P, S])
        score = at("score", R_MP + 6144, [P, 3, S])
        relu = at("relu", R_MP + 12288, [P, 2, S])
        key_twice = at("key_twice", R_MP + 14336, [P, TT, P])
        v_norm = at("v_norm", R_V, [P, TT, S])
        ln_rows = at("ln_rows", R_V + 8192, [P, 2, S])
        mixT = at("mixT", R_V + 12288, [P, 4, P])
        mix_b = at("mix_b", R_V + 14336, [P, 4, P])
        c_gate = at("c_gate", R_MP, [P, S])
        conv_in = at("conv_in", R_MP + 2048, [P, 2 + S])
        conv = at("conv", R_MP + 12288, [P, S])
        fox_q, fox_k = at("fox_q", M, [P, 4, S]), at("fox_k", M + 8192, [P, 4, S])
        fox_v = at("fox_v", R_MP + 8192, [P, TT, S])
        forget = at("forget", M + 24576, [4, 2, S])
        forget_r = at("forget_r", M + 32768, [36, S], f32r)
        z_d = at("z_d", M + 24576, [P, 4, S])
        silu_e2 = at("silu_e2", R_0, [P, S])
        y_tmp = at("y_tmp", R_0 + 2048, [P, S])
        y_tmp2 = at("mixed", R_MP + 14336, [P, S])[:, :]
        y_hi = {n: at(f"y{n}_hi", r, [P, 4, S], f32r) for n, r in zip("abcd", (R_K, R_Q, R_V, R_MP))}
        y_lo = {n: at(f"y{n}_lo", r + 8192, [P, 4, S], f32r) for n, r in zip("abcd", (R_K, R_Q, R_V, R_MP))}
        y_raw = {n: at(f"y{n}_raw", r, [P, 4, S]) for n, r in zip("abcd", (R_K, R_Q, R_V, R_MP))}
        sig = at("sig", R_GP, [P, 2, S])
        merged = at("merged", R_0, [P, S])
        merged_part = at("merged_part", R_0 + 2048, [P, S])
        m_hi, m_lo = at("m_hi", M, [P, KT, S], f32r), at("m_lo", M + 16384, [P, KT, S], f32r)
        h_squares = at("h_squares", R_Q, [P, TT, S])
        final_row = at("final_row", R_K, [P, D])
        assert M + 34816 <= nc.sbuf_usable_end, (M, nc.sbuf_usable_end)

        acc = [ctx.enter_context(nc.psum_tensor(f"acc{n}", [P, S], f32)) for n in range(4)]
        side = [ctx.enter_context(nc.psum_tensor(f"side{n}", [P, S], f32)) for n in range(4)]

        def sem(name):
            return ctx.enter_context(nc.semaphore(name))

        raw_in = [sem(f"raw_in{n}") for n in range(RING)]
        x_here, par_here, rows_here, x_again_here = sem("x_here"), sem("par_here"), sem("rows_here"), sem("x_again_here")
        norm_here = sem("norm_here")
        stored = sem("stored")
        hi_made, lo_made = sem("hi_made"), sem("lo_made")
        ada_summed = sem("ada_summed")
        unit_used = sem("unit_used")
        freed = {"act": sem("freed_act"), "dve": sem("freed_dve")}
        act_chain, dve_chain, pool_chain = sem("act_chain"), sem("dve_chain"), sem("pool_chain")
        consts = sem("consts")
        c_exp, lb_exp, lb_diff = sem("c_exp"), sem("lb_exp"), sem("lb_diff")
        x_normed, xT_made, xT_copied = sem("x_normed"), sem("xT_made"), sem("xT_copied")
        mod_summed, h_full, h_hi, h_lo = sem("mod_summed"), sem("h_full"), sem("h_hi"), sem("h_lo")
        f_made, log_made, b_made = sem("f_made"), sem("log_made"), sem("b_made")
        sum_made, d_made, d_hi_made, d_lo_made = sem("sum_made"), sem("d_made"), sem("d_hi_made"), sem("d_lo_made")
        silu_exp, silu_bound, silu_sig = sem("silu_exp"), sem("silu_bound"), sem("silu_sig")
        f_bound, f_sig = sem("f_bound"), sem("f_sig")
        level_diff, level_exp, level_x = sem("level_diff"), sem("level_exp"), sem("level_x")
        scores_made, level_copied = sem("scores_made"), sem("level_copied")
        decay_diff, decay_exp, prep_made = sem("decay_diff"), sem("decay_exp"), sem("prep_made")
        kT_made, kT_copied, outer_made, states_made = sem("kT_made"), sem("kT_copied"), sem("outer_made"), sem("states_made")
        even_made = sem("even_made")
        o_made, o_squared, ms_made, o_rstd = sem("o_made"), sem("o_squared"), sem("ms_made"), sem("o_rstd")
        o_final, mixh_hi_made, mixh_made = sem("o_final"), sem("mixh_hi_made"), sem("mixh_made")
        mixp_hi_made, mixp_made = sem("mixp_hi_made"), sem("mixp_made")
        gate_summed, gate_made = sem("gate_summed"), sem("gate_made")
        y_squared, y_bias_made, y_rstd, x2_made = sem("y_squared"), sem("y_bias_made"), sem("y_rstd"), sem("x2_made")
        y_tiles_made, out_tiles_made = sem("y_tiles_made"), sem("out_tiles_made")

        x2_rstd, gain_made, diag_made, x2T_made, h2_hi_made, h2_made = (
            sem(n) for n in ("x2_rstd", "gain_made", "diag_made", "x2T_made", "h2_hi_made", "h2_made"))
        small_rows, up_here, spatial_here, masked = sem("small_rows"), sem("up_here"), sem("spatial_here"), sem("masked")
        lat_rstd, lat_made, idxT_made, idxT_copied = sem("lat_rstd"), sem("lat_made"), sem("idxT_made"), sem("idxT_copied")
        dots_made, relu_made, cut_made = sem("dots_made"), sem("relu_made"), sem("cut_made")
        relu_used, sel_made = sem("relu_used"), sem("sel_made")
        latq_made, latq_copied = sem("latq_made"), sem("latq_copied")
        logits_made, max_made, exp_made, probs_made = sem("logits_made"), sem("max_made"), sem("exp_made"), sem("probs_made")
        turned, bank2_read, summed, bank3_read = (
            sem(n) for n in ("turned", "bank2_read", "summed", "bank3_read"))
        bn_made, bn_rstd, v_made, mixed_made, mixed_read = (
            sem(n) for n in ("bn_made", "bn_rstd", "v_made", "mixed_made", "mixed_read"))
        conv_freed = sem("conv_freed")
        y_final, y_hi_made, y_made = sem("y_final"), sem("y_hi_made"), sem("y_made")
        fgt_made, fgt_abs, fgt_ln, fgt_sum, fgt_hi, fgt_ready = (
            sem(n) for n in ("fgt_made", "fgt_abs", "fgt_ln", "fgt_sum", "fgt_hi", "fgt_ready"))
        cum_made, cum_read, pick_made = sem("cum_made"), sem("cum_read"), sem("pick_made")
        sig_made, m_sum, m_hi_made, m_made = sem("sig_made"), sem("m_sum"), sem("m_hi_made"), sem("m_made")
        h_sq, h_rstd, left_scaled, left_made, out_made, final_here = (
            sem(n) for n in ("h_sq", "h_rstd", "left_scaled", "left_made", "out_made", "final_here"))

        def wait_freed(eng, result):
            by, n = FREED[result]
            eng.wait_ge(freed[by], n)

        def wait_y(eng, t):
            if t < TT - 1:
                eng.wait_ge(y_tiles_made, t + 1)
            else:
                eng.wait_ge(unit_used, STEP["wo", 15] + 1)

        def gate_e(n):
            return silu_e[:, :] if n < 16 else silu_e2[:, :]

        def level_view(tile, half):
            return tile.rearrange("p (n w) -> p n w", w=2 * half)

        def diff_level(eng, ops, m):
            half = LEVELS[m % NL] if m < 4 * NL else 0
            if not half or (m in DIFF_BY_DVE) != (ops is nc.vector):
                return
            g = m // NL
            if m >= 2:
                eng.wait_ge(scores_made, m - 1)
            if m and ((m - 1) in DIFF_BY_DVE or m in DIFF_BY_DVE):
                eng.wait_ge(level_diff, pair_levels(m - 1))
            x = level_view(xq[:, m % 2, :], half)
            b = level_view(b_cum[:, 2 * g:2 * g + 2, :].rearrange("p h s -> p (h s)"), half)
            middle = b[:, :, half - 1:half].broadcast_to([P, S // half, half])
            ops.tensor_tensor(out=x[:, :, half:], in0=b[:, :, half:], in1=middle, op=ALU.subtract)
            ops.tensor_tensor(out=x[:, :, :half], in0=middle, in1=b[:, :, :half], op=ALU.subtract)\
                .then_inc(level_diff, 1)

        block = ctx.enter_context(nc.Block())

        @block.sync
        def _(sp):
            sp.dma_start(x_in[:, :, :], dram["x"].rearrange("(t p) d -> p t d", p=P)).then_inc(x_here, 16)
            for n, (kind, j) in enumerate(ORDER):
                if n >= RING:
                    last = ORDER[n - RING]
                    if last[0] in ADA:
                        sp.wait_ge(ada_summed, last[1] + 1 + 16 * (last[0] == "gate_ada"))
                    else:
                        sp.wait_ge(lo_made, STEP[last] + 1)
                if kind == "ada":
                    src = dram["ada_w"][(j // 2) * P:(j // 2 + 1) * P, (j % 2) * D:(j % 2 + 1) * D]
                elif kind == "gate_ada":
                    src = dram["ada_w"][j * P:(j + 1) * P, 2 * D:3 * D]
                else:
                    src = dram[kind][j, :, :]
                width = WIDTH.get(kind, U)
                sp.dma_start(raw[:, n % RING, 0:width], src).then_inc(raw_in[n % RING], 16)
            out_tiles = out.rearrange("(t p) d -> p t d", p=P)
            for t in range(TT):
                sp.wait_ge(left_made, t + 1)
                sp.wait_ge(out_made, t + 1)
                sp.dma_start(out_tiles[:, t, :], x2[:, t, :]).then_inc(stored, 16)
            sp.wait_ge(stored, 16 * TT)

        @block.gpsimd
        def _(pool):
            done = [0]

            def then(ins):
                done[0] += 1
                ins.then_inc(pool_chain, 1)
                pool.wait_ge(pool_chain, done[0])

            then(nc.gpsimd.memset(ident[:, :], 0.0))
            nc.gpsimd.affine_select(out=ident[:, :], in_=ident[:, :], compare_op=ALU.not_equal, fill=1.0, base=0,
                                    pattern=[[-1, P]], channel_multiplier=1).then_inc(consts, 1)
            nc.gpsimd.memset(ones[:, :], 1.0).then_inc(consts, 1)
            nc.gpsimd.iota(idx[:, 0, :], pattern=[[1, C]], base=0, channel_multiplier=0).then_inc(consts, 1)
            nc.gpsimd.iota(idx[:, 1, :], pattern=[[0, C]], base=0, channel_multiplier=1).then_inc(consts, 1)
            then(nc.gpsimd.memset(chunk_keep[:, :], 1.0))
            nc.gpsimd.memset(chunk_keep[:, :].rearrange("p (c t) -> p c t", t=C)[:, :, 0:1], 0.0).then_inc(consts, 1)
            nc.gpsimd.memset(attn[:, :, :], 0.0).then_inc(consts, 1)
            then(nc.gpsimd.memset(causal16[:, :], 0.0))
            nc.gpsimd.affine_select(out=causal16[:, :], in_=causal16[:, :], compare_op=ALU.is_ge, fill=NEG, base=0,
                                    pattern=[[-1, P]], channel_multiplier=1).then_inc(consts, 1)
            then(nc.gpsimd.memset(pick_f[0:36, :], 0.0))
            for base in (0, -32):
                then(nc.gpsimd.affine_select(out=pick_f[0:36, 0:4], in_=pick_f[0:36, 0:4], compare_op=ALU.not_equal,
                                             fill=1.0, base=base, pattern=[[-1, 4]], channel_multiplier=1))
            nc.gpsimd.memset(pick_f[0:36, 4:8], 0.0).then_inc(consts, 1)
            pool.dma_start(kv_row[:, :], dram["kv_g"].partition_broadcast(P)).then_inc(small_rows, 16)
            pool.dma_start(bf_col[0:4, :], dram["b_f"]).then_inc(small_rows, 16)
            pool.wait_ge(h_lo, KT)
            then(nc.gpsimd.memset(u_pad[:, :, 0:16], 0.0))
            pool.wait_ge(b_made, HEADS)
            for m in range(4 * NL):
                diff_level(pool, nc.gpsimd, m)
                if (m - 2) % 5 or m > 17:
                    continue
                g = m // 5
                wait_freed(pool, RESULT["u", 2 * g + 1])
                if g:
                    pool.wait_ge(d_lo_made, g)
                src, reach = u_pad, 0
                for r in range(g + 1):
                    dst, shift = sums[r % 2], 1 << r
                    reach += shift
                    ins = nc.gpsimd.tensor_tensor(out=dst[:, :, reach:], in0=src[:, :, reach:],
                                                  in1=src[:, :, reach - shift:16 + S - shift], op=ALU.add)
                    if r < g:
                        then(ins)
                    else:
                        ins.then_inc(sum_made, 1)
                    src = dst
            pool.wait_ge(unit_used, STEP["gh", 7] + 1)
            pool.dma_start(gate_row[:, :], dram["gate_b"].partition_broadcast(P)).then_inc(rows_here, 16)
            pool.dma_start(post_row[:, :], dram["post_w"].partition_broadcast(P)).then_inc(rows_here, 16)
            pool.wait_ge(o_made, HEADS)
            pool.dma_start(norm_row[:, :], dram["norm_g"].partition_broadcast(P)).then_inc(norm_here, 16)
            pool.dma_start(x_again[:, :, :], dram["x"].rearrange("(t p) d -> p t d", p=P)).then_inc(x_again_here, 16)
            pool.wait_ge(x2_made, TT)
            for o, name in enumerate(("w_uk", "w_uv")):
                pool.dma_start(w_up[:, o, :, :], dram[name]).then_inc(up_here, 16)
            pool.dma_start(ln_rows[:, 0, :], dram["ln_g"].partition_broadcast(P)).then_inc(spatial_here, 16)
            pool.dma_start(ln_rows[:, 1, :], dram["ln_b"].partition_broadcast(P)).then_inc(spatial_here, 16)
            pool.dma_start(mix_b[:, :, :].rearrange("p g t -> p (g t)"), dram["b_s"].partition_broadcast(P))\
                .then_inc(spatial_here, 16)
            pool.dma_start(mixT[:, :, :], dram["w_s"]).then_inc(spatial_here, 16)
            pool.wait_ge(spatial_here, 64)
            nc.gpsimd.affine_select(out=mixT[:, :, :], in_=mixT[:, :, :], compare_op=ALU.is_ge, fill=0.0, base=0,
                                    pattern=[[0, 4], [1, P]], channel_multiplier=-1).then_inc(masked, 1)
            for t in range(1, TT):
                pool.wait_ge(relu_used, 4 * t)
                diagonal = score[:, t - 1, t * P:(t + 1) * P]
                nc.gpsimd.affine_select(out=diagonal, in_=diagonal, compare_op=ALU.is_ge, fill=OUTSIDE, base=0,
                                        pattern=[[-1, P]], channel_multiplier=1).then_inc(cut_made, 1)
            pool.wait_ge(unit_used, STEP["br", 2 * KT - 1] + 1)
            pool.dma_start(final_row[:, :], dram["final_g"].partition_broadcast(P)).then_inc(final_here, 16)

        @block.scalar
        def _(act):
            done = [0]

            def then(ins):
                done[0] += 1
                ins.then_inc(act_chain, 1)
                act.wait_ge(act_chain, done[0])

            def split_hi(k):
                kind, j = USED[k]
                n, width = UNIT[kind, j], WIDTH.get(kind, U)
                act.wait_ge(raw_in[n % RING], 16 * (n // RING + 1))
                if k >= SPLITS:
                    act.wait_ge(unit_used, k - SPLITS + 1)
                nc.scalar.activation(w_hi[:, k % SPLITS, 0:width], raw[:, n % RING, 0:width], ACT.Copy)\
                    .then_inc(hi_made, 1)

            def exp_level(m):
                if m < 4 * NL and LEVELS[m % NL]:
                    act.wait_ge(level_diff, pair_levels(m))
                    nc.scalar.activation(xq[:, m % 2, :], xq[:, m % 2, :], ACT.Exp).then_inc(level_exp, 1)

            def exp_decays(n):
                act.wait_ge(decay_diff, n + 1)
                nc.scalar.activation(e_b[:, :], b_cum[:, n, :], ACT.Exp).then_inc(decay_exp, 1)
                nc.scalar.activation(k_dec[:, :], k_dec[:, :], ACT.Exp).then_inc(decay_exp, 1)

            act.preload_act_table_set("natural_log_exp_and_others")
            act.dma_start(par[:, :], dram["par"]).then_inc(par_here, 16)
            act.wait_ge(par_here, 16)
            nc.scalar.activation(tmp8, par[:, PAR["c"]], ACT.Exp, scale=-1.0).then_inc(c_exp, 1)
            act.wait_ge(lb_diff, 1)
            nc.scalar.activation(one_low, low_b, ACT.Exp).then_inc(lb_exp, 1)
            act.wait_ge(x_here, 16)
            for t in range(TT):
                then(nc.scalar.activation(junk[:, :], x_in[:, t, :], ACT.Square, accum_out=ss[:, t:t + 1]))
                then(nc.scalar.activation(rstd[:, t:t + 1], ss[:, t:t + 1], ACT.Ln, scale=1.0 / D, bias=EPS))
                then(nc.scalar.activation(rstd[:, t:t + 1], rstd[:, t:t + 1], ACT.Exp, scale=-0.5))
                nc.scalar.activation(x_in[:, t, :], x_in[:, t, :], ACT.Copy, scale=rstd[:, t:t + 1]).then_inc(x_normed, 1)
            for kt in range(KT):
                act.wait_ge(xT_made, kt + 1)
                nc.scalar.activation(hT_full[:, kt, :], (acc + side)[kt][:, :], ACT.Copy).then_inc(xT_copied, 1)
            split_hi(0)
            for kt in range(KT):
                act.wait_ge(h_full, kt + 1)
                nc.scalar.activation(hT_hi[:, kt, :], hT_full[:, kt, :], ACT.Copy).then_inc(h_hi, 1)
            for k in range(1, AHEAD):
                split_hi(k)

            def copy_out(dst, result, by, **more):
                nc.scalar.activation(dst, acc[result % 4][:, :], ACT.Copy, **more).then_inc(by, 1)

            def enter_second_block():
                def square_y(t):
                    wait_y(act, t)
                    nc.scalar.activation(y_squares[:, t, :], acc[(RESULT["wo", 1] + t) % 4][:, :], ACT.Square,
                                         accum_out=ss_y[:, 4 + t:5 + t]).then_inc(y_squared, 1)

                def rstd_of_y(t):
                    act.wait_ge(y_squared, t + 1)
                    then(nc.scalar.activation(rstd_y[:, t:t + 1], ss_y[:, 4 + t:5 + t], ACT.Ln, scale=1.0 / D,
                                              bias=ss_y[:, 8 + t:9 + t]))
                    nc.scalar.activation(rstd_y[:, t:t + 1], rstd_y[:, t:t + 1], ACT.Exp, scale=-0.5).then_inc(y_rstd, 1)

                def rstd_of_x2(t):
                    act.wait_ge(x2_made, t + 1)
                    then(nc.scalar.activation(x2_squares[:, :], x2[:, t, :], ACT.Square, accum_out=ss_h[:, t:t + 1]))
                    then(nc.scalar.activation(rstd_h[:, t:t + 1], ss_h[:, t:t + 1], ACT.Ln, scale=1.0 / D, bias=EPS))
                    nc.scalar.activation(rstd_h[:, t:t + 1], rstd_h[:, t:t + 1], ACT.Exp, scale=-0.5).then_inc(x2_rstd, 1)

                def upper_h2(t):
                    for n in (2 * t, 2 * t + 1):
                        act.wait_ge(x2T_made, n + 1)
                        half = n % 2
                        nc.scalar.activation(hT_hi[:, 4 * half:4 * half + 4, t * P:(t + 1) * P],
                                             side[n % 4][:, :].rearrange("p (k s) -> p k s", s=P), ACT.Copy)\
                            .then_inc(h2_hi_made, 1)

                act.wait_ge(y_bias_made, 1)
                wait_freed(act, RESULT["wo", 0] + TT - 1)
                square_y(0)
                rstd_of_y(0)
                square_y(1)
                rstd_of_y(1)
                rstd_of_x2(0)
                square_y(2)
                rstd_of_y(2)
                rstd_of_x2(1)
                square_y(3)
                upper_h2(0)
                rstd_of_y(3)
                split_hi(STEP["bs", 2])
                rstd_of_x2(2)
                upper_h2(1)
                rstd_of_x2(3)
                upper_h2(2)
                upper_h2(3)

            def side_slot(slot):
                for s in TURN_AT.get(slot, []):
                    n, w = BANK2.index(("turn", s)), (s // 4 % TT + 1) * P
                    act.wait_ge(turned, n + 1)
                    if s >= 2:
                        act.wait_ge(summed, s - 1)
                    nc.scalar.activation(probsT[:, s % 2, 0:w], side[2][:, 0:w], ACT.Copy).then_inc(bank2_read, 1)
                for s in SUM_AT.get(slot, []):
                    if s % 4 == 3:
                        q = s // 4
                        act.wait_ge(summed, s + 1)
                        if s < SPARSE:
                            if q:
                                act.wait_ge(turned, BANK2.index(("up", q - 1)) + 1)
                            nc.scalar.activation(lat_out[:, :], side[3][:, :], ACT.Copy).then_inc(bank3_read, 1)
                        else:
                            tok = slice((q % TT) * P, (q % TT + 1) * P)
                            nc.scalar.activation(y_raw["d"][:, :, tok], side[3][:, :].rearrange("p (h s) -> p h s", s=P),
                                                 ACT.Copy).then_inc(bank3_read, 1)
                if slot in UP_AT:
                    q = UP_AT[slot]
                    n = BANK2.index(("up", q))
                    act.wait_ge(turned, n + 1)
                    nc.scalar.activation(y_raw["b"][:, :, q * P:(q + 1) * P],
                                         side[2][:, :].rearrange("p (h s) -> p h s", s=P), ACT.Copy).then_inc(bank2_read, 1)
                for s in SCORES_AT.get(slot, []):
                    w = (s // 4 % TT + 1) * P
                    act.wait_ge(max_made, s + 1)
                    if s >= 2:
                        act.wait_ge(turned, BANK2.index(("turn", s - 2)) + 1)
                    nc.scalar.activation(probs[:, s % 2, 0:w], side[s % 2][:, 0:w], ACT.Exp, bias=top_neg[:, s:s + 1],
                                         accum_out=row_sum[:, s:s + 1]).then_inc(exp_made, 1)

            gates = 0
            finals = [0]
            before = None
            for k, (kind, j) in enumerate(USED):
                if k + AHEAD < len(USED) and (kind, j) != ("wo", 15):
                    split_hi(k + AHEAD)
                if before in GATES:
                    act.wait_ge(silu_bound, gates)
                    then(nc.scalar.activation(gate_e(gates - 1), gate_e(gates - 1), ACT.Ln))
                    nc.scalar.activation(gate_e(gates - 1), gate_e(gates - 1), ACT.Exp, scale=-1.0).then_inc(silu_sig, 1)
                before = kind
                m = LEVEL_AT.get((kind, j))
                if m is not None:
                    exp_level(m + 1)
                if k - 1 in range(HEADS):
                    act.wait_ge(f_bound, k)
                    then(nc.scalar.activation(b_cum[:, k - 1, :], b_cum[:, k - 1, :], ACT.Ln))
                    nc.scalar.activation(b_cum[:, k - 1, :], b_cum[:, k - 1, :], ACT.Exp, scale=-1.0).then_inc(f_sig, 1)
                if k - 2 in range(HEADS):
                    act.wait_ge(f_made, k - 1)
                    nc.scalar.activation(b_cum[:, k - 2, :], b_cum[:, k - 2, :], ACT.Ln).then_inc(log_made, 1)
                if (kind, j) not in EARLIER and (kind, j) not in (("wo", 15), ("w2", 7)):
                    act.wait_ge(unit_used, k + 1)
                if kind == "f":
                    nc.scalar.activation(b_cum[:, j, :], acc[RESULT[kind, j] % 4][:, :], ACT.Exp, scale=-1.0)\
                        .then_inc(freed["act"], 1)
                if kind == "q":
                    nc.scalar.activation(queries[:, j, :], acc[RESULT[kind, j] % 4][:, :], ACT.Copy)\
                        .then_inc(freed["act"], 1)
                    if j == 7:
                        exp_level(0)
                if kind == "u":
                    if j >= 2:
                        act.wait_ge(d_lo_made, j // 2)
                    nc.scalar.activation(u_pad[:, j % 2, 16:], acc[RESULT[kind, j] % 4][:, :], ACT.Copy)\
                        .then_inc(freed["act"], 1)
                if kind in GATES:
                    if gates:
                        wait_freed(act, RESULT[GATE_ORDER[gates - 1]])
                    nc.scalar.activation(gate_e(gates), acc[RESULT[kind, j] % 4][:, :], ACT.Exp, scale=-1.0)\
                        .then_inc(silu_exp, 1)
                    gates += 1
                if (kind, j % 2) == ("gp", 0):
                    g = j // 2
                    act.wait_ge(d_made, g + 1)
                    if g:
                        act.wait_ge(unit_used, STEP["pw", g - 1] + 1)
                    nc.scalar.activation(d_hi[:, :, :], sums[(g + 1) % 2][:, :, 0:S], ACT.Copy).then_inc(d_hi_made, 1)
                if (kind, j % 4) == ("i", 3):
                    for t in range(TT):
                        r = RESULT["i", j // 4] + t
                        nc.scalar.activation(values[:, t, (j // 4) * S:(j // 4 + 1) * S], acc[r % 4][:, :], ACT.Copy)\
                            .then_inc(freed["act"], 1)
                if (kind, j) == ("i", 7):
                    exp_decays(0)
                n = HEAD_AT.get((kind, j))
                if n is not None and n < HEADS:
                    act.wait_ge(kT_made, n + 1)
                    nc.scalar.activation(k_decT[:, :, :], side[0][:, :].rearrange("p (t k) -> p t k", t=TT), ACT.Copy)\
                        .then_inc(kT_copied, 1)
                if n:
                    act.wait_ge(o_made, n)
                    if n >= 2:
                        act.wait_ge(mixh_made, n - 1)
                    nc.scalar.activation(o_sq[:, :], side[3][:, :], ACT.Square)
                    nc.scalar.activation(o_sb[:, :], side[3][:, :], ACT.Copy).then_inc(o_squared, 1)
                if n is not None and n + 1 < HEADS:
                    exp_decays(n + 1)
                if n:
                    act.wait_ge(ms_made, n)
                    then(nc.scalar.activation(o_sq[:, :], side[0][:, :], ACT.Ln, scale=1.0 / P, bias=EPS))
                    nc.scalar.activation(o_sq[:, :], o_sq[:, :], ACT.Exp, scale=-0.5).then_inc(o_rstd, 1)
                    act.wait_ge(o_final, n)
                    nc.scalar.activation(mixh_hi[:, n - 1, :], o_sb[:, :], ACT.Copy).then_inc(mixh_hi_made, 1)
                if kind == "gh":
                    act.wait_ge(prep_made, j + 1)
                    wait_freed(act, RESULT["pw", 3] + 1)
                    nc.scalar.activation(mixp_hi[:, j, :], mix_pool[:, j, :], ACT.Copy).then_inc(mixp_hi_made, 1)
                if (kind, j) == ("wo", 7):
                    for t in range(TT):
                        r = RESULT["wo", 0] + t
                        nc.scalar.activation(y_squares[:, t, :], acc[r % 4][:, :], ACT.Square, accum_out=ss_y[:, t:t + 1])
                        nc.scalar.activation(y_left[:, t, :], acc[r % 4][:, :], ACT.Copy).then_inc(freed["act"], 1)
                if (kind, j) == ("wo", 15):
                    enter_second_block()
                r = RESULT.get((kind, j))
                if (kind, j) == ("bs", 3):
                    for t in range(TT):
                        nc.scalar.activation(side_tok[:, t, :], acc[(RESULT["bs", 0] + t) % 4][:, 0:SIDE], ACT.Copy)\
                            .then_inc(freed["act"], 1)
                    wait_freed(act, RESULT["bs", 0] + 3)
                    for t in range(TT):
                        then(nc.scalar.activation(lat[:, t, :], side_tok[:, t, 0:P], ACT.Square,
                                                  accum_out=ss_kv[:, t:t + 1]))
                    then(nc.scalar.activation(rstd_kv, ss_kv, ACT.Ln, scale=1.0 / P, bias=EPS))
                    nc.scalar.activation(rstd_kv, rstd_kv, ACT.Exp, scale=-0.5).then_inc(lat_rstd, 1)
                if kind == "bq":
                    copy_out(lat_q[:, j, :], r, freed["act"])
                    if j == 0:
                        act.wait_ge(idxT_made, 1)
                        for n, dst in enumerate((latT[:, :], idx_qT[:, 0, :], idx_qT[:, 1, :], idx_kT[:, :])):
                            nc.scalar.activation(dst, side[n][:, :], ACT.Copy).then_inc(idxT_copied, 1)
                    else:
                        for h in range(4):
                            n = 4 * (j - 1) + h
                            act.wait_ge(dots_made, n + 1)
                            if n >= 2:
                                act.wait_ge(relu_used, n - 1)
                            w = (j + 1) * P
                            nc.scalar.activation(relu[:, n % 2, 0:w], side[h][:, 0:w], ACT.Relu, scale=0.125)\
                                .then_inc(relu_made, 1)
                if (kind, j) == ("av", 0):
                    act.wait_ge(latq_made, 1)
                    for h in range(4):
                        nc.scalar.activation(lat_q[:, h, :], side[h][:, :], ACT.Copy, scale=float(P) ** -0.5)\
                            .then_inc(latq_copied, 1)
                if (kind, j) == ("av", 3):
                    act.wait_ge(bn_made, 1)
                    then(nc.scalar.activation(rstd_v, bn_mean.rearrange("p (t m) -> p t m", m=2)[:, :, 1], ACT.Ln, bias=EPS))
                    nc.scalar.activation(rstd_v, rstd_v, ACT.Exp, scale=-0.5).then_inc(bn_rstd, 1)
                if kind == "au":
                    copy_out(y_raw["a"][:, j, :], r, freed["act"])
                if kind == "cc":
                    if j:
                        wait_freed(act, RESULT["cx", j - 1])
                    copy_out(c_gate[:, :], r, freed["act"])
                if kind == "dq":
                    copy_out(fox_q[:, j, :], r, freed["act"], scale=float(P) ** -0.5)
                if kind == "dk":
                    copy_out(fox_k[:, j, :], r, freed["act"])
                if (kind, j) == ("dv", 3):
                    for t in range(TT):
                        copy_out(fox_v[:, t, :], RESULT["dv", 0] + t, freed["act"])
                for _ in range(finals_at(k)):
                    act.wait_ge(y_final, finals[0] + 1)
                    name, kt = FINAL[finals[0]]
                    nc.scalar.activation(y_hi[name][:, kt, :], y_tmp[:, :], ACT.Copy).then_inc(y_hi_made, 1)
                    finals[0] += 1
                slot = k - SLOT0
                side_slot(slot)
                if slot == FORGET_AT:
                    act.wait_ge(fgt_abs, 1)
                    then(nc.scalar.activation(forget[:, 1, :], forget[:, 1, :], ACT.Exp, scale=-1.0))
                    nc.scalar.activation(forget[:, 1, :], forget[:, 1, :], ACT.Ln, bias=1.0).then_inc(fgt_ln, 1)
                    act.wait_ge(fgt_sum, 1)
                    nc.scalar.activation(forget_r[0:4, :], forget[:, 0, :], ACT.Copy, scale=-1.0).then_inc(fgt_hi, 1)
                if kind == "ga":
                    if j >= 2:
                        wait_freed(act, RESULT["br", (j - 2) // 2] + j % 2)
                    nc.scalar.activation(sig[:, j % 2, :], acc[r % 4][:, :], ACT.Sigmoid).then_inc(freed["act"], 1)
                if kind == "br" and j % 2:
                    act.wait_ge(m_sum, j // 2 + 1)
                    nc.scalar.activation(m_hi[:, j // 2, :], merged[:, :], ACT.Copy).then_inc(m_hi_made, 1)
                if (kind, j) == ("w2", 3):
                    for t in range(TT):
                        wait_freed(act, RESULT["w2", 0] + t)
                        nc.scalar.activation(h_squares[:, t, :], x2[:, t, 0:S], ACT.Square, accum_out=ss_o[:, t:t + 1])\
                            .then_inc(h_sq, 1)
                if (kind, j) == ("w2", 7):
                    act.wait_ge(left_scaled, 1)
                    for t in range(TT):
                        wait_freed(act, RESULT["w2", 1] + t)
                        then(nc.scalar.activation(h_squares[:, t, :], x2[:, t, S:D], ACT.Square,
                                                  accum_out=ss_o[:, 4 + t:5 + t]))
                        then(nc.scalar.activation(rstd_o[:, t:t + 1], ss_o[:, 4 + t:5 + t], ACT.Ln, scale=1.0 / D,
                                                  bias=rstd_o[:, 4 + t:5 + t]))
                        nc.scalar.activation(rstd_o[:, t:t + 1], rstd_o[:, t:t + 1], ACT.Exp, scale=-0.5)\
                            .then_inc(h_rstd, 1)
                        act.wait_ge(h_rstd, t + 1)
                        nc.scalar.activation(x2[:, t, 0:S], x2[:, t, 0:S], ACT.Copy, scale=rstd_o[:, t:t + 1])\
                            .then_inc(left_made, 1)

        @block.vector
        def _(dve):
            done = [0]

            def then(ins):
                done[0] += 1
                ins.then_inc(dve_chain, 1)
                dve.wait_ge(dve_chain, done[0])

            def add_ada(kind, j):
                n = UNIT[kind, j]
                dve.wait_ge(raw_in[n % RING], 16 * (n // RING + 1))
                kt, dst = (j // 2, ada_acc[:, (j % 2) * D:(j % 2 + 1) * D]) if kind == "ada" else (j, gate_post[:, :])
                first = kt == 0
                if not first:
                    dve.wait_ge(ada_summed, j - 1 if kind == "ada" else 16 + j)
                if first:
                    nc.vector.tensor_scalar(dst, raw[:, n % RING, :], silu_c[:, kt:kt + 1], None, ALU.mult)\
                        .then_inc(ada_summed, 1)
                else:
                    nc.vector.scalar_tensor_tensor(out=dst, in0=raw[:, n % RING, :], scalar=silu_c[:, kt:kt + 1], in1=dst,
                                                   op0=ALU.mult, op1=ALU.add).then_inc(ada_summed, 1)

            def split_lo(k):
                kind, j = USED[k]
                n, width = UNIT[kind, j], WIDTH.get(kind, U)
                before = n - 1
                while before >= 0 and ORDER[before][0] == "gate_ada":
                    before -= 1
                for u in ORDER[before + 1:n]:
                    add_ada(*u)
                dve.wait_ge(hi_made, k + 1)
                nc.vector.tensor_tensor(out=w_lo[:, k % SPLITS, 0:width], in0=raw[:, n % RING, 0:width],
                                        in1=w_hi[:, k % SPLITS, 0:width].bitcast(f32), op=ALU.subtract).then_inc(lo_made, 1)

            def scale_level(m):
                half = LEVELS[m % NL]
                if not half:
                    return
                g = m // NL
                dve.wait_ge(level_exp, pair_levels(m))
                x = level_view(xq[:, m % 2, :], half)
                q = level_view(queries[:, 2 * g:2 * g + 2, :].rearrange("p h s -> p (h s)"), half)
                kk = level_view(keys[:, 2 * g:2 * g + 2, :].rearrange("p h s -> p (h s)"), half)
                nc.vector.tensor_tensor(out=x[:, :, half:], in0=x[:, :, half:], in1=q[:, :, half:], op=ALU.mult)
                nc.vector.tensor_tensor(out=x[:, :, :half], in0=x[:, :, :half], in1=kk[:, :, :half], op=ALU.mult)\
                    .then_inc(level_x, 1)

            def copy_level(m):
                dve.wait_ge(scores_made, m + 1)
                g, half = m // NL, LEVELS[m % NL]
                if m:
                    dve.wait_ge(level_copied, m)
                if half:
                    for odd in range(2):
                        rows, part = slice(odd * C, (odd + 1) * C), slice(odd * C // 2, (odd + 1) * C // 2)
                        dst = attn[rows, 2 * g:2 * g + 2, :].rearrange("p h (t n w) -> p (h t) n w", t=TT, w=2 * half)
                        mask = level_view(level_mask[rows, m % NL, :], half)[:, :, half:]
                        src = side[m % 2][rows, :].rearrange("p (t s) -> p t s", s=C)[:, :, part]
                        ins = nc.vector.copy_predicated(
                            dst[:, :, :, half:], mask.unsqueeze(1).broadcast_to([C, 2 * TT, C // (2 * half), half]),
                            src.rearrange("p t (n w) -> p t n w", w=half))
                else:
                    ins = nc.vector.copy_predicated(attn[:, 2 * g:2 * g + 2, :].rearrange("p h (t s) -> p (h t) s", s=C),
                                                    level_mask[:, m % NL, :].unsqueeze(1).broadcast_to([P, 2 * TT, C]),
                                                    side[m % 2][:, :].rearrange("p (n s) -> p n s", s=C))
                ins.then_inc(level_copied, 1)

            def bound_gate(n):
                dve.wait_ge(silu_exp, n + 1)
                nc.vector.tensor_scalar(gate_e(n), gate_e(n), 1.0, 1.0e19, ALU.add, ALU.min).then_inc(silu_bound, 1)

            def finish_gate(n, result, dst):
                dve.wait_ge(silu_sig, n + 1)
                ins = nc.vector.tensor_tensor(out=dst, in0=acc[result % 4][:, :], in1=gate_e(n), op=ALU.mult)
                ins.then_inc(freed["dve"], 1)

            def log_sum(j):
                dve.wait_ge(log_made, j + 1)
                nc.vector.tensor_tensor_scan(out=b_cum[:, j, :], data0=chunk_keep[:, :], data1=b_cum[:, j, :], initial=0.0,
                                             op0=ALU.mult, op1=ALU.add).then_inc(b_made, 1)

            def prepare_head(n):
                b = b_cum[:, n, :].rearrange("p (c t) -> p c t", t=C)
                if n:
                    dve.wait_ge(kT_made, n)
                else:
                    dve.wait_ge(scores_made, 4 * NL)
                nc.vector.tensor_tensor(out=k_dec[:, :].rearrange("p (c t) -> p c t", t=C),
                                        in0=b[:, :, C - 1:C].broadcast_to([P, NC, C]), in1=b, op=ALU.subtract)\
                    .then_inc(decay_diff, 1)
                dve.wait_ge(decay_exp, 2 * n + 1)
                nc.vector.tensor_copy(b_end[:, n % 2, :], e_b[:, :].rearrange("p (c t) -> p c t", t=C)[:, :, C - 1])
                if n >= 2:
                    dve.wait_ge(o_made, n - 1)
                nc.vector.tensor_tensor(out=q_dec[:, n % 2, :], in0=e_b[:, :], in1=queries[:, n, :], op=ALU.mult)
                dve.wait_ge(decay_exp, 2 * n + 2)
                nc.vector.tensor_tensor(out=k_dec[:, :], in0=k_dec[:, :], in1=keys[:, n, :], op=ALU.mult)\
                    .then_inc(prep_made, 1)

            def chain_states(n):
                dve.wait_ge(outer_made, n + 1)
                if n:
                    dve.wait_ge(o_made, n)
                then(nc.vector.tensor_copy(states[:, 0, :], side[1][:, 0:P]))
                for c in range(1, NC - 1):
                    ins = nc.vector.scalar_tensor_tensor(
                        out=states[:, c, :], in0=states[:, c - 1, :], scalar=b_end[:, n % 2, c:c + 1],
                        in1=side[1 + c % 2][:, (c // 2) * P:(c // 2 + 1) * P], op0=ALU.mult, op1=ALU.add)
                    if c < NC - 2:
                        then(ins)
                    else:
                        ins.then_inc(states_made, 1)

            def finish_head(n):
                dve.wait_ge(o_rstd, n + 1)
                then(nc.vector.tensor_tensor(out=o_sb[:, :], in0=o_sb[:, :], in1=o_sq[:, :], op=ALU.mult))
                nc.vector.scalar_tensor_tensor(out=o_sb[:, :], in0=o_sb[:, :], scalar=par[:, PAR["nw"]],
                                               in1=silu_out[:, n % 2, :], op0=ALU.mult, op1=ALU.mult).then_inc(o_final, 1)
                dve.wait_ge(o_final, n + 1)
                dve.wait_ge(mixh_hi_made, n + 1)
                nc.vector.tensor_tensor(out=mixh_lo[:, n, :], in0=o_sb[:, :], in1=mixh_hi[:, n, :].bitcast(f32),
                                        op=ALU.subtract).then_inc(mixh_made, 1)

            def end_tile(gate, raws):
                name, kt = FINAL[finals[0]]
                if finals[0]:
                    dve.wait_ge(y_made, finals[0])
                nc.vector.tensor_tensor(out=y_tmp[:, :], in0=gate, in1=raws[name][:, kt, :], op=ALU.mult).then_inc(y_final, 1)
                finals[0] += 1
                dve.wait_ge(y_final, finals[0])
                dve.wait_ge(y_hi_made, finals[0])
                nc.vector.tensor_tensor(out=y_lo[name][:, kt, :], in0=y_tmp[:, :], in1=y_hi[name][:, kt, :].bitcast(f32),
                                        op=ALU.subtract).then_inc(y_made, 1)

            def enter_second_block():
                def make_x2(t):
                    r = RESULT["wo", 1] + t
                    dve.wait_ge(y_rstd, t + 1)
                    if t == 2:
                        dve.wait_ge(unit_used, STEP["wo", 15] + 1)
                    then(nc.vector.scalar_tensor_tensor(out=x2[:, t, S:D], in0=acc[r % 4][:, :],
                                                        scalar=rstd_y[:, t:t + 1], in1=gate_post[:, S:D],
                                                        op0=ALU.mult, op1=ALU.mult))
                    nc.vector.tensor_tensor(out=x2[:, t, S:D], in0=x2[:, t, S:D], in1=x_again[:, t, S:D], op=ALU.add)\
                        .then_inc(freed["dve"], 1)
                    nc.vector.scalar_tensor_tensor(out=x2[:, t, 0:S], in0=y_left[:, t, :], scalar=rstd_y[:, t:t + 1],
                                                   in1=x_again[:, t, 0:S], op0=ALU.mult, op1=ALU.add).then_inc(x2_made, 1)

                def gain(t):
                    dve.wait_ge(x2_made, t + 1)
                    wait_freed(dve, RESULT["wo", 1] + t)
                    nc.vector.tensor_tensor(out=x2_gain[:, t, :], in0=x2[:, t, :], in1=norm_row[:, :], op=ALU.mult)\
                        .then_inc(gain_made, 1)

                def diagonal(t):
                    dve.wait_ge(x2_rstd, t + 1)
                    nc.vector.tensor_scalar(diag[:, t, :], ident[:, :], rstd_h[:, t:t + 1], None, ALU.mult)\
                        .then_inc(diag_made, 1)

                def lower_h2(t):
                    for n in (2 * t, 2 * t + 1):
                        dve.wait_ge(h2_hi_made, n + 1)
                        half = n % 2
                        tiles = (slice(None), slice(4 * half, 4 * half + 4), slice(t * P, (t + 1) * P))
                        nc.vector.tensor_tensor(out=hT_lo[tiles], in0=side[n % 4][:, :].rearrange("p (k s) -> p k s", s=P),
                                                in1=hT_hi[tiles].bitcast(f32), op=ALU.subtract).then_inc(h2_made, 1)

                dve.wait_ge(x_again_here, 16)
                dve.wait_ge(norm_here, 16)
                make_x2(0)
                gain(0)
                make_x2(1)
                diagonal(0)
                gain(1)
                make_x2(2)
                diagonal(1)
                lower_h2(0)
                split_lo(STEP["bs", 2])
                make_x2(3)
                gain(2)
                diagonal(2)
                lower_h2(1)
                gain(3)
                diagonal(3)
                lower_h2(2)
                lower_h2(3)

            def side_slot(slot):
                for s in SCORES_AT.get(slot, []):
                    w = (s // 4 % TT + 1) * P
                    dve.wait_ge(logits_made, s + 1)
                    col = slice(s, s + 1)
                    if s < SPARSE:
                        nc.vector.tensor_reduce(out=top_neg[:, col], in_=side[s % 2][:, 0:w], axis=AX.X, op=ALU.max,
                                                negate=True).then_inc(max_made, 1)
                    else:
                        cq = cum_q[:, s - SPARSE:s - SPARSE + 1]
                        then(nc.vector.tensor_reduce(out=top_max[:, col], in_=side[s % 2][:, 0:w], axis=AX.X, op=ALU.max))
                        then(nc.vector.tensor_tensor(out=top_max[:, col], in0=top_max[:, col], in1=cq, op=ALU.add))
                        nc.vector.tensor_tensor(out=top_neg[:, col], in0=cq, in1=top_max[:, col], op=ALU.subtract)\
                            .then_inc(max_made, 1)
                for s in SCORES_AT.get(slot, []):
                    w = (s // 4 % TT + 1) * P
                    dve.wait_ge(exp_made, s + 1)
                    then(nc.vector.reciprocal(row_inv[:, s:s + 1], row_sum[:, s:s + 1]))
                    nc.vector.tensor_scalar(probs[:, s % 2, 0:w], probs[:, s % 2, 0:w], row_inv[:, s:s + 1], None, ALU.mult)\
                        .then_inc(probs_made, 1)

            def topk_round(t, r):
                w = (t + 1) * P
                sc = score[:, t - 1, 0:w]
                if r == 0:
                    dve.wait_ge(cut_made, t)
                then(nc.vector.max(top8, sc))
                then(nc.vector.match_replace(sc, top8, sc, TAKEN))
                if r == ROUNDS - 1:
                    nc.vector.tensor_scalar(sel16[:, t - 1, 0:w], sc, (OUTSIDE + TAKEN) / 2, NEG, ALU.is_gt, ALU.mult)\
                        .then_inc(sel_made, 1)

            dve.wait_ge(consts, 8)
            nc.vector.tensor_copy(ident16[:, :], ident[:, :])
            nc.vector.tensor_copy(pick[:, :], pick_f[0:36, :]).then_inc(pick_made, 1)
            then(nc.vector.tensor_scalar(idx[:, 1, :], idx[:, 1, :], C - 1, None, ALU.bitwise_and))
            then(nc.vector.tensor_tensor(out=later[:, :], in0=idx[:, 0, :], in1=idx[:, 1, :], op=ALU.is_gt))
            then(nc.vector.tensor_tensor(out=idx[:, 0, :], in0=idx[:, 0, :], in1=idx[:, 1, :], op=ALU.bitwise_xor))
            nc.vector.tensor_scalar(level_mask[:, NL - 1, :], idx[:, 0, :], 0, None, ALU.is_equal)
            then(nc.vector.tensor_tensor(out=later[:, :], in0=idx[:, 0, :], in1=later[:, :], op=ALU.mult))
            for l, half in enumerate(LEVELS[:-1]):
                then(nc.vector.tensor_scalar(junk[:, 0:C], later[:, :], float(half), None, ALU.is_ge))
                then(nc.vector.scalar_tensor_tensor(out=level_mask[:, l, :], in0=later[:, :], scalar=float(2 * half),
                                                    in1=junk[:, 0:C], op0=ALU.is_lt, op1=ALU.mult))
            for r in range(16):
                nc.vector.memset(inv_count[:, r:r + 1], 1.0 / (r + 1))
            dve.wait_ge(par_here, 16)
            nc.vector.tensor_tensor(out=low_b, in0=par[:, PAR["lb"]], in1=par[:, PAR["lb"]], op=ALU.subtract)\
                .then_inc(lb_diff, 1)
            dve.wait_ge(c_exp, 1)
            then(nc.vector.tensor_scalar(tmp8, tmp8, 1.0, None, ALU.add))
            then(nc.vector.reciprocal(tmp8, tmp8))
            then(nc.vector.tensor_tensor(out=silu_c, in0=tmp8, in1=par[:, PAR["c"]], op=ALU.mult))
            dve.wait_ge(lb_exp, 1)
            then(nc.vector.reciprocal(tmp8, one_low))
            then(nc.vector.tensor_tensor(out=one_low, in0=one_low, in1=tmp8, op=ALU.mult))
            then(nc.vector.tensor_tensor(out=low_b, in0=one_low, in1=one_low, op=ALU.subtract))
            then(nc.vector.tensor_scalar(one_low, low_b, -1.0, 1.0, ALU.mult, ALU.add))
            for j in range(16):
                add_ada("ada", j)
            dve.wait_ge(mod_summed, 1)
            then(nc.vector.tensor_tensor(out=mod, in0=side[0][:, 0:16], in1=par[:, PAR["ada_b"]], op=ALU.add))
            then(nc.vector.scalar_tensor_tensor(out=scale_a, in0=mod[:, 8:16], scalar=1.0, in1=par[:, PAR["pre_w"]],
                                                op0=ALU.add, op1=ALU.mult))
            for kt in range(KT):
                dve.wait_ge(xT_copied, kt + 1)
                nc.vector.tensor_scalar(hT_full[:, kt, :], hT_full[:, kt, :], scale_a[:, kt:kt + 1], mod[:, kt:kt + 1],
                                        ALU.mult, ALU.add).then_inc(h_full, 1)
            split_lo(0)
            for kt in range(KT):
                dve.wait_ge(h_full, kt + 1)
                dve.wait_ge(h_hi, kt + 1)
                nc.vector.tensor_tensor(out=hT_lo[:, kt, :], in0=hT_full[:, kt, :], in1=hT_hi[:, kt, :].bitcast(f32),
                                        op=ALU.subtract).then_inc(h_lo, 1)
            for k in range(1, AHEAD):
                split_lo(k)

            gates = 0
            finals = [0]
            before = (None, 0)
            for k, (kind, j) in enumerate(USED):
                if k + AHEAD < len(USED) and (kind, j) != ("wo", 15):
                    split_lo(k + AHEAD)
                if before[0] in ("gp", "gh"):
                    finish_gate(gates - 1, RESULT[before], silu_out[:, before[1] % 2, :])
                if before[0] == "dz":
                    finish_gate(gates - 1, RESULT[before], z_d[:, before[1], :])
                if before[0] in ("az", "bz", "cz"):
                    if finals[0]:
                        dve.wait_ge(y_made, finals[0])
                    finish_gate(gates - 1, RESULT[before], y_tmp[:, :])
                    dve.wait_ge(freed["dve"], FREED[RESULT[before]][1])
                    end_tile(y_tmp[:, :], y_raw)
                if k == D_FINAL_AT:
                    dve.wait_ge(bank3_read, 2 * TT)
                    for h in range(4):
                        end_tile(z_d[:, h, :], y_raw)
                before = (kind, j)
                m = LEVEL_AT.get((kind, j))
                if m is not None:
                    scale_level(m)
                    diff_level(dve, nc.vector, m + 1)
                    if m:
                        copy_level(m - 1)
                if k - 2 in range(HEADS):
                    log_sum(k - 2)
                if k - 1 in range(HEADS):
                    h = k - 1
                    dve.wait_ge(f_sig, h + 1)
                    then(nc.vector.tensor_scalar(b_cum[:, h, :], b_cum[:, h, :], one_low[:, h:h + 1], low_b[:, h:h + 1],
                                                 ALU.mult, ALU.add))
                    nc.vector.tensor_scalar(keys[:, h, :], b_cum[:, h, :], -1.0, 1.0, ALU.mult, ALU.add).then_inc(f_made, 1)
                if kind == "f":
                    wait_freed(dve, RESULT[kind, j])
                    nc.vector.tensor_scalar(b_cum[:, j, :], b_cum[:, j, :], 1.0, 1.0e19, ALU.add, ALU.min).then_inc(f_bound, 1)
                if (kind, j) == ("q", 7):
                    wait_freed(dve, RESULT["q", 7])
                    dve.wait_ge(b_made, HEADS)
                    dve.wait_ge(f_made, HEADS)
                    diff_level(dve, nc.vector, 0)
                if (kind, j % 2) == ("gp", 0):
                    g, w = j // 2, 2 << (j // 2)
                    total, diff = sums[g % 2], sums[(g + 1) % 2][:, :, 0:S]
                    dve.wait_ge(sum_made, g + 1)
                    then(nc.vector.scalar_tensor_tensor(out=diff, in0=total[:, :, 16:], scalar=1.0 / w,
                                                        in1=u_pad[:, :, 16:], op0=ALU.mult, op1=ALU.subtract))
                    then(nc.vector.tensor_tensor(out=diff[:, :, 0:w - 1], in0=total[:, :, 16:15 + w],
                                                 in1=inv_count[:, 0:w - 1].unsqueeze(1).broadcast_to([P, 2, w - 1]),
                                                 op=ALU.mult))
                    nc.vector.tensor_tensor(out=diff[:, :, 0:w - 1], in0=diff[:, :, 0:w - 1],
                                            in1=u_pad[:, :, 16:15 + w], op=ALU.subtract).then_inc(d_made, 1)
                if kind in GATES:
                    bound_gate(gates)
                    gates += 1
                if (kind, j % 2) == ("gp", 0):
                    dve.wait_ge(d_hi_made, g + 1)
                    dve.wait_ge(d_made, g + 1)
                    nc.vector.tensor_tensor(out=d_lo[:, :, :], in0=diff, in1=d_hi[:, :, :].bitcast(f32),
                                            op=ALU.subtract).then_inc(d_lo_made, 1)
                if kind == "pw":
                    dve.wait_ge(unit_used, k + 1)
                    wait_freed(dve, RESULT["gp", 2 * j + 1])
                    for o in range(2):
                        r = RESULT["pw", j] + o
                        nc.vector.scalar_tensor_tensor(out=mix_pool[:, 2 * j + o, :], in0=acc[r % 4][:, :],
                                                       scalar=par[:, PAR["pool_scale"]][:, 2 * j + o:2 * j + o + 1],
                                                       in1=silu_out[:, o, :], op0=ALU.mult, op1=ALU.mult)\
                            .then_inc(freed["dve"], 1)
                if (kind, j) == ("i", 7):
                    copy_level(4 * NL - 1)
                    prepare_head(0)
                n = HEAD_AT.get((kind, j))
                if n is not None:
                    if n + 1 < HEADS:
                        prepare_head(n + 1)
                    if n < HEADS:
                        chain_states(n)
                    if n:
                        finish_head(n - 1)
                if kind == "gh":
                    dve.wait_ge(mixp_hi_made, j + 1)
                    nc.vector.tensor_tensor(out=mixp_lo[:, j, :], in0=mix_pool[:, j, :],
                                            in1=mixp_hi[:, j, :].bitcast(f32), op=ALU.subtract).then_inc(mixp_made, 1)
                if (kind, j) == ("wo", 10):
                    dve.wait_ge(gate_summed, 2)
                    dve.wait_ge(rows_here, 32)
                    for o in range(2):
                        half = slice(o * S, (o + 1) * S)
                        then(nc.vector.tensor_tensor(out=gate_row[:, half], in0=side[1 + o][:, :], in1=gate_row[:, half],
                                                     op=ALU.add))
                        then(nc.vector.tensor_tensor(out=gate_post[:, half], in0=gate_row[:, half], in1=post_row[:, half],
                                                     op=ALU.mult))
                    wait_freed(dve, RESULT["wo", 0] + TT - 1)
                    nc.vector.tensor_scalar(ss_y[:, 8:12], ss_y[:, 0:4], 1.0 / D, EPS, ALU.mult, ALU.add)\
                        .then_inc(y_bias_made, 1)
                    for t in range(TT):
                        then(nc.vector.tensor_tensor(out=y_left[:, t, :], in0=y_left[:, t, :], in1=gate_post[:, 0:S],
                                                     op=ALU.mult))
                if (kind, j) == ("wo", 15):
                    enter_second_block()
                r = RESULT.get((kind, j))
                if (kind, j) == ("bs", 3):
                    dve.wait_ge(small_rows, 32)
                    dve.wait_ge(lat_rstd, 1)
                    for twice in range(2):
                        then(nc.vector.tensor_copy(key_twice[:, :, 64 * twice:64 * twice + 64], side_tok[:, :, 384:448]))
                    for t in range(TT):
                        ins = nc.vector.scalar_tensor_tensor(out=lat[:, t, :], in0=side_tok[:, t, 0:P],
                                                             scalar=rstd_kv[:, t:t + 1], in1=kv_row[:, :],
                                                             op0=ALU.mult, op1=ALU.mult)
                        ins.then_inc(lat_made, 1)
                    then(nc.vector.tensor_scalar(idx_w.rearrange("p (t h) -> p t h", h=4), side_tok[:, :, 448:452], 0.5,
                                                 None, ALU.mult))
                if kind == "bq" and j:
                    w = (j + 1) * P
                    for h in range(4):
                        n = 4 * (j - 1) + h
                        dve.wait_ge(relu_made, n + 1)
                        if h:
                            dve.wait_ge(relu_used, n)
                        weight = idx_w[:, 4 * j + h:4 * j + h + 1]
                        sc = score[:, j - 1, 0:w]
                        if h == 0:
                            ins = nc.vector.tensor_scalar(sc, relu[:, n % 2, 0:w], weight, None, ALU.mult)
                        else:
                            ins = nc.vector.scalar_tensor_tensor(out=sc, in0=relu[:, n % 2, 0:w], scalar=weight, in1=sc,
                                                                 op0=ALU.mult, op1=ALU.add)
                        ins.then_inc(relu_used, 1)
                if (kind, j) == ("av", 3):
                    for t in range(TT):
                        dve.wait_ge(unit_used, k + 1)
                        then(nc.vector.bn_stats(bn[:, 6 * t:6 * t + 6], acc[(RESULT["av", 0] + t) % 4][:, :]))
                    for t in range(TT):
                        ins = nc.vector.bn_aggr(bn_mean[:, 2 * t:2 * t + 2], bn[:, 6 * t:6 * t + 6])
                    ins.then_inc(bn_made, 1)
                    dve.wait_ge(bn_made, 1)
                    dve.wait_ge(bn_rstd, 1)
                    dve.wait_ge(spatial_here, 64)
                    for t in range(TT):
                        r = RESULT["av", 0] + t
                        nc.vector.tensor_scalar(v_norm[:, t, :], acc[r % 4][:, :], bn_mean[:, 2 * t:2 * t + 1],
                                                rstd_v[:, t:t + 1], ALU.subtract, ALU.mult).then_inc(freed["dve"], 1)
                    for t in range(TT):
                        wait_freed(dve, RESULT["av", 0] + t)
                        then(nc.vector.tensor_tensor(out=v_norm[:, t, :], in0=v_norm[:, t, :], in1=ln_rows[:, 0, :],
                                                     op=ALU.mult))
                        nc.vector.tensor_tensor(out=v_norm[:, t, :], in0=v_norm[:, t, :], in1=ln_rows[:, 1, :],
                                                op=ALU.add).then_inc(v_made, 1)
                if kind == "cx":
                    wait_freed(dve, RESULT["cc", j])
                    dve.wait_ge(unit_used, k + 1)
                    if j == 0:
                        then(nc.vector.memset(conv_in[:, 0:2], 0.0))
                    nc.vector.tensor_tensor(out=conv_in[:, 2:], in0=acc[r % 4][:, :], in1=c_gate[:, :], op=ALU.mult)\
                        .then_inc(freed["dve"], 1)
                    wait_freed(dve, r)
                    taps = par[:, PAR["conv_w"]]
                    then(nc.vector.tensor_scalar(conv[:, :], conv_in[:, 0:S], taps[:, j:j + 1], None, ALU.mult))
                    for tap in (1, 2):
                        then(nc.vector.scalar_tensor_tensor(out=conv[:, :], in0=conv_in[:, tap:tap + S],
                                                            scalar=taps[:, 4 * tap + j:4 * tap + j + 1], in1=conv[:, :],
                                                            op0=ALU.mult, op1=ALU.add))
                if kind == "cb":
                    dve.wait_ge(unit_used, k + 1)
                    nc.vector.tensor_tensor(out=y_raw["c"][:, j, :], in0=acc[r % 4][:, :], in1=conv[:, :], op=ALU.mult)\
                        .then_inc(freed["dve"], 1)
                slot = k - SLOT0
                side_slot(slot)
                if slot in MIXED_AT:
                    g = MIXED_AT[slot]
                    dve.wait_ge(mixed_made, g + 1)
                    wait_freed(dve, RESULT["au", g])
                    nc.vector.tensor_tensor(out=y_tmp2.rearrange("p (c t) -> p c t", t=P),
                                            in0=side[g % 2][:, :].rearrange("p (c t) -> p c t", t=P),
                                            in1=mix_b[:, g, :].unsqueeze(1).broadcast_to([P, TT, P]), op=ALU.add)\
                        .then_inc(mixed_read, 1)
                    dve.wait_ge(mixed_read, g + 1)
                    then(nc.vector.tensor_tensor(out=y_raw["a"][:, g, :], in0=y_raw["a"][:, g, :], in1=y_tmp2, op=ALU.mult))
                if slot == FORGET_AT:
                    dve.wait_ge(fgt_made, 1)
                    then(nc.vector.memset(forget_r[:, :].bitcast(f32), 0.0))
                    then(nc.vector.tensor_scalar(forget[:, 0, :], side[0][0:4, :], bf_col[0:4, :], None, ALU.add))
                    then(nc.vector.tensor_scalar(forget[:, 1, :], forget[:, 0, :], -1.0, None, ALU.mult))
                    nc.vector.tensor_tensor(out=forget[:, 1, :], in0=forget[:, 0, :], in1=forget[:, 1, :], op=ALU.max)\
                        .then_inc(fgt_abs, 1)
                    dve.wait_ge(fgt_abs, 1)
                    then(nc.vector.tensor_scalar(forget[:, 0, :], forget[:, 0, :], 0.0, None, ALU.min))
                    dve.wait_ge(fgt_ln, 1)
                    then(nc.vector.tensor_tensor(out=forget[:, 0, :], in0=forget[:, 0, :], in1=forget[:, 1, :],
                                                 op=ALU.subtract))
                    then(nc.vector.memset(forget[:, 1, :], 1.0))
                    nc.vector.tensor_tensor_scan(out=forget[:, 0, :], data0=forget[:, 1, :], data1=forget[:, 0, :],
                                                 initial=0.0, op0=ALU.mult, op1=ALU.add).then_inc(fgt_sum, 1)
                    dve.wait_ge(fgt_sum, 1)
                    dve.wait_ge(fgt_hi, 1)
                    then(nc.vector.tensor_tensor(out=forget[:, 1, :], in0=forget[:, 0, :],
                                                 in1=forget_r[0:4, :].bitcast(f32), op=ALU.add))
                    nc.vector.tensor_scalar(forget_r[32:36, :], forget[:, 1, :], -1.0, None, ALU.mult).then_inc(fgt_ready, 1)
                if slot == CUM_AT:
                    dve.wait_ge(cum_made, 1)
                    nc.vector.tensor_copy(cum_q, side[1][:, 0:16]).then_inc(cum_read, 1)
                for t, rr in topk_rounds(slot):
                    topk_round(t, rr)
                if kind == "br":
                    dve.wait_ge(unit_used, k + 1)
                    for o in range(2):
                        g = 2 * j + o
                        wait_freed(dve, RESULT["ga", g])
                        first = g % 4 == 0
                        if first and j >= 2:
                            dve.wait_ge(m_made, j // 2)
                        dst = merged[:, :] if first else merged_part[:, :]
                        nc.vector.tensor_tensor(out=dst, in0=acc[(r + o) % 4][:, :], in1=sig[:, g % 2, :], op=ALU.mult)\
                            .then_inc(freed["dve"], 1)
                        wait_freed(dve, r + o)
                        if not first:
                            ins = nc.vector.tensor_tensor(out=merged[:, :], in0=merged[:, :], in1=merged_part[:, :],
                                                          op=ALU.add)
                            if g % 4 == 3:
                                ins.then_inc(m_sum, 1)
                            else:
                                then(ins)
                    if j % 2:
                        dve.wait_ge(m_sum, j // 2 + 1)
                        dve.wait_ge(m_hi_made, j // 2 + 1)
                        nc.vector.tensor_tensor(out=m_lo[:, j // 2, :], in0=merged[:, :],
                                                in1=m_hi[:, j // 2, :].bitcast(f32), op=ALU.subtract).then_inc(m_made, 1)
                if (kind, j) == ("w2", 3):
                    dve.wait_ge(unit_used, k + 1)
                    for t in range(TT):
                        r = RESULT["w2", 0] + t
                        nc.vector.tensor_tensor(out=x2[:, t, 0:S], in0=acc[r % 4][:, :], in1=x2[:, t, 0:S],
                                                op=ALU.add).then_inc(freed["dve"], 1)
                if (kind, j) == ("w2", 4):
                    dve.wait_ge(h_sq, 4)
                    dve.wait_ge(final_here, 16)
                    nc.vector.tensor_scalar(rstd_o[:, 4:8], ss_o[:, 0:4], 1.0 / D, EPS, ALU.mult, ALU.add)
                    for t in range(TT):
                        wait_freed(dve, RESULT["w2", 0] + t)
                        ins = nc.vector.tensor_tensor(out=x2[:, t, 0:S], in0=x2[:, t, 0:S], in1=final_row[:, 0:S],
                                                      op=ALU.mult)
                    ins.then_inc(left_scaled, 1)
                if (kind, j) == ("w2", 7):
                    def finish_right(t):
                        dve.wait_ge(h_rstd, t + 1)
                        nc.vector.scalar_tensor_tensor(out=x2[:, t, S:D], in0=x2[:, t, S:D], scalar=rstd_o[:, t:t + 1],
                                                       in1=final_row[:, S:D], op0=ALU.mult, op1=ALU.mult)\
                            .then_inc(out_made, 1)

                    for t in range(TT):
                        r = RESULT["w2", 1] + t
                        if t < TT - 1:
                            dve.wait_ge(out_tiles_made, t + 1)
                        else:
                            dve.wait_ge(unit_used, k + 1)
                        nc.vector.tensor_tensor(out=x2[:, t, S:D], in0=acc[r % 4][:, :], in1=x2[:, t, S:D],
                                                op=ALU.add).then_inc(freed["dve"], 1)
                        if t:
                            finish_right(t - 1)
                    finish_right(TT - 1)

        @block.tensor
        def _(pe):
            def weights(k):
                pe.wait_ge(lo_made, k + 1)
                return w_hi[:, k % SPLITS, :], w_lo[:, k % SPLITS, :]

            def bank(result):
                if result >= 4:
                    wait_freed(pe, result - 4)
                return acc[result % 4]

            def product(ps, w, x, first, last):
                nc.tensor.matmul(ps, w[0], x[0], start=first, stop=False)
                nc.tensor.matmul(ps, w[0], x[1], start=False, stop=False)
                return nc.tensor.matmul(ps, w[1], x[0], start=False, stop=last)

            def panel(k, kind, j, x, tiles, ready=None):
                hi, lo = weights(k)
                ps = bank(RESULT[kind, j])
                for kt in range(tiles):
                    if ready is not None:
                        pe.wait_ge(ready, kt + 1)
                    cols = slice(kt * P, (kt + 1) * P)
                    ins = product(ps[:, :], (hi[:, cols], lo[:, cols]), (x[0][:, kt, :], x[1][:, kt, :]),
                                  kt == 0, kt == tiles - 1)
                ins.then_inc(unit_used, 1)

            def token_units(k, kind, j, source, width, x_ready=None, tile_made=None):
                per, count = TOKEN_UNITS[kind], TOGETHER.get((kind, j), 1)
                for t in range(TT):
                    r = RESULT[kind, j // per] + t
                    tok = slice(t * P, (t + 1) * P)
                    if x_ready is not None:
                        x_ready(t)
                    for i in range(count - 1, -1, -1):
                        hi, lo = weights(k - i)
                        first, last = (j - i) % per == 0, (j - i) % per == per - 1
                        ps = bank(r) if first else acc[r % 4]
                        for a in range(2):
                            x = source(2 * ((j - i) % per) + a)
                            cols = slice(a * width, (a + 1) * width)
                            ins = product(ps[:, 0:width], (x[0][:, tok], x[1][:, tok]), (hi[:, cols], lo[:, cols]),
                                          first and a == 0, last and a == 1)
                    if tile_made is not None and t < TT - 1:
                        ins.then_inc(tile_made, 1)
                ins.then_inc(unit_used, count)

            def level_scores(m):
                g = m // NL
                if LEVELS[m % NL]:
                    pe.wait_ge(level_x, pair_levels(m))
                if m >= 2:
                    pe.wait_ge(level_copied, m - 1)
                half = LEVELS[m % NL]
                for h in range(2):
                    if half:
                        for c in range(0, NC, 2):
                            both = xq[:, m % 2, h * S + c * C:h * S + (c + 2) * C]
                            n0 = (h * NC + c) * C // 2
                            ins = nc.tensor.matmul(side[m % 2][:, n0:n0 + C], both, level_view(both, half)[:, :, half:],
                                                   start=True, stop=True)
                        continue
                    for c in range(NC):
                        left, right = (t[:, 2 * g + h, c * C:(c + 1) * C] for t in (keys, queries))
                        p0, n0 = (c % 2) * C, h * (S // 2) + (c // 2) * C
                        ins = nc.tensor.matmul(side[m % 2][p0:p0 + C, n0:n0 + C], left, right, start=True, stop=True)
                ins.then_inc(scores_made, 1)

            def transpose_keys(n):
                pe.wait_ge(prep_made, n + 1)
                if n >= 2:
                    pe.wait_ge(o_rstd, n - 1)
                elif n == 0:
                    pe.wait_ge(level_copied, 4 * NL)
                for t in range(TT):
                    ins = nc.tensor.transpose(side[0][:, t * P:(t + 1) * P], k_dec[:, t * P:(t + 1) * P], ident[:, :])
                ins.then_inc(kT_made, 1)

            def outer_products(n):
                pe.wait_ge(kT_copied, n + 1)
                if n:
                    pe.wait_ge(states_made, n)
                for c in range(NC - 1):
                    rows = slice((c % 2) * C, (c % 2 + 1) * C)
                    ins = nc.tensor.matmul(side[1 + c % 2][:, (c // 2) * P:(c // 2 + 1) * P], k_decT[rows, c // 2, :],
                                           values[rows, c // 2, n * P:(n + 1) * P], start=True, stop=True)
                ins.then_inc(outer_made, 1)

            def head_output(n):
                pe.wait_ge(states_made, n + 1)
                if n:
                    pe.wait_ge(o_squared, n)
                for c in range(1, NC):
                    cols = slice(c * C, (c + 1) * C)
                    nc.tensor.matmul(side[3][:, cols], states[:, c - 1, :], q_dec[:, n % 2, cols],
                                     start=(c == 1), stop=False)
                for parity in range(2):
                    if parity:
                        even.then_inc(even_made, 1)
                        pe.wait_ge(even_made, n + 1)
                    rows = slice(parity * C, (parity + 1) * C)
                    for c in range(parity, NC, 2):
                        ins = nc.tensor.matmul(side[3][:, c * C:(c + 1) * C], values[rows, c // 2, n * P:(n + 1) * P],
                                               attn[rows, n, (c // 2) * C:(c // 2 + 1) * C], start=False,
                                               stop=(c == NC - 1))
                    even = ins
                ins.then_inc(o_made, 1)

            def head_mean_squares(n):
                pe.wait_ge(o_squared, n + 1)
                nc.tensor.matmul(side[0][:, :], ones[:, :], o_sq[:, :], start=True, stop=True).then_inc(ms_made, 1)

            def transpose_x2(t):
                pe.wait_ge(gain_made, t + 1)
                pe.wait_ge(diag_made, t + 1)
                for n in (2 * t, 2 * t + 1):
                    if n >= 4:
                        pe.wait_ge(h2_made, n - 3)
                    for i in range(4):
                        kt = 4 * (n % 2) + i
                        ins = nc.tensor.matmul(side[n % 4][:, i * P:(i + 1) * P], x2_gain[:, t, kt * P:(kt + 1) * P],
                                               diag[:, t, :], start=True, stop=True)
                    ins.then_inc(x2T_made, 1)

            def h2_tile(t):
                if t == 0:
                    transpose_x2(0)
                if t < TT - 1:
                    transpose_x2(t + 1)
                pe.wait_ge(h2_made, 2 * t + 2)

            def turn(s):
                n = BANK2.index(("turn", s))
                pe.wait_ge(probs_made, s + 1)
                if n:
                    pe.wait_ge(bank2_read, n)
                for b in range(s // 4 % TT + 1):
                    ins = nc.tensor.transpose(side[2][:, b * P:(b + 1) * P], probs[:, s % 2, b * P:(b + 1) * P], ident[:, :])
                ins.then_inc(turned, 1)

            def sum_values(s):
                n = BANK2.index(("turn", s))
                pe.wait_ge(bank2_read, n + 1)
                h, blocks = s % 4, s // 4 % TT + 1
                if h == 0 and s:
                    pe.wait_ge(bank3_read, s // 4)
                if s == SPARSE:
                    wait_freed(pe, RESULT["dv", 0] + 3)
                for b in range(blocks):
                    v = lat[:, b, :] if s < SPARSE else fox_v[:, b, h * P:(h + 1) * P]
                    ins = nc.tensor.matmul(side[3][:, h * P:(h + 1) * P], v, probsT[:, s % 2, b * P:(b + 1) * P],
                                           start=(b == 0), stop=(b == blocks - 1))
                ins.then_inc(summed, 1)

            def logits(s):
                q, h = s // 4 % TT, s % 4
                w = (q + 1) * P
                ps = side[s % 2]
                tok = slice(q * P, (q + 1) * P)
                if s >= 2:
                    pe.wait_ge(exp_made, s - 1)
                if s < SPARSE:
                    if s == 0:
                        pe.wait_ge(latq_copied, 4)
                    if q:
                        pe.wait_ge(sel_made, q)
                    nc.tensor.matmul(ps[:, 0:w], lat_q[:, h, tok], latT[:, 0:w], start=True, stop=False)
                    bias = sel16[:, q - 1, 0:w] if q else causal16[:, :]
                    ins = nc.tensor.matmul(ps[:, 0:w], ident16[:, :], bias, start=False, stop=True)
                else:
                    if s == SPARSE:
                        wait_freed(pe, RESULT["dk", 3])
                        pe.wait_ge(fgt_ready, 1)
                        pe.wait_ge(cum_read, 1)
                    nc.tensor.matmul(ps[:, 0:w], fox_q[:, h, tok], fox_k[:, h, 0:w], start=True, stop=False)
                    nc.tensor.matmul(ps[:, 0:w], pick[:, h:h + 1].broadcast_to([36, P]), forget_r[:, 0:w],
                                     start=False, stop=False)
                    ins = nc.tensor.matmul(ps[:, w - P:w], ident16[:, :], causal16[:, :], start=False, stop=True)
                ins.then_inc(logits_made, 1)

            def side_slot(slot):
                turns, sums_ = TURN_AT.get(slot, []), SUM_AT.get(slot, [])
                for i in range(max(len(turns), len(sums_))):
                    if i < len(turns):
                        turn(turns[i])
                    if i < len(sums_):
                        sum_values(sums_[i])
                if slot in UP_AT:
                    q = UP_AT[slot]
                    n = BANK2.index(("up", q))
                    pe.wait_ge(bank2_read, n)
                    pe.wait_ge(bank3_read, q + 1)
                    for h in range(4):
                        ins = nc.tensor.matmul(side[2][:, h * P:(h + 1) * P], w_up[:, 1, h, :],
                                               lat_out[:, h * P:(h + 1) * P], start=True, stop=True)
                    ins.then_inc(turned, 1)
                for s in SCORES_AT.get(slot, []):
                    if 6 <= s <= 9:
                        pe.wait_ge(mixed_read, s - 5)
                    logits(s)
                if slot in MIXED_AT:
                    g = MIXED_AT[slot]
                    pe.wait_ge(v_made, TT)
                    pe.wait_ge(masked, 1)
                    pe.wait_ge(exp_made, 5 + g)
                    for t in range(TT):
                        ins = nc.tensor.matmul(side[g % 2][:, t * P:(t + 1) * P], v_norm[:, t, g * P:(g + 1) * P],
                                               mixT[:, g, :], start=True, stop=True)
                    ins.then_inc(mixed_made, 1)

            pe.wait_ge(consts, 2)
            for t in range(TT):
                pe.wait_ge(x_normed, t + 1)
                for kt in range(KT):
                    ins = nc.tensor.transpose((acc + side)[kt][:, t * P:(t + 1) * P], x_in[:, t, kt * P:(kt + 1) * P],
                                              ident[:, :])
                    if t == TT - 1:
                        ins.then_inc(xT_made, 1)
            pe.wait_ge(ada_summed, 16)
            pe.wait_ge(xT_copied, KT)
            for o in range(16):
                ins = nc.tensor.matmul(side[0][:, o:o + 1], ada_acc[:, o * P:(o + 1) * P], ones[:, 0:1],
                                       start=True, stop=True)
            ins.then_inc(mod_summed, 1)

            for k, (kind, j) in enumerate(USED):
                if (kind, j) in EARLIER:
                    continue
                if kind in PANELS:
                    panel(k, kind, j, (hT_hi, hT_lo), KT, h_lo if k == 0 else None)
                if kind in ("i", "bs", "av", "dv"):
                    token_units(k, kind, j, lambda kt: (hT_hi[:, kt, :], hT_lo[:, kt, :]), SIDE if kind == "bs" else S,
                                x_ready=h2_tile if (kind, j) == ("bs", 2) else None)
                if kind == "br":
                    hi, lo = weights(k)
                    for o in range(2):
                        name = "abcd"[2 * (j % 2) + o]
                        pe.wait_ge(y_made, 1 + FINAL.index((name, 3)))
                        ps = bank(RESULT[kind, j] + o)
                        for kt in range(4):
                            cols = slice((4 * o + kt) * P, (4 * o + kt + 1) * P)
                            ins = product(ps[:, :], (hi[:, cols], lo[:, cols]),
                                          (y_hi[name][:, kt, :], y_lo[name][:, kt, :]), kt == 0, kt == 3)
                    ins.then_inc(unit_used, 1)
                if kind == "w2":
                    pe.wait_ge(m_made, 2 * (j % 4) + 2)
                    token_units(k, kind, j, lambda kt: (m_hi[:, kt, :], m_lo[:, kt, :]), S,
                                tile_made=out_tiles_made if j == 7 else None)
                if kind == "pw":
                    pe.wait_ge(d_lo_made, j + 1)
                    hi, lo = weights(k)
                    for o in range(2):
                        ps = bank(RESULT[kind, j] + o)
                        for a in range(2):
                            cols = slice(a * 256 + o * P, a * 256 + (o + 1) * P)
                            ins = product(ps[:, :], (hi[:, cols], lo[:, cols]), (d_hi[:, a, :], d_lo[:, a, :]),
                                          a == 0, a == 1)
                    ins.then_inc(unit_used, 1)
                if kind == "wo":
                    ktp = j % 8
                    if ktp < 4:
                        pe.wait_ge(mixp_made, 2 * ktp + 2)
                    else:
                        pe.wait_ge(mixh_made, 2 * ktp - 6)
                    token_units(k, kind, j, lambda kt: (mixp_hi[:, kt, :], mixp_lo[:, kt, :]) if kt < KT else
                                (mixh_hi[:, kt - KT, :], mixh_lo[:, kt - KT, :]), S,
                                tile_made=y_tiles_made if j == 15 else None)
                if (kind, j) in LEVEL_AT:
                    level_scores(LEVEL_AT[kind, j])
                n = HEAD_AT.get((kind, j))
                if n is not None:
                    if n < HEADS:
                        transpose_keys(n)
                    if n:
                        head_output(n - 1)
                    if n < HEADS:
                        outer_products(n)
                    if n:
                        head_mean_squares(n - 1)
                if (kind, j) == ("wo", 8):
                    pe.wait_ge(ada_summed, 24)
                    for o in range(2):
                        nc.tensor.matmul(side[1 + o][:, :], ones[:, :], gate_post[:, o * S:(o + 1) * S],
                                         start=True, stop=True).then_inc(gate_summed, 1)
                if (kind, j) == ("bq", 0):
                    pe.wait_ge(lat_made, TT)
                    for t in range(TT):
                        for n, src in enumerate((lat[:, t, :], side_tok[:, t, P:2 * P], side_tok[:, t, 2 * P:3 * P],
                                                 key_twice[:, t, :])):
                            ins = nc.tensor.transpose(side[n][:, t * P:(t + 1) * P], src, ident[:, :])
                    ins.then_inc(idxT_made, 1)
                if kind == "bq" and j:
                    pe.wait_ge(idxT_copied, 4)
                    w = (j + 1) * P
                    for h in range(4):
                        if j > 1:
                            pe.wait_ge(relu_made, 4 * (j - 2) + h + 1)
                        rows = slice((h % 2) * 64, (h % 2 + 1) * 64)
                        nc.tensor.matmul(side[h][:, 0:w], idx_qT[rows, h // 2, j * P:(j + 1) * P], idx_kT[rows, 0:w],
                                         start=True, stop=True).then_inc(dots_made, 1)
                if (kind, j) == ("av", 0):
                    wait_freed(pe, RESULT["bq", 3])
                    pe.wait_ge(up_here, 32)
                    pe.wait_ge(relu_made, 12)
                    for h in range(4):
                        ins = nc.tensor.matmul(side[h][:, :], w_up[:, 0, h, :], lat_q[:, h, :], start=True, stop=True)
                    ins.then_inc(latq_made, 1)
                slot = k - SLOT0
                side_slot(slot)
                if slot == FORGET_AT:
                    pe.wait_ge(exp_made, SPARSE)
                    for t in range(TT):
                        ins = nc.tensor.transpose(side[0][0:4, t * P:(t + 1) * P], side_tok[:, t, 452:456], ident[:, :])
                    ins.then_inc(fgt_made, 1)
                if slot == CUM_AT:
                    pe.wait_ge(fgt_sum, 1)
                    for t in range(TT):
                        ins = nc.tensor.transpose(side[1][:, 4 * t:4 * t + 4], forget[:, 0, t * P:(t + 1) * P],
                                                  ident[0:4, 0:4])
                    ins.then_inc(cum_made, 1)


def kernel(**inputs):
    import numpy as _np
    import concourse.bacc as _bacc
    from concourse import mybir as _mybir
    from concourse.bass_utils import run_bass_kernel_spmd as _run

    def panels(w):
        k, n = w.shape
        return w.reshape(k // 128, 128, n // 128, 128).transpose(2, 1, 0, 3).reshape(n // 128, 128, k)

    def strips(w, n):
        k, total = w.shape
        return w.reshape(k // 256, 2, 128, total // n, n).transpose(3, 0, 2, 1, 4).reshape(-1, 128, 2 * n)

    def columns(v):
        return v.reshape(-1, 128).T

    a = {k: _np.asarray(v) for k, v in inputs.items()}
    w = a["w_in"][0]
    sec = {name: w[:, i * 1024:(i + 1) * 1024] for i, name in enumerate(("u", "gp", "q", "f", "i", "gh"))}
    arrays = {
        "x": a["x"][0],
        "ada_w": a["ada_w"][0],
        "par": _np.concatenate([
            columns(a["c"]), columns(a["ada_b"][0, :2048]), columns(a["norm_pre_w"]), columns(a["pool_scale"]),
            columns(a["hgrn_lower_bounds"]), columns(a["hgrn_norm_w"]),
            columns(a["conv_w_2"][0])], axis=1),
        "norm_g": a["norm_g_2"][0],
        "gate_b": a["ada_b"][0, 2048:],
        "post_w": a["norm_post_w"][0],
        "pw": a["pool_w"][0].reshape(4, 2, 128, 256).transpose(0, 2, 1, 3).reshape(4, 128, 512),
        "i": strips(sec["i"], 512),
        "wo": strips(a["w_out"][0], 512),
    }
    for name in ("f", "q", "u", "gp", "gh"):
        arrays[name] = panels(sec[name])
    w = a["w_in_2"][0]
    starts = _np.cumsum([0, 512, 512, 512, 512, 128 + 256 + 64 + 4, 512, 512, 512, 512, 512, 512, 512, 512, 4, 512, 4096])
    names = ("au", "av", "az", "bq", "side", "bz", "cb", "cc", "cx", "cz", "dq", "dk", "dv", "df", "dz", "ga")
    sec = {name: w[:, starts[i]:starts[i + 1]] for i, name in enumerate(names)}
    for name in ("au", "az", "bq", "bz", "cb", "cc", "cx", "cz", "dq", "dk", "dz"):
        arrays[name] = panels(sec[name])
    for name in ("av", "dv"):
        arrays[name] = strips(sec[name], 512)
    arrays["bs"] = strips(_np.concatenate([sec["side"], sec["df"]], axis=1), 456)
    arrays["ga"] = panels(sec["ga"]).reshape(4, 8, 128, 1024).transpose(1, 0, 2, 3).reshape(32, 128, 1024)
    arrays["br"] = a["w_branch_2"][0].reshape(2, 2, 4, 128, 8, 128).transpose(4, 0, 3, 1, 2, 5).reshape(16, 128, 1024)
    arrays["w2"] = strips(a["w_out_2"][0], 512)
    arrays["kv_g"] = a["dsa_kv_g_2"][0]
    arrays["b_f"] = a["fox_b_f_2"].reshape(4, 1)
    arrays["w_uk"] = a["dsa_w_uk_2"][0].transpose(2, 0, 1)
    arrays["w_uv"] = a["dsa_w_uv_2"][0].transpose(1, 0, 2)
    arrays["w_s"] = a["gm_w_s_2"][0].transpose(2, 0, 1)
    arrays["b_s"] = a["gm_b_s_2"][0].reshape(-1)
    arrays["ln_g"], arrays["ln_b"] = a["gm_ln_g_2"][0], a["gm_ln_b_2"][0]
    arrays["final_g"] = a["final_g_2"]
    nc = _bacc.Bacc("TRN2", target_bir_lowering=False, num_devices=1)
    feeds, dram = {}, {}
    for name, v in arrays.items():
        v = _np.ascontiguousarray(v)
        feeds[f"in_{name}"] = v
        dram[name] = nc.dram_tensor(f"in_{name}", v.shape, _mybir.dt.from_np(v.dtype), kind="ExternalInput").ap()
    out = nc.dram_tensor("out", (512, 1024), _mybir.dt.float32, kind="ExternalOutput").ap()
    program(nc, dram, out)
    r = _run(nc, [feeds], core_ids=[0])
    return r.results[0]["out"].reshape(1, 512, 1024)
```

```python
import numpy as np
import concourse.bass as bass
from concourse import mybir
from contextlib import ExitStack

P = 128
S = 512
TT = S // P
D = 1024
KT = D // P
W = 512
HEADS = 8
C = 64
NC = S // C
EPS = 1e-6
U = 1024
RING = 5
SPLITS = 4
AHEAD = SPLITS - 1
NEG = -1.0e30
OUTSIDE = -3.0e38
TAKEN = -3.3e38
SIDE = 128 + 256 + 64 + 4 + 4

ORDER = []
for kt in range(KT):
    ORDER += [("ada", 2 * kt), ("ada", 2 * kt + 1), ("fk", kt)]
ORDER += [("f", 7)] + [("q", j) for j in range(8)]
for g in range(4):
    ORDER += [("u", 2 * g), ("u", 2 * g + 1), ("gp", 2 * g), ("gp", 2 * g + 1),
              ("gate_ada", 2 * g), ("gate_ada", 2 * g + 1), ("pw", g)]
ORDER += [("i", j) for j in range(8)] + [("gh", j) for j in range(8)]
ORDER += [("wo", j) for j in range(16)]
for kind in ("bs", "bq", "av", "au", "az"):
    ORDER += [(kind, j) for j in range(4)]
for j in range(4):
    ORDER += [("cc", j), ("cx", j), ("cb", j), ("cz", j)]
for kind in ("dq", "dk", "dv", "bz", "dz"):
    ORDER += [(kind, j) for j in range(4)]
for j in range(KT):
    ORDER += [("ga", 4 * j), ("ga", 4 * j + 1), ("br", 2 * j), ("ga", 4 * j + 2), ("ga", 4 * j + 3), ("br", 2 * j + 1)]
ORDER += [("w2", j) for j in range(8)]
ADA = ("ada", "gate_ada")
UNIT = {u: n for n, u in enumerate(ORDER)}
USED = [u for u in ORDER if u[0] not in ADA]
STEP = {u: k for k, u in enumerate(USED)}
WIDTH = {"fk": 7 * P, "pw": 512, "bs": 2 * SIDE}
TOKEN_UNITS = {"i": 4, "wo": 8, "bs": 4, "av": 4, "dv": 4, "w2": 4}
GATES = ("gp", "gh", "az", "bz", "cz", "dz")
PANELS = ("f", "q", "u", "gp", "gh", "bq", "au", "az", "bz", "cc", "cx", "cb", "cz", "dq", "dk", "dz", "ga")
PAIRS = ("pw", "br")
BY_DVE = ("gp", "gh", "pw", "az", "bz", "cz", "dz", "cx", "cb", "br", "w2")

GATE_ORDER = [u for u in USED if u[0] in GATES]

RESULT = {}
FREED = []
_freed = {"act": 0, "dve": 0}
for _kind, _j in USED:
    _per = TOKEN_UNITS.get(_kind, 1)
    if _j % _per:
        continue
    RESULT[_kind, _j // _per] = len(FREED)
    if _kind == "fk" and _j:
        continue
    for _ in range(TT if _kind in TOKEN_UNITS or _kind == "fk" else 2 if _kind in PAIRS else 1):
        _by = "dve" if _kind in BY_DVE or (_kind, _j) == ("wo", 8) else "act"
        _freed[_by] += 1
        FREED.append((_by, _freed[_by]))

def to_split(k):
    if k < KT - 1:
        return [k + 1]
    return [KT, KT + 1, KT + 2] if k == KT - 1 else [k + AHEAD] if k + AHEAD < len(USED) else []


F_LAST = STEP["f", 7]


def gates_in(step):
    return [j for j in (2 * (step - F_LAST), 2 * (step - F_LAST) + 1) if j in range(HEADS)]


LEVELS = [32, 16, 8, 4, 2, 1, 0]
NL = len(LEVELS)
LEVEL_AT = {u: m for m, u in enumerate([u for u in USED if u[0] in ("u", "gp", "pw", "i")])}
assert len(LEVEL_AT) == 4 * NL
HEAD_AT = {u: n for n, u in enumerate([("gh", j) for j in range(8)] + [("wo", 0)])}


SLOT0 = STEP["av", 0]
SPARSE = TT * 4
SCORES_AT = {t: [] for t in range(-8, 200)}
for _s in range(2 * SPARSE):
    SCORES_AT[(1, 9, 19, 27)[_s // 4] + _s % 4 if _s < SPARSE else 38 + (_s - SPARSE) // 2].append(_s)
SLOT_OF = {_s: _t for _t, _l in SCORES_AT.items() for _s in _l}
TURN_AT = {t: SCORES_AT.get(t - 1, []) for t in range(-7, 200)}
SUM_AT = {t: SCORES_AT.get(t - 2, []) for t in range(-6, 200)}
UP_AT = {SLOT_OF[4 * q + 3] + 3: q for q in range(TT)}
BANK2 = []
for _t in range(0, 60):
    BANK2 += [("turn", _s) for _s in TURN_AT[_t]] + ([("up", UP_AT[_t])] if _t in UP_AT else [])
ROUNDS = 128 // 8
TOPK_STEPS = [3, 3, 3, 0, 2, 2, 1, 1, 1, 1, 1, 1] + 15 * [2]
MIXED_AT = {6 + g: g for g in range(4)}
FORGET_AT, CUM_AT = 34, 36


FINAL = [("a", j) for j in range(4)] + [("c", j) for j in range(4)] + [("b", j) for j in range(4)] + \
    [("d", j) for j in range(4)]
D_FINAL_AT = SLOT0 + max(t for t, l in SUM_AT.items() if l) + 1


TOGETHER = {("wo", 15): 2, ("bs", 2): 3, ("w2", 7): 2}
EARLIER = {(kind, j - i) for (kind, j), n in TOGETHER.items() for i in range(1, n)}


def finals_at(k):
    return 4 if k == D_FINAL_AT else int(k > 0 and USED[k - 1][0] in ("az", "bz", "cz"))


def topk_rounds(slot):
    if slot not in range(len(TOPK_STEPS)):
        return []
    first = sum(TOPK_STEPS[:slot])
    return [(1 + i // ROUNDS, i % ROUNDS) for i in range(first, min(first + TOPK_STEPS[slot], 3 * ROUNDS))]


DIFF_BY_DVE = (0, 3, 8, 18, 19)


def pair_levels(m):
    return m + 1 - (m + 1) // NL


PAR = {}
_at = 0
for _name, _n in (("c", 8), ("ada_b", 16), ("pre_w", 8), ("pool_scale", 8), ("lb", 8), ("nw", 1),
                  ("conv_w", 12)):
    PAR[_name] = slice(_at, _at + _n)
    _at += _n
NPAR = _at


def program(nc, dram, out):
    f32, f32r, bf16, i32 = mybir.dt.float32, mybir.dt.float32r, mybir.dt.bfloat16, mybir.dt.int32
    ALU, ACT, AX = mybir.AluOpType, mybir.ActivationFunctionType, mybir.AxisListType
    with ExitStack() as ctx:
        top = [16512]

        def at(name, offset, shape, dt=f32):
            return nc.alloc_sbuf_tensor_at(name, shape, dt, offset=offset)

        def take(nbytes):
            top[0] += nbytes
            return top[0] - nbytes

        def fixed(name, shape, dt=f32):
            nbytes = int(np.prod(shape[1:])) * (2 if dt == bf16 else 4)
            return at(name, take(-(-nbytes // 32) * 32), shape, dt)

        ident = fixed("ident", [P, P])
        ones = fixed("ones", [P, P])
        R_0 = take(4096)
        level_mask = at("level_mask", R_0, [P, NL, C], i32)
        chunk_keep = at("chunk_keep", R_0 + 1792, [P, S])
        inv_count = at("inv_count", R_0 + 3840, [P, 16])
        ident16 = fixed("ident16", [P, P], bf16)
        causal16 = fixed("causal16", [P, P], bf16)
        pick = fixed("pick", [36, 8], f32r)
        par = fixed("par", [P, NPAR])
        small = fixed("small", [P, 384])
        R_GP = take(4096)
        gate_post = at("gate_post", R_GP, [P, D])
        raw = fixed("raw", [P, RING, U])
        w_hi = fixed("w_hi", [P, SPLITS, U], f32r)
        w_lo = fixed("w_lo", [P, SPLITS, U], f32r)
        R_HT = take(32768)
        R_B, R_K, R_Q, R_V, R_MP = (take(16384) for _ in range(5))
        R_G = take(4096)
        R_X = take(8192)
        R_ATT = take(8192)
        R_H = top[0]
        assert R_H + 11776 <= nc.sbuf_usable_end, (R_H, nc.sbuf_usable_end)

        silu_c, ss, rstd, mod, scale_a, low_b, one_low, tmp8 = (
            small[:, a:a + n] for a, n in ((0, 8), (8, 8), (16, 8), (24, 16), (40, 8), (48, 8), (56, 8), (64, 8)))
        b_end = small[:, 72:88].rearrange("p (s c) -> p s c", s=2)
        ss_y, rstd_y = small[:, 88:100], small[:, 100:104]

        _c = [104]

        def cols(n):
            _c[0] += n
            assert _c[0] <= 384
            return small[:, _c[0] - n:_c[0]]

        ss_h, rstd_h, ss_kv, rstd_kv, ss_o, rstd_o = (cols(n) for n in (4, 4, 4, 4, 8, 8))
        top_max, top_neg, row_sum, row_inv = cols(32), cols(32), cols(32), cols(32)
        bn, bn_mean, rstd_v, cum_q, idx_w, top8, bf_col, pick_f, forget_tok = (
            cols(n) for n in (24, 8, 4, 16, 16, 8, 1, 8, 16))

        x_in = at("x_in", R_V, [P, TT, D])
        ada_acc = at("ada_acc", R_MP, [P, 2, 2, 2 * P])
        x_diag = at("x_diag", R_MP + 4096, [P, TT, P])
        hT_full = at("hT_full", R_Q, [P, KT, S])
        hT_hi = at("hT_hi", R_HT, [P, KT, S], f32r)
        hT_lo = at("hT_lo", R_HT + 16384, [P, KT, S], f32r)
        junk = at("junk", R_X, [P, D])
        idx = at("idx", R_X + 4096, [P, 2, C], i32)
        later = at("later", R_X + 4608, [P, C])
        b_cum = at("b_cum", R_B, [P, HEADS, S])
        keys = at("keys", R_K, [P, HEADS, S])
        queries = at("queries", R_Q, [P, HEADS, S])
        values = at("values", R_V, [P, TT, D])
        attn = at("attn", R_ATT, [P, HEADS, S // 2])
        xq = at("xq", R_X, [P, 2, 2 * S])
        u_pad = at("u_pad", R_V, [P, 2, 16 + S])
        sums = [at("sums0", R_V + 4224, [P, 2, 16 + S]), at("sums1", R_V + 8448, [P, 2, 16 + S])]
        d_hi = at("d_hi", R_H, [P, 2, S], f32r)
        d_lo = at("d_lo", R_H + 4096, [P, 2, S], f32r)
        silu_out = at("silu_out", R_G, [P, 2, S])
        silu_e = at("silu_e", R_0 + 1792, [P, S])
        mix_pool = at("mix_pool", R_MP, [P, KT, S])
        e_b = at("e_b", R_X, [P, S])
        k_dec = at("k_dec", R_X + 2048, [P, S])
        k_decT = at("k_decT", R_X + 4096, [P, TT, P])
        q_dec = at("q_dec", R_H, [P, 2, S])
        o_sb = at("o_sb", R_H + 4096, [P, S])
        o_sq = at("o_sq", R_H + 6144, [P, S])
        states = at("states", R_H + 8192, [P, NC - 1, P])
        mixh_hi = at("mixh_hi", R_B, [P, HEADS, S], f32r)
        mixh_lo = at("mixh_lo", R_K, [P, HEADS, S], f32r)
        mixp_hi = at("mixp_hi", R_Q, [P, KT, S], f32r)
        mixp_lo = at("mixp_lo", R_MP, [P, KT, S], f32r)
        y_left = at("y_left", R_ATT, [P, TT, S])
        x_again = at("x_again", R_V, [P, TT, D])
        x2 = at("x2", R_B, [P, TT, D])
        gate_row = at("gate_row", R_HT + 16384, [P, D])
        post_row = at("post_row", R_HT + 20480, [P, D])
        kv_row = at("kv_row", R_H + 8192, [P, P])
        norm_row = at("norm_row", R_H, [P, D])
        x2_gain = at("x2_gain", R_Q, [P, TT, D])
        y_squares = at("y_squares", R_X, [P, TT, S])
        x2_squares = at("x2_squares", R_MP, [P, D])
        diag = at("diag", R_H + 4096, [P, TT, P])
        M = R_G
        side_tok = at("side_tok", M, [P, TT, SIDE])
        lat_q = at("lat_q", M + 8192, [P, 4, S])
        probs = at("probs", M + 16384, [P, 2, S])
        probsT = at("probsT", M + 20480, [P, 2, S])
        latT = at("latT", M + 24576, [P, S])
        lat = at("lat", M + 26624, [P, TT, P])
        lat_out = at("lat_out", M + 28672, [P, S])
        sel16 = at("sel16", M + 30720, [P, 9 * P], bf16)
        sel_of = {t: sel16[:, s0 * P:(s0 + t + 1) * P] for t, s0 in ((1, 0), (2, 2), (3, 5))}
        w_up = at("w_up", R_GP, [P, 2, 4, P])
        idx_qT = at("idx_qT", R_MP, [P, 2, S])
        idx_kT = at("idx_kT", R_MP + 4096, [P, S])
        score = at("score", R_MP + 6144, [P, 3, S])
        relu = at("relu", R_MP + 12288, [P, 2, S])
        key_twice = at("key_twice", R_MP + 14336, [P, TT, P])
        v_norm = at("v_norm", R_V, [P, TT, S])
        ln_rows = at("ln_rows", R_V + 8192, [P, 2, S])
        mixT = at("mixT", R_V + 12288, [P, 4, P])
        mix_b = at("mix_b", R_V + 14336, [P, 4, P])
        c_gate = at("c_gate", R_MP, [P, S])
        conv_in = at("conv_in", R_MP + 2048, [P, 2 + S])
        conv = at("conv", R_MP + 12288, [P, S])
        fox_q, fox_k = at("fox_q", M, [P, 4, S]), at("fox_k", M + 8192, [P, 4, S])
        fox_v = at("fox_v", R_MP + 8192, [P, TT, S])
        forget = at("forget", M + 24576, [4, 2, S])
        forget_r = at("forget_r", R_GP, [36, S], f32r)
        z_d = at("z_d", M + 24576, [P, 4, S])
        silu_e2 = at("silu_e2", R_0, [P, S])
        y_tmp = at("y_tmp", R_0 + 2048, [P, S])
        y_tmp2 = at("mixed", R_MP + 14336, [P, S])[:, :]
        y_hi = {n: at(f"y{n}_hi", r, [P, 4, S], f32r) for n, r in zip("abcd", (R_K, R_Q, R_V, R_MP))}
        y_lo = {n: at(f"y{n}_lo", r + 8192, [P, 4, S], f32r) for n, r in zip("abcd", (R_K, R_Q, R_V, R_MP))}
        y_raw = {n: at(f"y{n}_raw", r, [P, 4, S]) for n, r in zip("abcd", (R_K, R_Q, R_V, R_MP))}
        sig = at("sig", R_GP, [P, 2, S])
        merged = at("merged", R_0, [P, S])
        merged_part = at("merged_part", R_0 + 2048, [P, S])
        m_hi, m_lo = at("m_hi", M, [P, KT, S], f32r), at("m_lo", M + 16384, [P, KT, S], f32r)
        h_squares = at("h_squares", R_Q, [P, TT, S])
        final_row = at("final_row", R_K, [P, D])
        assert M + 33024 <= nc.sbuf_usable_end, (M, nc.sbuf_usable_end)

        acc = [ctx.enter_context(nc.psum_tensor(f"acc{n}", [P, S], f32)) for n in range(4)]
        side = [ctx.enter_context(nc.psum_tensor(f"side{n}", [P, S], f32)) for n in range(4)]

        def sem(name):
            return ctx.enter_context(nc.semaphore(name))

        raw_in = [sem(f"raw_in{n}") for n in range(RING)]
        x_here = [sem(f"x_here{t}") for t in range(TT)]
        par_here, rows_here, x_again_here = sem("par_here"), sem("rows_here"), sem("x_again_here")
        norm_here = sem("norm_here")
        stored = sem("stored")
        hi_made, lo_made = sem("hi_made"), sem("lo_made")
        ada_summed = sem("ada_summed")
        unit_used = sem("unit_used")
        freed = {"act": sem("freed_act"), "dve": sem("freed_dve")}
        act_chain, dve_chain, pool_chain = sem("act_chain"), sem("dve_chain"), sem("pool_chain")
        consts = sem("consts")
        c_exp, lb_exp, lb_diff = sem("c_exp"), sem("lb_exp"), sem("lb_diff")
        x_rstd, x_diag_made, xT_made, xT_copied = sem("x_rstd"), sem("x_diag_made"), sem("xT_made"), sem("xT_copied")
        mod_summed, h_full, h_hi, h_lo = sem("mod_summed"), sem("h_full"), sem("h_hi"), sem("h_lo")
        xT_taken = sem("xT_taken")
        side_f_read = sem("side_f_read")
        f_made, log_made, b_made = sem("f_made"), sem("log_made"), sem("b_made")
        sum_made, d_made, d_hi_made, d_lo_made = sem("sum_made"), sem("d_made"), sem("d_hi_made"), sem("d_lo_made")
        silu_exp, silu_bound, silu_sig = sem("silu_exp"), sem("silu_bound"), sem("silu_sig")
        f_bound, f_sig = sem("f_bound"), sem("f_sig")
        level_diff, level_exp, level_x = sem("level_diff"), sem("level_exp"), sem("level_x")
        scores_made, level_copied = sem("scores_made"), sem("level_copied")
        decay_diff, decay_exp, prep_made = sem("decay_diff"), sem("decay_exp"), sem("prep_made")
        kT_made, kT_copied, outer_made, states_made = sem("kT_made"), sem("kT_copied"), sem("outer_made"), sem("states_made")
        even_made = sem("even_made")
        o_made, o_squared, ms_made, o_rstd = sem("o_made"), sem("o_squared"), sem("ms_made"), sem("o_rstd")
        o_final, mixh_hi_made, mixh_made = sem("o_final"), sem("mixh_hi_made"), sem("mixh_made")
        mixp_hi_made, mixp_made = sem("mixp_hi_made"), sem("mixp_made")
        gate_summed, gate_made = sem("gate_summed"), sem("gate_made")
        y_squared, y_bias_made, y_rstd, x2_made = sem("y_squared"), sem("y_bias_made"), sem("y_rstd"), sem("x2_made")
        y_tiles_made, out_tiles_made = sem("y_tiles_made"), sem("out_tiles_made")

        x2_rstd, gain_made, diag_made, x2T_made, h2_hi_made, h2_made = (
            sem(n) for n in ("x2_rstd", "gain_made", "diag_made", "x2T_made", "h2_hi_made", "h2_made"))
        small_rows, up_here, spatial_here, masked = sem("small_rows"), sem("up_here"), sem("spatial_here"), sem("masked")
        lat_rstd, lat_made, idxT_made, idxT_copied = sem("lat_rstd"), sem("lat_made"), sem("idxT_made"), sem("idxT_copied")
        dots_made, relu_made, cut_made = sem("dots_made"), sem("relu_made"), sem("cut_made")
        relu_used, sel_made = sem("relu_used"), sem("sel_made")
        latq_made, latq_copied = sem("latq_made"), sem("latq_copied")
        logits_made, max_made, exp_made, probs_made = sem("logits_made"), sem("max_made"), sem("exp_made"), sem("probs_made")
        turned, bank2_read, summed, bank3_read = (
            sem(n) for n in ("turned", "bank2_read", "summed", "bank3_read"))
        bn_made, bn_rstd, v_made, mixed_made, mixed_read = (
            sem(n) for n in ("bn_made", "bn_rstd", "v_made", "mixed_made", "mixed_read"))
        conv_freed = sem("conv_freed")
        y_final, y_hi_made, y_made = sem("y_final"), sem("y_hi_made"), sem("y_made")
        fgt_made, fgt_abs, fgt_ln, fgt_sum, fgt_hi, fgt_ready = (
            sem(n) for n in ("fgt_made", "fgt_abs", "fgt_ln", "fgt_sum", "fgt_hi", "fgt_ready"))
        cum_made, cum_read, pick_made = sem("cum_made"), sem("cum_read"), sem("pick_made")
        sig_made, m_sum, m_hi_made, m_made = sem("sig_made"), sem("m_sum"), sem("m_hi_made"), sem("m_made")
        h_sq, h_rstd, left_scaled, left_made, out_made, final_here = (
            sem(n) for n in ("h_sq", "h_rstd", "left_scaled", "left_made", "out_made", "final_here"))

        def wait_freed(eng, result):
            by, n = FREED[result]
            eng.wait_ge(freed[by], n)

        def wait_y(eng, t):
            if t < TT - 1:
                eng.wait_ge(y_tiles_made, t + 1)
            else:
                eng.wait_ge(unit_used, STEP["wo", 15] + 1)

        def gate_e(n):
            return silu_e[:, :] if n < 16 else silu_e2[:, :]

        def level_view(tile, half):
            return tile.rearrange("p (n w) -> p n w", w=2 * half)

        def diff_level(eng, ops, m):
            half = LEVELS[m % NL] if m < 4 * NL else 0
            if not half or (m in DIFF_BY_DVE) != (ops is nc.vector):
                return
            g = m // NL
            if m >= 2:
                eng.wait_ge(scores_made, m - 1)
            if m and ((m - 1) in DIFF_BY_DVE or m in DIFF_BY_DVE):
                eng.wait_ge(level_diff, pair_levels(m - 1))
            x = level_view(xq[:, m % 2, :], half)
            b = level_view(b_cum[:, 2 * g:2 * g + 2, :].rearrange("p h s -> p (h s)"), half)
            middle = b[:, :, half - 1:half].broadcast_to([P, S // half, half])
            ops.tensor_tensor(out=x[:, :, half:], in0=b[:, :, half:], in1=middle, op=ALU.subtract)
            ops.tensor_tensor(out=x[:, :, :half], in0=middle, in1=b[:, :, :half], op=ALU.subtract)\
                .then_inc(level_diff, 1)

        block = ctx.enter_context(nc.Block())

        @block.sync
        def _(sp):
            for t in range(TT):
                sp.dma_start(x_in[:, t, :], dram["x"][t * P:(t + 1) * P, :]).then_inc(x_here[t], 16)
            for n, (kind, j) in enumerate(ORDER):
                if n >= RING:
                    last = ORDER[n - RING]
                    if last[0] in ADA:
                        sp.wait_ge(ada_summed, last[1] + 1 + 16 * (last[0] == "gate_ada"))
                    else:
                        sp.wait_ge(lo_made, STEP[last] + 1)
                if kind == "gate_ada":
                    src = dram["ada_w"][j * P:(j + 1) * P, 2 * D:3 * D]
                else:
                    src = dram[kind][j, :, :]
                width = WIDTH.get(kind, U)
                sp.dma_start(raw[:, n % RING, 0:width], src).then_inc(raw_in[n % RING], 16)
            out_tiles = out.rearrange("(t p) d -> p t d", p=P)
            for t in range(TT):
                sp.wait_ge(left_made, t + 1)
                sp.wait_ge(out_made, t + 1)
                sp.dma_start(out_tiles[:, t, :], x2[:, t, :]).then_inc(stored, 16)
            sp.wait_ge(stored, 16 * TT)

        @block.gpsimd
        def _(pool):
            done = [0]

            def then(ins):
                done[0] += 1
                ins.then_inc(pool_chain, 1)
                pool.wait_ge(pool_chain, done[0])

            then(nc.gpsimd.memset(ident[:, :], 0.0))
            nc.gpsimd.affine_select(out=ident[:, :], in_=ident[:, :], compare_op=ALU.not_equal, fill=1.0, base=0,
                                    pattern=[[-1, P]], channel_multiplier=1).then_inc(consts, 1)
            nc.gpsimd.memset(ones[:, :], 1.0).then_inc(consts, 1)
            nc.gpsimd.iota(idx[:, 0, :], pattern=[[1, C]], base=0, channel_multiplier=0).then_inc(consts, 1)
            nc.gpsimd.iota(idx[:, 1, :], pattern=[[0, C]], base=0, channel_multiplier=1).then_inc(consts, 1)
            then(nc.gpsimd.memset(chunk_keep[:, :], 1.0))
            nc.gpsimd.memset(chunk_keep[:, :].rearrange("p (c t) -> p c t", t=C)[:, :, 0:1], 0.0).then_inc(consts, 1)
            nc.gpsimd.memset(attn[:, :, :], 0.0).then_inc(consts, 1)
            then(nc.gpsimd.memset(causal16[:, :], 0.0))
            nc.gpsimd.affine_select(out=causal16[:, :], in_=causal16[:, :], compare_op=ALU.is_ge, fill=NEG, base=0,
                                    pattern=[[-1, P]], channel_multiplier=1).then_inc(consts, 1)
            then(nc.gpsimd.memset(pick_f[0:36, :], 0.0))
            for base in (0, -32):
                then(nc.gpsimd.affine_select(out=pick_f[0:36, 0:4], in_=pick_f[0:36, 0:4], compare_op=ALU.not_equal,
                                             fill=1.0, base=base, pattern=[[-1, 4]], channel_multiplier=1))
            nc.gpsimd.memset(pick_f[0:36, 4:8], 0.0).then_inc(consts, 1)
            pool.dma_start(bf_col[0:4, :], dram["b_f"]).then_inc(small_rows, 16)
            for k in range(KT):
                n = UNIT["fk", k]
                pool.wait_ge(hi_made, k + 1)
                nc.gpsimd.tensor_tensor(out=w_lo[:, k % SPLITS, 0:7 * P], in0=raw[:, n % RING, 0:7 * P],
                                        in1=w_hi[:, k % SPLITS, 0:7 * P].bitcast(f32), op=ALU.subtract)\
                    .then_inc(lo_made, 1)
            pool.wait_ge(h_lo, KT)
            then(nc.gpsimd.memset(u_pad[:, :, 0:16], 0.0))
            pool.wait_ge(b_made, HEADS)
            for m in range(4 * NL):
                diff_level(pool, nc.gpsimd, m)
                if (m - 2) % 5 or m > 17:
                    continue
                g = m // 5
                wait_freed(pool, RESULT["u", 2 * g + 1])
                if g:
                    pool.wait_ge(d_lo_made, g)
                src, reach = u_pad, 0
                for r in range(g + 1):
                    dst, shift = sums[r % 2], 1 << r
                    reach += shift
                    ins = nc.gpsimd.tensor_tensor(out=dst[:, :, reach:], in0=src[:, :, reach:],
                                                  in1=src[:, :, reach - shift:16 + S - shift], op=ALU.add)
                    if r < g:
                        then(ins)
                    else:
                        ins.then_inc(sum_made, 1)
                    src = dst
            pool.wait_ge(unit_used, STEP["gh", 7] + 1)
            pool.dma_start(gate_row[:, :], dram["gate_b"].partition_broadcast(P)).then_inc(rows_here, 16)
            pool.dma_start(post_row[:, :], dram["post_w"].partition_broadcast(P)).then_inc(rows_here, 16)
            pool.wait_ge(o_made, HEADS)
            pool.dma_start(kv_row[:, :], dram["kv_g"].partition_broadcast(P)).then_inc(small_rows, 16)
            pool.dma_start(norm_row[:, :], dram["norm_g"].partition_broadcast(P)).then_inc(norm_here, 16)
            pool.dma_start(x_again[:, :, :], dram["x"].rearrange("(t p) d -> p t d", p=P)).then_inc(x_again_here, 16)
            pool.wait_ge(x2_made, TT)
            for o, name in enumerate(("w_uk", "w_uv")):
                pool.dma_start(w_up[:, o, :, :], dram[name]).then_inc(up_here, 16)
            pool.dma_start(ln_rows[:, 0, :], dram["ln_g"].partition_broadcast(P)).then_inc(spatial_here, 16)
            pool.dma_start(ln_rows[:, 1, :], dram["ln_b"].partition_broadcast(P)).then_inc(spatial_here, 16)
            pool.dma_start(mix_b[:, :, :].rearrange("p g t -> p (g t)"), dram["b_s"].partition_broadcast(P))\
                .then_inc(spatial_here, 16)
            pool.dma_start(mixT[:, :, :], dram["w_s"]).then_inc(spatial_here, 16)
            pool.wait_ge(spatial_here, 64)
            nc.gpsimd.affine_select(out=mixT[:, :, :], in_=mixT[:, :, :], compare_op=ALU.is_ge, fill=0.0, base=0,
                                    pattern=[[0, 4], [1, P]], channel_multiplier=-1).then_inc(masked, 1)
            for t in range(1, TT):
                pool.wait_ge(relu_used, 4 * t)
                diagonal = score[:, t - 1, t * P:(t + 1) * P]
                nc.gpsimd.affine_select(out=diagonal, in_=diagonal, compare_op=ALU.is_ge, fill=OUTSIDE, base=0,
                                        pattern=[[-1, P]], channel_multiplier=1).then_inc(cut_made, 1)
            pool.wait_ge(unit_used, STEP["br", 2 * KT - 1] + 1)
            pool.dma_start(final_row[:, :], dram["final_g"].partition_broadcast(P)).then_inc(final_here, 16)

        @block.scalar
        def _(act):
            done = [0]

            def then(ins):
                done[0] += 1
                ins.then_inc(act_chain, 1)
                act.wait_ge(act_chain, done[0])

            def split_hi(k):
                kind, j = USED[k]
                n, width = UNIT[kind, j], WIDTH.get(kind, U)
                act.wait_ge(raw_in[n % RING], 16 * (n // RING + 1))
                if k >= SPLITS:
                    act.wait_ge(unit_used, k - SPLITS + 1)
                nc.scalar.activation(w_hi[:, k % SPLITS, 0:width], raw[:, n % RING, 0:width], ACT.Copy)\
                    .then_inc(hi_made, 1)

            def exp_level(m):
                if m < 4 * NL and LEVELS[m % NL]:
                    act.wait_ge(level_diff, pair_levels(m))
                    nc.scalar.activation(xq[:, m % 2, :], xq[:, m % 2, :], ACT.Exp).then_inc(level_exp, 1)

            def exp_decays(n):
                act.wait_ge(decay_diff, n + 1)
                nc.scalar.activation(e_b[:, :], b_cum[:, n, :], ACT.Exp).then_inc(decay_exp, 1)
                nc.scalar.activation(k_dec[:, :], k_dec[:, :], ACT.Exp).then_inc(decay_exp, 1)

            act.preload_act_table_set("natural_log_exp_and_others")
            act.dma_start(par[:, :], dram["par"]).then_inc(par_here, 16)
            act.wait_ge(par_here, 16)
            nc.scalar.activation(tmp8, par[:, PAR["c"]], ACT.Exp, scale=-1.0).then_inc(c_exp, 1)
            for t in range(TT):
                act.wait_ge(x_here[t], 16)
                then(nc.scalar.activation(junk[:, :], x_in[:, t, :], ACT.Square, accum_out=ss[:, t:t + 1]))
                then(nc.scalar.activation(rstd[:, t:t + 1], ss[:, t:t + 1], ACT.Ln, scale=1.0 / D, bias=EPS))
                nc.scalar.activation(rstd[:, t:t + 1], rstd[:, t:t + 1], ACT.Exp, scale=-0.5).then_inc(x_rstd, 1)
            act.wait_ge(lb_diff, 1)
            nc.scalar.activation(one_low, low_b, ACT.Exp).then_inc(lb_exp, 1)
            for kt in (7, 0, 1, 2):
                act.wait_ge(xT_made, kt + 1)
                nc.scalar.activation(hT_full[:, kt, :], (acc + side)[kt][:, :], ACT.Copy).then_inc(xT_copied, 1)

            def upper_h(kt):
                act.wait_ge(h_full, kt + 1)
                nc.scalar.activation(hT_hi[:, kt, :], hT_full[:, kt, :], ACT.Copy).then_inc(h_hi, 1)

            split_hi(0)
            upper_h(0)

            def copy_out(dst, result, by, **more):
                nc.scalar.activation(dst, acc[result % 4][:, :], ACT.Copy, **more).then_inc(by, 1)

            def enter_second_block():
                def square_y(t):
                    wait_y(act, t)
                    nc.scalar.activation(y_squares[:, t, :], acc[(RESULT["wo", 1] + t) % 4][:, :], ACT.Square,
                                         accum_out=ss_y[:, 4 + t:5 + t]).then_inc(y_squared, 1)

                def rstd_of_y(t):
                    act.wait_ge(y_squared, t + 1)
                    then(nc.scalar.activation(rstd_y[:, t:t + 1], ss_y[:, 4 + t:5 + t], ACT.Ln, scale=1.0 / D,
                                              bias=ss_y[:, 8 + t:9 + t]))
                    nc.scalar.activation(rstd_y[:, t:t + 1], rstd_y[:, t:t + 1], ACT.Exp, scale=-0.5).then_inc(y_rstd, 1)

                def rstd_of_x2(t):
                    act.wait_ge(x2_made, t + 1)
                    then(nc.scalar.activation(x2_squares[:, :], x2[:, t, :], ACT.Square, accum_out=ss_h[:, t:t + 1]))
                    then(nc.scalar.activation(rstd_h[:, t:t + 1], ss_h[:, t:t + 1], ACT.Ln, scale=1.0 / D, bias=EPS))
                    nc.scalar.activation(rstd_h[:, t:t + 1], rstd_h[:, t:t + 1], ACT.Exp, scale=-0.5).then_inc(x2_rstd, 1)

                def upper_h2(t):
                    for n in (2 * t, 2 * t + 1):
                        act.wait_ge(x2T_made, n + 1)
                        half = n % 2
                        nc.scalar.activation(hT_hi[:, 4 * half:4 * half + 4, t * P:(t + 1) * P],
                                             side[n % 4][:, :].rearrange("p (k s) -> p k s", s=P), ACT.Copy)\
                            .then_inc(h2_hi_made, 1)

                act.wait_ge(y_bias_made, 1)
                wait_freed(act, RESULT["wo", 0] + TT - 1)
                square_y(0)
                rstd_of_y(0)
                square_y(1)
                rstd_of_y(1)
                rstd_of_x2(0)
                square_y(2)
                rstd_of_y(2)
                rstd_of_x2(1)
                square_y(3)
                upper_h2(0)
                rstd_of_y(3)
                split_hi(STEP["bs", 2])
                rstd_of_x2(2)
                upper_h2(1)
                rstd_of_x2(3)
                upper_h2(2)
                upper_h2(3)

            def side_slot(slot):
                for s in TURN_AT.get(slot, []):
                    n, w = BANK2.index(("turn", s)), (s // 4 % TT + 1) * P
                    act.wait_ge(turned, n + 1)
                    if s >= 2:
                        act.wait_ge(summed, s - 1)
                    nc.scalar.activation(probsT[:, s % 2, 0:w], side[2][:, 0:w], ACT.Copy).then_inc(bank2_read, 1)
                for s in SUM_AT.get(slot, []):
                    if s % 4 == 3:
                        q = s // 4
                        act.wait_ge(summed, s + 1)
                        if s < SPARSE:
                            if q:
                                act.wait_ge(turned, BANK2.index(("up", q - 1)) + 1)
                            nc.scalar.activation(lat_out[:, :], side[3][:, :], ACT.Copy).then_inc(bank3_read, 1)
                        else:
                            tok = slice((q % TT) * P, (q % TT + 1) * P)
                            nc.scalar.activation(y_raw["d"][:, :, tok], side[3][:, :].rearrange("p (h s) -> p h s", s=P),
                                                 ACT.Copy).then_inc(bank3_read, 1)
                if slot in UP_AT:
                    q = UP_AT[slot]
                    n = BANK2.index(("up", q))
                    act.wait_ge(turned, n + 1)
                    nc.scalar.activation(y_raw["b"][:, :, q * P:(q + 1) * P],
                                         side[2][:, :].rearrange("p (h s) -> p h s", s=P), ACT.Copy).then_inc(bank2_read, 1)
                for s in SCORES_AT.get(slot, []):
                    w = (s // 4 % TT + 1) * P
                    act.wait_ge(max_made, s + 1)
                    if s >= 2:
                        act.wait_ge(turned, BANK2.index(("turn", s - 2)) + 1)
                    nc.scalar.activation(probs[:, s % 2, 0:w], side[s % 2][:, 0:w], ACT.Exp, bias=top_neg[:, s:s + 1],
                                         accum_out=row_sum[:, s:s + 1]).then_inc(exp_made, 1)

            def gate_sigmoid(n):
                act.wait_ge(silu_bound, n + 1)
                then(nc.scalar.activation(gate_e(n), gate_e(n), ACT.Ln))
                nc.scalar.activation(gate_e(n), gate_e(n), ACT.Exp, scale=-1.0).then_inc(silu_sig, 1)

            gates = 0
            finals = [0]
            before = None
            for k, (kind, j) in enumerate(USED):
                if k + 1 < KT:
                    upper_h(k + 1)
                if (kind, j) != ("wo", 15):
                    for later_k in to_split(k):
                        split_hi(later_k)
                if before in GATES and (kind, j) != ("wo", 0):
                    gate_sigmoid(gates - 1)
                before = kind
                m = LEVEL_AT.get((kind, j))
                if m is not None:
                    exp_level(m + 1)
                if (kind, j % 2) == ("gp", 1):
                    g = j // 2
                    act.wait_ge(d_made, g + 1)
                    if g:
                        act.wait_ge(unit_used, STEP["pw", g - 1] + 1)
                    nc.scalar.activation(d_hi[:, :, :], sums[(g + 1) % 2][:, :, 0:S], ACT.Copy).then_inc(d_hi_made, 1)
                for h in gates_in(k):
                    act.wait_ge(f_bound, h + 1)
                    then(nc.scalar.activation(b_cum[:, h, :], b_cum[:, h, :], ACT.Ln))
                    nc.scalar.activation(b_cum[:, h, :], b_cum[:, h, :], ACT.Exp, scale=-1.0).then_inc(f_sig, 1)
                for h in gates_in(k - 1):
                    act.wait_ge(f_made, h + 1)
                    nc.scalar.activation(b_cum[:, h, :], b_cum[:, h, :], ACT.Ln).then_inc(log_made, 1)
                if (kind, j) not in EARLIER and (kind, j) not in (("wo", 15), ("w2", 7)) and not k < KT - 1:
                    act.wait_ge(unit_used, k + 1)
                if (kind, j) == ("fk", KT - 1):
                    for h in range(HEADS - 1):
                        nc.scalar.activation(b_cum[:, h, :], (acc + side)[h][:, :], ACT.Exp, scale=-1.0)\
                            .then_inc(freed["act"] if h < 4 else side_f_read, 1)
                if kind == "f":
                    nc.scalar.activation(b_cum[:, j, :], acc[RESULT[kind, j] % 4][:, :], ACT.Exp, scale=-1.0)\
                        .then_inc(freed["act"], 1)
                if kind == "q":
                    nc.scalar.activation(queries[:, j, :], acc[RESULT[kind, j] % 4][:, :], ACT.Copy)\
                        .then_inc(freed["act"], 1)
                    if j == 7:
                        exp_level(0)
                if kind == "u":
                    if j >= 2:
                        act.wait_ge(d_lo_made, j // 2)
                    nc.scalar.activation(u_pad[:, j % 2, 16:], acc[RESULT[kind, j] % 4][:, :], ACT.Copy)\
                        .then_inc(freed["act"], 1)
                n = HEAD_AT.get((kind, j))
                if n is not None and n < HEADS:
                    act.wait_ge(kT_made, n + 1)
                    nc.scalar.activation(k_decT[:, :, :], side[0][:, :].rearrange("p (t k) -> p t k", t=TT), ACT.Copy)\
                        .then_inc(kT_copied, 1)
                if kind in GATES:
                    if gates:
                        wait_freed(act, RESULT[GATE_ORDER[gates - 1]])
                    else:
                        act.wait_ge(b_made, HEADS)
                    nc.scalar.activation(gate_e(gates), acc[RESULT[kind, j] % 4][:, :], ACT.Exp, scale=-1.0)\
                        .then_inc(silu_exp, 1)
                    gates += 1
                    if (kind, j) == ("gh", 7):
                        gate_sigmoid(gates - 1)
                if (kind, j % 4) == ("i", 3):
                    for t in range(TT):
                        r = RESULT["i", j // 4] + t
                        nc.scalar.activation(values[:, t, (j // 4) * S:(j // 4 + 1) * S], acc[r % 4][:, :], ACT.Copy)\
                            .then_inc(freed["act"], 1)
                if (kind, j) == ("i", 7):
                    exp_decays(0)
                if n:
                    act.wait_ge(o_made, n)
                    if n >= 2:
                        act.wait_ge(mixh_made, n - 1)
                    nc.scalar.activation(o_sq[:, :], side[3][:, :], ACT.Square)
                    nc.scalar.activation(o_sb[:, :], side[3][:, :], ACT.Copy).then_inc(o_squared, 1)
                if n is not None and n + 1 < HEADS:
                    exp_decays(n + 1)
                if n:
                    act.wait_ge(ms_made, n)
                    then(nc.scalar.activation(o_sq[:, :], side[0][:, :], ACT.Ln, scale=1.0 / P, bias=EPS))
                    nc.scalar.activation(o_sq[:, :], o_sq[:, :], ACT.Exp, scale=-0.5).then_inc(o_rstd, 1)
                    act.wait_ge(o_final, n)
                    nc.scalar.activation(mixh_hi[:, n - 1, :], o_sb[:, :], ACT.Copy).then_inc(mixh_hi_made, 1)
                if kind == "gh":
                    act.wait_ge(prep_made, j + 1)
                    wait_freed(act, RESULT["pw", 3] + 1)
                    nc.scalar.activation(mixp_hi[:, j, :], mix_pool[:, j, :], ACT.Copy).then_inc(mixp_hi_made, 1)
                if (kind, j) == ("wo", 7):
                    for t in range(TT):
                        r = RESULT["wo", 0] + t
                        nc.scalar.activation(y_squares[:, t, :], acc[r % 4][:, :], ACT.Square, accum_out=ss_y[:, t:t + 1])
                        nc.scalar.activation(y_left[:, t, :], acc[r % 4][:, :], ACT.Copy).then_inc(freed["act"], 1)
                if (kind, j) == ("wo", 15):
                    enter_second_block()
                r = RESULT.get((kind, j))
                if (kind, j) == ("bs", 3):
                    for t in range(TT):
                        nc.scalar.activation(side_tok[:, t, :], acc[(RESULT["bs", 0] + t) % 4][:, 0:SIDE], ACT.Copy)\
                            .then_inc(freed["act"], 1)
                    wait_freed(act, RESULT["bs", 0] + 3)
                    for t in range(TT):
                        then(nc.scalar.activation(lat[:, t, :], side_tok[:, t, 0:P], ACT.Square,
                                                  accum_out=ss_kv[:, t:t + 1]))
                    then(nc.scalar.activation(rstd_kv, ss_kv, ACT.Ln, scale=1.0 / P, bias=EPS))
                    nc.scalar.activation(rstd_kv, rstd_kv, ACT.Exp, scale=-0.5).then_inc(lat_rstd, 1)
                if kind == "bq":
                    copy_out(lat_q[:, j, :], r, freed["act"])
                    if j == 0:
                        act.wait_ge(idxT_made, 1)
                        for n, dst in enumerate((latT[:, :], idx_qT[:, 0, :], idx_qT[:, 1, :], idx_kT[:, :])):
                            nc.scalar.activation(dst, side[n][:, :], ACT.Copy).then_inc(idxT_copied, 1)
                    else:
                        for h in range(4):
                            n = 4 * (j - 1) + h
                            act.wait_ge(dots_made, n + 1)
                            if n >= 2:
                                act.wait_ge(relu_used, n - 1)
                            w = (j + 1) * P
                            nc.scalar.activation(relu[:, n % 2, 0:w], side[h][:, 0:w], ACT.Relu, scale=0.125)\
                                .then_inc(relu_made, 1)
                if (kind, j) == ("av", 0):
                    act.wait_ge(latq_made, 1)
                    for h in range(4):
                        nc.scalar.activation(lat_q[:, h, :], side[h][:, :], ACT.Copy, scale=float(P) ** -0.5)\
                            .then_inc(latq_copied, 1)
                if (kind, j) == ("av", 3):
                    act.wait_ge(spatial_here, 64)
                    for t in range(TT):
                        copy_out(v_norm[:, t, :], RESULT["av", 0] + t, freed["act"])
                    act.wait_ge(bn_made, 1)
                    then(nc.scalar.activation(rstd_v, bn_mean.rearrange("p (t m) -> p t m", m=2)[:, :, 1], ACT.Ln, bias=EPS))
                    nc.scalar.activation(rstd_v, rstd_v, ACT.Exp, scale=-0.5).then_inc(bn_rstd, 1)
                if kind == "au":
                    copy_out(y_raw["a"][:, j, :], r, freed["act"])
                if kind == "cc":
                    if j:
                        wait_freed(act, RESULT["cx", j - 1])
                    copy_out(c_gate[:, :], r, freed["act"])
                if kind == "dq":
                    copy_out(fox_q[:, j, :], r, freed["act"], scale=float(P) ** -0.5)
                if kind == "dk":
                    copy_out(fox_k[:, j, :], r, freed["act"])
                if (kind, j) == ("dv", 3):
                    for t in range(TT):
                        copy_out(fox_v[:, t, :], RESULT["dv", 0] + t, freed["act"])
                for _ in range(finals_at(k)):
                    act.wait_ge(y_final, finals[0] + 1)
                    name, kt = FINAL[finals[0]]
                    nc.scalar.activation(y_hi[name][:, kt, :], y_tmp[:, :], ACT.Copy).then_inc(y_hi_made, 1)
                    finals[0] += 1
                slot = k - SLOT0
                side_slot(slot)
                if slot == FORGET_AT:
                    act.wait_ge(fgt_abs, 1)
                    then(nc.scalar.activation(forget[:, 1, :], forget[:, 1, :], ACT.Exp, scale=-1.0))
                    nc.scalar.activation(forget[:, 1, :], forget[:, 1, :], ACT.Ln, bias=1.0).then_inc(fgt_ln, 1)
                    act.wait_ge(fgt_sum, 1)
                    nc.scalar.activation(forget_r[0:4, :], forget[:, 0, :], ACT.Copy, scale=-1.0).then_inc(fgt_hi, 1)
                if kind == "ga":
                    if j >= 2:
                        wait_freed(act, RESULT["br", (j - 2) // 2] + j % 2)
                    nc.scalar.activation(sig[:, j % 2, :], acc[r % 4][:, :], ACT.Sigmoid).then_inc(freed["act"], 1)
                if kind == "br" and j % 2:
                    act.wait_ge(m_sum, j // 2 + 1)
                    nc.scalar.activation(m_hi[:, j // 2, :], merged[:, :], ACT.Copy).then_inc(m_hi_made, 1)
                if (kind, j) == ("w2", 0):
                    act.preload_act_table_set("natural_log_exp_and_others")
                if (kind, j) == ("w2", 3):
                    for t in range(TT):
                        wait_freed(act, RESULT["w2", 0] + t)
                        nc.scalar.activation(h_squares[:, t, :], x2[:, t, 0:S], ACT.Square, accum_out=ss_o[:, t:t + 1])\
                            .then_inc(h_sq, 1)
                if (kind, j) == ("w2", 7):
                    act.wait_ge(left_scaled, 1)
                    for t in range(TT):
                        wait_freed(act, RESULT["w2", 1] + t)
                        then(nc.scalar.activation(h_squares[:, t, :], x2[:, t, S:D], ACT.Square,
                                                  accum_out=ss_o[:, 4 + t:5 + t]))
                        then(nc.scalar.activation(rstd_o[:, t:t + 1], ss_o[:, 4 + t:5 + t], ACT.Ln, scale=1.0 / D,
                                                  bias=rstd_o[:, 4 + t:5 + t]))
                        nc.scalar.activation(rstd_o[:, t:t + 1], rstd_o[:, t:t + 1], ACT.Exp, scale=-0.5)\
                            .then_inc(h_rstd, 1)
                        act.wait_ge(h_rstd, t + 1)
                        nc.scalar.activation(x2[:, t, 0:S], x2[:, t, 0:S], ACT.Copy, scale=rstd_o[:, t:t + 1])\
                            .then_inc(left_made, 1)

        @block.vector
        def _(dve):
            done = [0]

            def then(ins):
                done[0] += 1
                ins.then_inc(dve_chain, 1)
                dve.wait_ge(dve_chain, done[0])

            def add_ada(kind, j):
                n = UNIT[kind, j]
                dve.wait_ge(raw_in[n % RING], 16 * (n // RING + 1))
                if j:
                    dve.wait_ge(ada_summed, 16 + j)
                if j == 0:
                    nc.vector.tensor_scalar(gate_post[:, :], raw[:, n % RING, :], silu_c[:, j:j + 1], None, ALU.mult)\
                        .then_inc(ada_summed, 1)
                else:
                    nc.vector.scalar_tensor_tensor(out=gate_post[:, :], in0=raw[:, n % RING, :], scalar=silu_c[:, j:j + 1],
                                                   in1=gate_post[:, :], op0=ALU.mult, op1=ALU.add).then_inc(ada_summed, 1)

            strips = {}

            def sum_modulation(kt, part):
                for strip in range(4 * part, 4 * part + 4):
                    n = UNIT["ada", 2 * kt + strip // 4]
                    if strip % 4 == 0:
                        dve.wait_ge(raw_in[n % RING], 16 * (n // RING + 1))
                    if strip == 0 and kt >= 2:
                        dve.wait_ge(mod_summed, kt - 1)
                    src = raw[:, n % RING, (strip % 4) * 256:(strip % 4 + 1) * 256]
                    dst, weight = ada_acc[:, kt % 2, strip % 2, :], silu_c[:, strip:strip + 1]
                    if strip < 2:
                        ins = nc.vector.tensor_scalar(dst, src, weight, None, ALU.mult)
                    else:
                        if strip == 5:
                            dve.wait_ge(ada_summed, 2 * kt + 1)
                        else:
                            dve.wait_ge(dve_chain, strips[strip - 2])
                        ins = nc.vector.scalar_tensor_tensor(out=dst, in0=src, scalar=weight, in1=dst,
                                                             op0=ALU.mult, op1=ALU.add)
                    if strip % 4 == 3:
                        ins.then_inc(ada_summed, 1)
                    else:
                        ins.then_inc(dve_chain, 1)
                        done[0] += 1
                        strips[strip] = done[0]

            def modulate(kt):
                shift, scale = mod[:, kt:kt + 1], mod[:, 8 + kt:9 + kt]
                dve.wait_ge(mod_summed, kt + 1)
                ada_b = par[:, PAR["ada_b"]]
                nc.vector.tensor_tensor(out=shift, in0=side[3][:, kt:kt + 1], in1=ada_b[:, kt:kt + 1], op=ALU.add)
                then(nc.vector.tensor_tensor(out=scale, in0=side[3][:, 8 + kt:9 + kt], in1=ada_b[:, 8 + kt:9 + kt],
                                             op=ALU.add))
                then(nc.vector.scalar_tensor_tensor(out=scale_a[:, kt:kt + 1], in0=scale, scalar=1.0,
                                                    in1=par[:, PAR["pre_w"]][:, kt:kt + 1], op0=ALU.add, op1=ALU.mult))
                if kt in range(3, 7):
                    dve.wait_ge(xT_taken, kt - 2)
                else:
                    dve.wait_ge(xT_copied, kt + 2 if kt < 3 else 1)
                nc.vector.tensor_scalar(hT_full[:, kt, :], hT_full[:, kt, :], scale_a[:, kt:kt + 1], shift,
                                        ALU.mult, ALU.add).then_inc(h_full, 1)

            def lower_h(kt):
                dve.wait_ge(h_full, kt + 1)
                dve.wait_ge(h_hi, kt + 1)
                nc.vector.tensor_tensor(out=hT_lo[:, kt, :], in0=hT_full[:, kt, :], in1=hT_hi[:, kt, :].bitcast(f32),
                                        op=ALU.subtract).then_inc(h_lo, 1)

            def split_lo(k):
                kind, j = USED[k]
                n, width = UNIT[kind, j], WIDTH.get(kind, U)
                before = n - 1
                while before >= 0 and ORDER[before][0] == "gate_ada":
                    before -= 1
                for u in ORDER[before + 1:n]:
                    add_ada(*u)
                dve.wait_ge(hi_made, k + 1)
                nc.vector.tensor_tensor(out=w_lo[:, k % SPLITS, 0:width], in0=raw[:, n % RING, 0:width],
                                        in1=w_hi[:, k % SPLITS, 0:width].bitcast(f32), op=ALU.subtract).then_inc(lo_made, 1)

            def scale_level(m):
                half = LEVELS[m % NL]
                if not half:
                    return
                g = m // NL
                dve.wait_ge(level_exp, pair_levels(m))
                x = level_view(xq[:, m % 2, :], half)
                q = level_view(queries[:, 2 * g:2 * g + 2, :].rearrange("p h s -> p (h s)"), half)
                kk = level_view(keys[:, 2 * g:2 * g + 2, :].rearrange("p h s -> p (h s)"), half)
                nc.vector.tensor_tensor(out=x[:, :, half:], in0=x[:, :, half:], in1=q[:, :, half:], op=ALU.mult)
                nc.vector.tensor_tensor(out=x[:, :, :half], in0=x[:, :, :half], in1=kk[:, :, :half], op=ALU.mult)\
                    .then_inc(level_x, 1)

            def copy_level(m):
                dve.wait_ge(scores_made, m + 1)
                g, half = m // NL, LEVELS[m % NL]
                if m:
                    dve.wait_ge(level_copied, m)
                if half:
                    for odd in range(2):
                        rows, part = slice(odd * C, (odd + 1) * C), slice(odd * C // 2, (odd + 1) * C // 2)
                        dst = attn[rows, 2 * g:2 * g + 2, :].rearrange("p h (t n w) -> p (h t) n w", t=TT, w=2 * half)
                        mask = level_view(level_mask[rows, m % NL, :], half)[:, :, half:]
                        src = side[m % 2][rows, :].rearrange("p (t s) -> p t s", s=C)[:, :, part]
                        ins = nc.vector.copy_predicated(
                            dst[:, :, :, half:], mask.unsqueeze(1).broadcast_to([C, 2 * TT, C // (2 * half), half]),
                            src.rearrange("p t (n w) -> p t n w", w=half))
                else:
                    ins = nc.vector.copy_predicated(attn[:, 2 * g:2 * g + 2, :].rearrange("p h (t s) -> p (h t) s", s=C),
                                                    level_mask[:, m % NL, :].unsqueeze(1).broadcast_to([P, 2 * TT, C]),
                                                    side[m % 2][:, :].rearrange("p (n s) -> p n s", s=C))
                ins.then_inc(level_copied, 1)

            def bound_gate(n):
                dve.wait_ge(silu_exp, n + 1)
                nc.vector.tensor_scalar(gate_e(n), gate_e(n), 1.0, 1.0e19, ALU.add, ALU.min).then_inc(silu_bound, 1)

            def finish_gate(n, result, dst):
                dve.wait_ge(silu_sig, n + 1)
                ins = nc.vector.tensor_tensor(out=dst, in0=acc[result % 4][:, :], in1=gate_e(n), op=ALU.mult)
                ins.then_inc(freed["dve"], 1)

            def log_sum(j):
                dve.wait_ge(log_made, j + 1)
                nc.vector.tensor_tensor_scan(out=b_cum[:, j, :], data0=chunk_keep[:, :], data1=b_cum[:, j, :], initial=0.0,
                                             op0=ALU.mult, op1=ALU.add).then_inc(b_made, 1)

            def prepare_head(n):
                b = b_cum[:, n, :].rearrange("p (c t) -> p c t", t=C)
                if n:
                    dve.wait_ge(kT_made, n)
                else:
                    dve.wait_ge(scores_made, 4 * NL)
                nc.vector.tensor_tensor(out=k_dec[:, :].rearrange("p (c t) -> p c t", t=C),
                                        in0=b[:, :, C - 1:C].broadcast_to([P, NC, C]), in1=b, op=ALU.subtract)\
                    .then_inc(decay_diff, 1)
                dve.wait_ge(decay_exp, 2 * n + 1)
                nc.vector.tensor_copy(b_end[:, n % 2, :], e_b[:, :].rearrange("p (c t) -> p c t", t=C)[:, :, C - 1])
                if n >= 2:
                    dve.wait_ge(o_made, n - 1)
                nc.vector.tensor_tensor(out=q_dec[:, n % 2, :], in0=e_b[:, :], in1=queries[:, n, :], op=ALU.mult)
                dve.wait_ge(decay_exp, 2 * n + 2)
                nc.vector.tensor_tensor(out=k_dec[:, :], in0=k_dec[:, :], in1=keys[:, n, :], op=ALU.mult)\
                    .then_inc(prep_made, 1)

            def chain_states(n):
                dve.wait_ge(outer_made, n + 1)
                if n:
                    dve.wait_ge(o_made, n)
                then(nc.vector.tensor_copy(states[:, 0, :], side[1][:, 0:P]))
                for c in range(1, NC - 1):
                    ins = nc.vector.scalar_tensor_tensor(
                        out=states[:, c, :], in0=states[:, c - 1, :], scalar=b_end[:, n % 2, c:c + 1],
                        in1=side[1 + c % 2][:, (c // 2) * P:(c // 2 + 1) * P], op0=ALU.mult, op1=ALU.add)
                    if c < NC - 2:
                        then(ins)
                    else:
                        ins.then_inc(states_made, 1)

            def finish_head(n):
                dve.wait_ge(o_rstd, n + 1)
                then(nc.vector.tensor_tensor(out=o_sb[:, :], in0=o_sb[:, :], in1=o_sq[:, :], op=ALU.mult))
                nc.vector.scalar_tensor_tensor(out=o_sb[:, :], in0=o_sb[:, :], scalar=par[:, PAR["nw"]],
                                               in1=silu_out[:, n % 2, :], op0=ALU.mult, op1=ALU.mult).then_inc(o_final, 1)
                dve.wait_ge(o_final, n + 1)
                dve.wait_ge(mixh_hi_made, n + 1)
                nc.vector.tensor_tensor(out=mixh_lo[:, n, :], in0=o_sb[:, :], in1=mixh_hi[:, n, :].bitcast(f32),
                                        op=ALU.subtract).then_inc(mixh_made, 1)

            def end_tile(gate, raws):
                name, kt = FINAL[finals[0]]
                if finals[0]:
                    dve.wait_ge(y_made, finals[0])
                nc.vector.tensor_tensor(out=y_tmp[:, :], in0=gate, in1=raws[name][:, kt, :], op=ALU.mult).then_inc(y_final, 1)
                finals[0] += 1
                dve.wait_ge(y_final, finals[0])
                dve.wait_ge(y_hi_made, finals[0])
                nc.vector.tensor_tensor(out=y_lo[name][:, kt, :], in0=y_tmp[:, :], in1=y_hi[name][:, kt, :].bitcast(f32),
                                        op=ALU.subtract).then_inc(y_made, 1)

            def enter_second_block():
                def make_x2(t):
                    r = RESULT["wo", 1] + t
                    dve.wait_ge(y_rstd, t + 1)
                    if t == 2:
                        dve.wait_ge(unit_used, STEP["wo", 15] + 1)
                    then(nc.vector.scalar_tensor_tensor(out=x2[:, t, S:D], in0=acc[r % 4][:, :],
                                                        scalar=rstd_y[:, t:t + 1], in1=gate_post[:, S:D],
                                                        op0=ALU.mult, op1=ALU.mult))
                    nc.vector.tensor_tensor(out=x2[:, t, S:D], in0=x2[:, t, S:D], in1=x_again[:, t, S:D], op=ALU.add)\
                        .then_inc(freed["dve"], 1)
                    nc.vector.scalar_tensor_tensor(out=x2[:, t, 0:S], in0=y_left[:, t, :], scalar=rstd_y[:, t:t + 1],
                                                   in1=x_again[:, t, 0:S], op0=ALU.mult, op1=ALU.add).then_inc(x2_made, 1)

                def gain(t):
                    dve.wait_ge(x2_made, t + 1)
                    wait_freed(dve, RESULT["wo", 1] + t)
                    nc.vector.tensor_tensor(out=x2_gain[:, t, :], in0=x2[:, t, :], in1=norm_row[:, :], op=ALU.mult)\
                        .then_inc(gain_made, 1)

                def diagonal(t):
                    dve.wait_ge(x2_rstd, t + 1)
                    nc.vector.tensor_scalar(diag[:, t, :], ident[:, :], rstd_h[:, t:t + 1], None, ALU.mult)\
                        .then_inc(diag_made, 1)

                def lower_h2(t):
                    for n in (2 * t, 2 * t + 1):
                        dve.wait_ge(h2_hi_made, n + 1)
                        half = n % 2
                        tiles = (slice(None), slice(4 * half, 4 * half + 4), slice(t * P, (t + 1) * P))
                        nc.vector.tensor_tensor(out=hT_lo[tiles], in0=side[n % 4][:, :].rearrange("p (k s) -> p k s", s=P),
                                                in1=hT_hi[tiles].bitcast(f32), op=ALU.subtract).then_inc(h2_made, 1)

                dve.wait_ge(x_again_here, 16)
                dve.wait_ge(norm_here, 16)
                make_x2(0)
                gain(0)
                make_x2(1)
                diagonal(0)
                gain(1)
                make_x2(2)
                diagonal(1)
                lower_h2(0)
                split_lo(STEP["bs", 2])
                make_x2(3)
                gain(2)
                diagonal(2)
                lower_h2(1)
                gain(3)
                diagonal(3)
                lower_h2(2)
                lower_h2(3)

            def side_slot(slot):
                for s in SCORES_AT.get(slot, []):
                    w = (s // 4 % TT + 1) * P
                    dve.wait_ge(logits_made, s + 1)
                    col = slice(s, s + 1)
                    if s < SPARSE:
                        nc.vector.tensor_reduce(out=top_neg[:, col], in_=side[s % 2][:, 0:w], axis=AX.X, op=ALU.max,
                                                negate=True).then_inc(max_made, 1)
                    else:
                        cq = cum_q[:, s - SPARSE:s - SPARSE + 1]
                        then(nc.vector.tensor_reduce(out=top_max[:, col], in_=side[s % 2][:, 0:w], axis=AX.X, op=ALU.max))
                        then(nc.vector.tensor_tensor(out=top_max[:, col], in0=top_max[:, col], in1=cq, op=ALU.add))
                        nc.vector.tensor_tensor(out=top_neg[:, col], in0=cq, in1=top_max[:, col], op=ALU.subtract)\
                            .then_inc(max_made, 1)
                for s in SCORES_AT.get(slot, []):
                    w = (s // 4 % TT + 1) * P
                    dve.wait_ge(exp_made, s + 1)
                    then(nc.vector.reciprocal(row_inv[:, s:s + 1], row_sum[:, s:s + 1]))
                    nc.vector.tensor_scalar(probs[:, s % 2, 0:w], probs[:, s % 2, 0:w], row_inv[:, s:s + 1], None, ALU.mult)\
                        .then_inc(probs_made, 1)

            def topk_round(t, r):
                w = (t + 1) * P
                sc = score[:, t - 1, 0:w]
                if r == 0:
                    dve.wait_ge(cut_made, t)
                then(nc.vector.max(top8, sc))
                then(nc.vector.match_replace(sc, top8, sc, TAKEN))
                if r == ROUNDS - 1:
                    nc.vector.tensor_scalar(sel_of[t], sc, (OUTSIDE + TAKEN) / 2, NEG, ALU.is_gt, ALU.mult)\
                        .then_inc(sel_made, 1)

            def make_constants():
                dve.wait_ge(consts, 8)
                nc.vector.tensor_copy(ident16[:, :], ident[:, :])
                nc.vector.tensor_copy(pick[:, :], pick_f[0:36, :]).then_inc(pick_made, 1)
                then(nc.vector.tensor_scalar(idx[:, 1, :], idx[:, 1, :], C - 1, None, ALU.bitwise_and))
                then(nc.vector.tensor_tensor(out=later[:, :], in0=idx[:, 0, :], in1=idx[:, 1, :], op=ALU.is_gt))
                then(nc.vector.tensor_tensor(out=idx[:, 0, :], in0=idx[:, 0, :], in1=idx[:, 1, :], op=ALU.bitwise_xor))
                nc.vector.tensor_scalar(level_mask[:, NL - 1, :], idx[:, 0, :], 0, None, ALU.is_equal)
                then(nc.vector.tensor_tensor(out=later[:, :], in0=idx[:, 0, :], in1=later[:, :], op=ALU.mult))
                for l, half in enumerate(LEVELS[:-1]):
                    then(nc.vector.tensor_scalar(junk[:, 0:C], later[:, :], float(half), None, ALU.is_ge))
                    then(nc.vector.scalar_tensor_tensor(out=level_mask[:, l, :], in0=later[:, :], scalar=float(2 * half),
                                                        in1=junk[:, 0:C], op0=ALU.is_lt, op1=ALU.mult))
                for r in range(16):
                    nc.vector.memset(inv_count[:, r:r + 1], 1.0 / (r + 1))
                dve.wait_ge(lb_exp, 1)
                then(nc.vector.reciprocal(tmp8, one_low))
                then(nc.vector.tensor_tensor(out=one_low, in0=one_low, in1=tmp8, op=ALU.mult))
                then(nc.vector.tensor_tensor(out=low_b, in0=one_low, in1=one_low, op=ALU.subtract))
                then(nc.vector.tensor_scalar(one_low, low_b, -1.0, 1.0, ALU.mult, ALU.add))

            dve.wait_ge(consts, 2)
            dve.wait_ge(par_here, 16)
            nc.vector.tensor_tensor(out=low_b, in0=par[:, PAR["lb"]], in1=par[:, PAR["lb"]], op=ALU.subtract)\
                .then_inc(lb_diff, 1)
            dve.wait_ge(c_exp, 1)
            then(nc.vector.tensor_scalar(tmp8, tmp8, 1.0, None, ALU.add))
            then(nc.vector.reciprocal(tmp8, tmp8))
            then(nc.vector.tensor_tensor(out=silu_c, in0=tmp8, in1=par[:, PAR["c"]], op=ALU.mult))
            for t in range(TT):
                dve.wait_ge(x_rstd, t + 1)
                nc.vector.tensor_scalar(x_diag[:, t, :], ident[:, :], rstd[:, t:t + 1], None, ALU.mult)\
                    .then_inc(x_diag_made, 1)
            sum_modulation(0, 0)
            sum_modulation(0, 1)
            for kt in range(3, 7):
                dve.wait_ge(xT_made, kt + 1)
                nc.vector.tensor_copy(hT_full[:, kt, :], (acc + side)[kt][:, :]).then_inc(xT_taken, 1)
            modulate(0)
            lower_h(0)
            sum_modulation(1, 0)
            sum_modulation(1, 1)

            gates = 0
            finals = [0]
            before = (None, 0)
            for k, (kind, j) in enumerate(USED):
                if k + 1 < KT:
                    modulate(k + 1)
                    if k + 2 < KT:
                        sum_modulation(k + 2, 0)
                    lower_h(k + 1)
                    if k + 2 < KT:
                        sum_modulation(k + 2, 1)
                elif (kind, j) != ("wo", 15):
                    if k == KT - 1:
                        dve.wait_ge(lo_made, KT)
                    for later_k in to_split(k):
                        split_lo(later_k)
                if before[0] in ("gp", "gh") and (kind, j) != ("wo", 0):
                    finish_gate(gates - 1, RESULT[before], silu_out[:, before[1] % 2, :])
                if before[0] == "dz":
                    finish_gate(gates - 1, RESULT[before], z_d[:, before[1], :])
                if before[0] in ("az", "bz", "cz"):
                    if finals[0]:
                        dve.wait_ge(y_made, finals[0])
                    finish_gate(gates - 1, RESULT[before], y_tmp[:, :])
                    dve.wait_ge(freed["dve"], FREED[RESULT[before]][1])
                    end_tile(y_tmp[:, :], y_raw)
                if k == D_FINAL_AT:
                    dve.wait_ge(bank3_read, 2 * TT)
                    for h in range(4):
                        end_tile(z_d[:, h, :], y_raw)
                before = (kind, j)
                if (kind, j % 2) == ("gp", 1):
                    g, w = j // 2, 2 << (j // 2)
                    total, diff = sums[g % 2], sums[(g + 1) % 2][:, :, 0:S]
                    dve.wait_ge(sum_made, g + 1)
                    then(nc.vector.scalar_tensor_tensor(out=diff, in0=total[:, :, 16:], scalar=1.0 / w,
                                                        in1=u_pad[:, :, 16:], op0=ALU.mult, op1=ALU.subtract))
                    then(nc.vector.tensor_tensor(out=diff[:, :, 0:w - 1], in0=total[:, :, 16:15 + w],
                                                 in1=inv_count[:, 0:w - 1].unsqueeze(1).broadcast_to([P, 2, w - 1]),
                                                 op=ALU.mult))
                    nc.vector.tensor_tensor(out=diff[:, :, 0:w - 1], in0=diff[:, :, 0:w - 1],
                                            in1=u_pad[:, :, 16:15 + w], op=ALU.subtract).then_inc(d_made, 1)
                m = LEVEL_AT.get((kind, j))
                if m is not None:
                    scale_level(m)
                    diff_level(dve, nc.vector, m + 1)
                    if m:
                        copy_level(m - 1)
                for h in gates_in(k - 1):
                    log_sum(h)
                for h in gates_in(k):
                    dve.wait_ge(f_sig, h + 1)
                    then(nc.vector.tensor_scalar(b_cum[:, h, :], b_cum[:, h, :], one_low[:, h:h + 1], low_b[:, h:h + 1],
                                                 ALU.mult, ALU.add))
                    nc.vector.tensor_scalar(keys[:, h, :], b_cum[:, h, :], -1.0, 1.0, ALU.mult, ALU.add).then_inc(f_made, 1)
                if (kind, j) == ("fk", KT - 2):
                    make_constants()
                for h in range(HEADS - 1) if (kind, j) == ("fk", KT - 1) else [7] if kind == "f" else []:
                    if h in range(4, 7):
                        dve.wait_ge(side_f_read, h - 3)
                    else:
                        wait_freed(dve, RESULT["f", 7] if h == 7 else RESULT["fk", 0] + h)
                    nc.vector.tensor_scalar(b_cum[:, h, :], b_cum[:, h, :], 1.0, 1.0e19, ALU.add, ALU.min).then_inc(f_bound, 1)
                if (kind, j) == ("q", 7):
                    wait_freed(dve, RESULT["q", 7])
                    dve.wait_ge(b_made, HEADS)
                    dve.wait_ge(f_made, HEADS)
                    diff_level(dve, nc.vector, 0)
                if (kind, j % 2) == ("gp", 1):
                    dve.wait_ge(d_hi_made, g + 1)
                    dve.wait_ge(d_made, g + 1)
                    nc.vector.tensor_tensor(out=d_lo[:, :, :], in0=diff, in1=d_hi[:, :, :].bitcast(f32),
                                            op=ALU.subtract).then_inc(d_lo_made, 1)
                if kind in GATES:
                    bound_gate(gates)
                    gates += 1
                    if (kind, j) == ("gh", 7):
                        finish_gate(gates - 1, RESULT["gh", 7], silu_out[:, j % 2, :])
                if kind == "pw":
                    dve.wait_ge(unit_used, k + 1)
                    wait_freed(dve, RESULT["gp", 2 * j + 1])
                    for o in range(2):
                        r = RESULT["pw", j] + o
                        nc.vector.scalar_tensor_tensor(out=mix_pool[:, 2 * j + o, :], in0=acc[r % 4][:, :],
                                                       scalar=par[:, PAR["pool_scale"]][:, 2 * j + o:2 * j + o + 1],
                                                       in1=silu_out[:, o, :], op0=ALU.mult, op1=ALU.mult)\
                            .then_inc(freed["dve"], 1)
                if (kind, j) == ("i", 7):
                    copy_level(4 * NL - 1)
                    prepare_head(0)
                n = HEAD_AT.get((kind, j))
                if n is not None:
                    if n + 1 < HEADS:
                        prepare_head(n + 1)
                    if n < HEADS:
                        chain_states(n)
                    if n:
                        finish_head(n - 1)
                if kind == "gh":
                    dve.wait_ge(mixp_hi_made, j + 1)
                    nc.vector.tensor_tensor(out=mixp_lo[:, j, :], in0=mix_pool[:, j, :],
                                            in1=mixp_hi[:, j, :].bitcast(f32), op=ALU.subtract).then_inc(mixp_made, 1)
                if (kind, j) == ("wo", 10):
                    dve.wait_ge(gate_summed, 2)
                    dve.wait_ge(rows_here, 32)
                    for o in range(2):
                        half = slice(o * S, (o + 1) * S)
                        then(nc.vector.tensor_tensor(out=gate_row[:, half], in0=side[1 + o][:, :], in1=gate_row[:, half],
                                                     op=ALU.add))
                        then(nc.vector.tensor_tensor(out=gate_post[:, half], in0=gate_row[:, half], in1=post_row[:, half],
                                                     op=ALU.mult))
                    wait_freed(dve, RESULT["wo", 0] + TT - 1)
                    nc.vector.tensor_scalar(ss_y[:, 8:12], ss_y[:, 0:4], 1.0 / D, EPS, ALU.mult, ALU.add)\
                        .then_inc(y_bias_made, 1)
                    for t in range(TT):
                        then(nc.vector.tensor_tensor(out=y_left[:, t, :], in0=y_left[:, t, :], in1=gate_post[:, 0:S],
                                                     op=ALU.mult))
                if (kind, j) == ("wo", 15):
                    enter_second_block()
                r = RESULT.get((kind, j))
                if (kind, j) == ("bs", 3):
                    dve.wait_ge(small_rows, 32)
                    dve.wait_ge(lat_rstd, 1)
                    for twice in range(2):
                        then(nc.vector.tensor_copy(key_twice[:, :, 64 * twice:64 * twice + 64], side_tok[:, :, 384:448]))
                    for t in range(TT):
                        ins = nc.vector.scalar_tensor_tensor(out=lat[:, t, :], in0=side_tok[:, t, 0:P],
                                                             scalar=rstd_kv[:, t:t + 1], in1=kv_row[:, :],
                                                             op0=ALU.mult, op1=ALU.mult)
                        ins.then_inc(lat_made, 1)
                    nc.vector.tensor_copy(forget_tok.rearrange("p (t h) -> p t h", h=4), side_tok[:, :, 452:456])
                    then(nc.vector.tensor_scalar(idx_w.rearrange("p (t h) -> p t h", h=4), side_tok[:, :, 448:452], 0.5,
                                                 None, ALU.mult))
                if kind == "bq" and j:
                    w = (j + 1) * P
                    for h in range(4):
                        n = 4 * (j - 1) + h
                        dve.wait_ge(relu_made, n + 1)
                        if h:
                            dve.wait_ge(relu_used, n)
                        weight = idx_w[:, 4 * j + h:4 * j + h + 1]
                        sc = score[:, j - 1, 0:w]
                        if h == 0:
                            ins = nc.vector.tensor_scalar(sc, relu[:, n % 2, 0:w], weight, None, ALU.mult)
                        else:
                            ins = nc.vector.scalar_tensor_tensor(out=sc, in0=relu[:, n % 2, 0:w], scalar=weight, in1=sc,
                                                                 op0=ALU.mult, op1=ALU.add)
                        ins.then_inc(relu_used, 1)
                if (kind, j) == ("av", 3):
                    for t in range(TT):
                        wait_freed(dve, RESULT["av", 0] + t)
                        then(nc.vector.bn_stats(bn[:, 6 * t:6 * t + 6], v_norm[:, t, :]))
                    for t in range(TT):
                        ins = nc.vector.bn_aggr(bn_mean[:, 2 * t:2 * t + 2], bn[:, 6 * t:6 * t + 6])
                    ins.then_inc(bn_made, 1)
                    dve.wait_ge(bn_made, 1)
                    dve.wait_ge(bn_rstd, 1)
                    dve.wait_ge(spatial_here, 64)
                if kind == "au" and j < 2:
                    for t in (2 * j, 2 * j + 1):
                        then(nc.vector.scalar_tensor_tensor(out=v_norm[:, t, :], in0=v_norm[:, t, :],
                                                            scalar=bn_mean[:, 2 * t:2 * t + 1], in1=ln_rows[:, 0, :],
                                                            op0=ALU.subtract, op1=ALU.mult))
                        nc.vector.scalar_tensor_tensor(out=v_norm[:, t, :], in0=v_norm[:, t, :],
                                                       scalar=rstd_v[:, t:t + 1], in1=ln_rows[:, 1, :],
                                                       op0=ALU.mult, op1=ALU.add).then_inc(v_made, 1)
                if kind == "cx":
                    wait_freed(dve, RESULT["cc", j])
                    dve.wait_ge(unit_used, k + 1)
                    if j == 0:
                        then(nc.vector.memset(conv_in[:, 0:2], 0.0))
                    nc.vector.tensor_tensor(out=conv_in[:, 2:], in0=acc[r % 4][:, :], in1=c_gate[:, :], op=ALU.mult)\
                        .then_inc(freed["dve"], 1)
                    wait_freed(dve, r)
                    taps = par[:, PAR["conv_w"]]
                    then(nc.vector.tensor_scalar(conv[:, :], conv_in[:, 0:S], taps[:, j:j + 1], None, ALU.mult))
                    for tap in (1, 2):
                        then(nc.vector.scalar_tensor_tensor(out=conv[:, :], in0=conv_in[:, tap:tap + S],
                                                            scalar=taps[:, 4 * tap + j:4 * tap + j + 1], in1=conv[:, :],
                                                            op0=ALU.mult, op1=ALU.add))
                if kind == "cb":
                    dve.wait_ge(unit_used, k + 1)
                    nc.vector.tensor_tensor(out=y_raw["c"][:, j, :], in0=acc[r % 4][:, :], in1=conv[:, :], op=ALU.mult)\
                        .then_inc(freed["dve"], 1)
                slot = k - SLOT0
                side_slot(slot)
                if slot in MIXED_AT:
                    g = MIXED_AT[slot]
                    dve.wait_ge(mixed_made, g + 1)
                    wait_freed(dve, RESULT["au", g])
                    nc.vector.tensor_tensor(out=y_tmp2.rearrange("p (c t) -> p c t", t=P),
                                            in0=side[g % 2][:, :].rearrange("p (c t) -> p c t", t=P),
                                            in1=mix_b[:, g, :].unsqueeze(1).broadcast_to([P, TT, P]), op=ALU.add)\
                        .then_inc(mixed_read, 1)
                    dve.wait_ge(mixed_read, g + 1)
                    then(nc.vector.tensor_tensor(out=y_raw["a"][:, g, :], in0=y_raw["a"][:, g, :], in1=y_tmp2, op=ALU.mult))
                if slot == FORGET_AT:
                    dve.wait_ge(fgt_made, 1)
                    then(nc.vector.memset(forget_r[:, :].bitcast(f32), 0.0))
                    then(nc.vector.tensor_scalar(forget[:, 0, :], side[0][0:4, :], bf_col[0:4, :], None, ALU.add))
                    then(nc.vector.tensor_scalar(forget[:, 1, :], forget[:, 0, :], -1.0, None, ALU.mult))
                    nc.vector.tensor_tensor(out=forget[:, 1, :], in0=forget[:, 0, :], in1=forget[:, 1, :], op=ALU.max)\
                        .then_inc(fgt_abs, 1)
                    dve.wait_ge(fgt_abs, 1)
                    then(nc.vector.tensor_scalar(forget[:, 0, :], forget[:, 0, :], 0.0, None, ALU.min))
                    dve.wait_ge(fgt_ln, 1)
                    then(nc.vector.tensor_tensor(out=forget[:, 0, :], in0=forget[:, 0, :], in1=forget[:, 1, :],
                                                 op=ALU.subtract))
                    then(nc.vector.memset(forget[:, 1, :], 1.0))
                    nc.vector.tensor_tensor_scan(out=forget[:, 0, :], data0=forget[:, 1, :], data1=forget[:, 0, :],
                                                 initial=0.0, op0=ALU.mult, op1=ALU.add).then_inc(fgt_sum, 1)
                    dve.wait_ge(fgt_sum, 1)
                    dve.wait_ge(fgt_hi, 1)
                    then(nc.vector.tensor_tensor(out=forget[:, 1, :], in0=forget[:, 0, :],
                                                 in1=forget_r[0:4, :].bitcast(f32), op=ALU.add))
                    nc.vector.tensor_scalar(forget_r[32:36, :], forget[:, 1, :], -1.0, None, ALU.mult).then_inc(fgt_ready, 1)
                if slot == CUM_AT:
                    dve.wait_ge(cum_made, 1)
                    nc.vector.tensor_copy(cum_q, side[1][:, 0:16]).then_inc(cum_read, 1)
                for t, rr in topk_rounds(slot):
                    topk_round(t, rr)
                if kind == "br":
                    dve.wait_ge(unit_used, k + 1)
                    for o in range(2):
                        g = 2 * j + o
                        wait_freed(dve, RESULT["ga", g])
                        first = g % 4 == 0
                        if first and j >= 2:
                            dve.wait_ge(m_made, j // 2)
                        dst = merged[:, :] if first else merged_part[:, :]
                        nc.vector.tensor_tensor(out=dst, in0=acc[(r + o) % 4][:, :], in1=sig[:, g % 2, :], op=ALU.mult)\
                            .then_inc(freed["dve"], 1)
                        wait_freed(dve, r + o)
                        if not first:
                            ins = nc.vector.tensor_tensor(out=merged[:, :], in0=merged[:, :], in1=merged_part[:, :],
                                                          op=ALU.add)
                            if g % 4 == 3:
                                ins.then_inc(m_sum, 1)
                            else:
                                then(ins)
                    if j % 2:
                        dve.wait_ge(m_sum, j // 2 + 1)
                        dve.wait_ge(m_hi_made, j // 2 + 1)
                        nc.vector.tensor_tensor(out=m_lo[:, j // 2, :], in0=merged[:, :],
                                                in1=m_hi[:, j // 2, :].bitcast(f32), op=ALU.subtract).then_inc(m_made, 1)
                if (kind, j) == ("w2", 3):
                    dve.wait_ge(unit_used, k + 1)
                    for t in range(TT):
                        r = RESULT["w2", 0] + t
                        nc.vector.tensor_tensor(out=x2[:, t, 0:S], in0=acc[r % 4][:, :], in1=x2[:, t, 0:S],
                                                op=ALU.add).then_inc(freed["dve"], 1)
                if (kind, j) == ("w2", 4):
                    dve.wait_ge(h_sq, 4)
                    dve.wait_ge(final_here, 16)
                    nc.vector.tensor_scalar(rstd_o[:, 4:8], ss_o[:, 0:4], 1.0 / D, EPS, ALU.mult, ALU.add)
                    for t in range(TT):
                        wait_freed(dve, RESULT["w2", 0] + t)
                        ins = nc.vector.tensor_tensor(out=x2[:, t, 0:S], in0=x2[:, t, 0:S], in1=final_row[:, 0:S],
                                                      op=ALU.mult)
                    ins.then_inc(left_scaled, 1)
                if (kind, j) == ("w2", 7):
                    def finish_right(t):
                        dve.wait_ge(h_rstd, t + 1)
                        nc.vector.scalar_tensor_tensor(out=x2[:, t, S:D], in0=x2[:, t, S:D], scalar=rstd_o[:, t:t + 1],
                                                       in1=final_row[:, S:D], op0=ALU.mult, op1=ALU.mult)\
                            .then_inc(out_made, 1)

                    for t in range(TT):
                        r = RESULT["w2", 1] + t
                        if t < TT - 1:
                            dve.wait_ge(out_tiles_made, t + 1)
                        else:
                            dve.wait_ge(unit_used, k + 1)
                        nc.vector.tensor_tensor(out=x2[:, t, S:D], in0=acc[r % 4][:, :], in1=x2[:, t, S:D],
                                                op=ALU.add).then_inc(freed["dve"], 1)
                        if t:
                            finish_right(t - 1)
                    finish_right(TT - 1)

        @block.tensor
        def _(pe):
            def weights(k, first=True):
                if first:
                    pe.wait_ge(lo_made, k + 1)
                return w_hi[:, k % SPLITS, :], w_lo[:, k % SPLITS, :]

            def bank(result):
                if result >= 4:
                    wait_freed(pe, result - 4)
                return acc[result % 4]

            def product(ps, w, x, first, last):
                nc.tensor.matmul(ps, w[0], x[0], start=first, stop=False)
                nc.tensor.matmul(ps, w[0], x[1], start=False, stop=False)
                return nc.tensor.matmul(ps, w[1], x[0], start=False, stop=last)

            def panel(k, kind, j):
                hi, lo = weights(k)
                ps = bank(RESULT[kind, j])
                for kt in range(KT):
                    cols = slice(kt * P, (kt + 1) * P)
                    ins = product(ps[:, :], (hi[:, cols], lo[:, cols]), (hT_hi[:, kt, :], hT_lo[:, kt, :]),
                                  kt == 0, kt == KT - 1)
                ins.then_inc(unit_used, 1)

            def token_units(k, kind, j, source, width, x_ready=None, tile_made=None):
                per, count = TOKEN_UNITS[kind], TOGETHER.get((kind, j), 1)
                for t in range(TT):
                    r = RESULT[kind, j // per] + t
                    tok = slice(t * P, (t + 1) * P)
                    if x_ready is not None:
                        x_ready(t)
                    for i in range(count - 1, -1, -1):
                        hi, lo = weights(k - i, t == 0)
                        first, last = (j - i) % per == 0, (j - i) % per == per - 1
                        ps = bank(r) if first else acc[r % 4]
                        for a in range(2):
                            x = source(2 * ((j - i) % per) + a)
                            cols = slice(a * width, (a + 1) * width)
                            ins = product(ps[:, 0:width], (x[0][:, tok], x[1][:, tok]), (hi[:, cols], lo[:, cols]),
                                          first and a == 0, last and a == 1)
                    if tile_made is not None and t < TT - 1:
                        ins.then_inc(tile_made, 1)
                ins.then_inc(unit_used, count)

            def level_scores(m):
                g = m // NL
                if LEVELS[m % NL]:
                    pe.wait_ge(level_x, pair_levels(m))
                if m >= 2:
                    pe.wait_ge(level_copied, m - 1)
                half = LEVELS[m % NL]
                for h in range(2):
                    if half:
                        for c in range(0, NC, 2):
                            both = xq[:, m % 2, h * S + c * C:h * S + (c + 2) * C]
                            n0 = (h * NC + c) * C // 2
                            ins = nc.tensor.matmul(side[m % 2][:, n0:n0 + C], both, level_view(both, half)[:, :, half:],
                                                   start=True, stop=True)
                        continue
                    for c in range(NC):
                        left, right = (t[:, 2 * g + h, c * C:(c + 1) * C] for t in (keys, queries))
                        p0, n0 = (c % 2) * C, h * (S // 2) + (c // 2) * C
                        ins = nc.tensor.matmul(side[m % 2][p0:p0 + C, n0:n0 + C], left, right, start=True, stop=True)
                ins.then_inc(scores_made, 1)

            def transpose_keys(n):
                pe.wait_ge(prep_made, n + 1)
                if n >= 2:
                    pe.wait_ge(o_rstd, n - 1)
                elif n == 0:
                    pe.wait_ge(level_copied, 4 * NL)
                for t in range(TT):
                    ins = nc.tensor.transpose(side[0][:, t * P:(t + 1) * P], k_dec[:, t * P:(t + 1) * P], ident[:, :])
                ins.then_inc(kT_made, 1)

            def outer_products(n):
                pe.wait_ge(kT_copied, n + 1)
                if n:
                    pe.wait_ge(states_made, n)
                for c in range(NC - 1):
                    rows = slice((c % 2) * C, (c % 2 + 1) * C)
                    ins = nc.tensor.matmul(side[1 + c % 2][:, (c // 2) * P:(c // 2 + 1) * P], k_decT[rows, c // 2, :],
                                           values[rows, c // 2, n * P:(n + 1) * P], start=True, stop=True)
                ins.then_inc(outer_made, 1)

            def head_output(n):
                pe.wait_ge(states_made, n + 1)
                if n:
                    pe.wait_ge(o_squared, n)
                for c in range(1, NC):
                    cols = slice(c * C, (c + 1) * C)
                    nc.tensor.matmul(side[3][:, cols], states[:, c - 1, :], q_dec[:, n % 2, cols],
                                     start=(c == 1), stop=False)
                for parity in range(2):
                    if parity:
                        even.then_inc(even_made, 1)
                        pe.wait_ge(even_made, n + 1)
                    rows = slice(parity * C, (parity + 1) * C)
                    for c in range(parity, NC, 2):
                        ins = nc.tensor.matmul(side[3][:, c * C:(c + 1) * C], values[rows, c // 2, n * P:(n + 1) * P],
                                               attn[rows, n, (c // 2) * C:(c // 2 + 1) * C], start=False,
                                               stop=(c == NC - 1))
                    even = ins
                ins.then_inc(o_made, 1)

            def head_mean_squares(n):
                pe.wait_ge(o_squared, n + 1)
                nc.tensor.matmul(side[0][:, :], ones[:, :], o_sq[:, :], start=True, stop=True).then_inc(ms_made, 1)

            def transpose_x2(t):
                pe.wait_ge(gain_made, t + 1)
                pe.wait_ge(diag_made, t + 1)
                for n in (2 * t, 2 * t + 1):
                    if n >= 4:
                        pe.wait_ge(h2_made, n - 3)
                    for i in range(4):
                        kt = 4 * (n % 2) + i
                        ins = nc.tensor.matmul(side[n % 4][:, i * P:(i + 1) * P], x2_gain[:, t, kt * P:(kt + 1) * P],
                                               diag[:, t, :], start=True, stop=True)
                    ins.then_inc(x2T_made, 1)

            def h2_tile(t):
                if t == 0:
                    transpose_x2(0)
                if t < TT - 1:
                    transpose_x2(t + 1)
                pe.wait_ge(h2_made, 2 * t + 2)

            def turn(s):
                n = BANK2.index(("turn", s))
                pe.wait_ge(probs_made, s + 1)
                if n:
                    pe.wait_ge(bank2_read, n)
                for b in range(s // 4 % TT + 1):
                    ins = nc.tensor.transpose(side[2][:, b * P:(b + 1) * P], probs[:, s % 2, b * P:(b + 1) * P], ident[:, :])
                ins.then_inc(turned, 1)

            def sum_values(s):
                n = BANK2.index(("turn", s))
                pe.wait_ge(bank2_read, n + 1)
                h, blocks = s % 4, s // 4 % TT + 1
                if h == 0 and s:
                    pe.wait_ge(bank3_read, s // 4)
                if s == SPARSE:
                    wait_freed(pe, RESULT["dv", 0] + 3)
                for b in range(blocks):
                    v = lat[:, b, :] if s < SPARSE else fox_v[:, b, h * P:(h + 1) * P]
                    ins = nc.tensor.matmul(side[3][:, h * P:(h + 1) * P], v, probsT[:, s % 2, b * P:(b + 1) * P],
                                           start=(b == 0), stop=(b == blocks - 1))
                ins.then_inc(summed, 1)

            def logits(s):
                q, h = s // 4 % TT, s % 4
                w = (q + 1) * P
                ps = side[s % 2]
                tok = slice(q * P, (q + 1) * P)
                if s >= 2:
                    pe.wait_ge(exp_made, s - 1)
                if s < SPARSE:
                    if s == 0:
                        pe.wait_ge(latq_copied, 4)
                    if q:
                        pe.wait_ge(sel_made, q)
                    nc.tensor.matmul(ps[:, 0:w], lat_q[:, h, tok], latT[:, 0:w], start=True, stop=False)
                    bias = sel_of[q] if q else causal16[:, :]
                    ins = nc.tensor.matmul(ps[:, 0:w], ident16[:, :], bias, start=False, stop=True)
                else:
                    if s == SPARSE:
                        wait_freed(pe, RESULT["dk", 3])
                        pe.wait_ge(fgt_ready, 1)
                        pe.wait_ge(cum_read, 1)
                    nc.tensor.matmul(ps[:, 0:w], fox_q[:, h, tok], fox_k[:, h, 0:w], start=True, stop=False)
                    nc.tensor.matmul(ps[:, 0:w], pick[:, h:h + 1].broadcast_to([36, P]), forget_r[:, 0:w],
                                     start=False, stop=False)
                    ins = nc.tensor.matmul(ps[:, w - P:w], ident16[:, :], causal16[:, :], start=False, stop=True)
                ins.then_inc(logits_made, 1)

            def side_slot(slot):
                turns, sums_, scores_ = TURN_AT.get(slot, []), SUM_AT.get(slot, []), SCORES_AT.get(slot, [])
                for i in range(max(len(turns), len(sums_), len(scores_))):
                    if i < len(turns):
                        turn(turns[i])
                    if i < len(sums_):
                        sum_values(sums_[i])
                    if i < len(scores_):
                        if scores_[i] in (4, 5):
                            pe.wait_ge(mixed_read, scores_[i] - 1)
                        logits(scores_[i])
                if slot in UP_AT:
                    q = UP_AT[slot]
                    n = BANK2.index(("up", q))
                    pe.wait_ge(bank2_read, n)
                    pe.wait_ge(bank3_read, q + 1)
                    for h in range(4):
                        ins = nc.tensor.matmul(side[2][:, h * P:(h + 1) * P], w_up[:, 1, h, :],
                                               lat_out[:, h * P:(h + 1) * P], start=True, stop=True)
                    ins.then_inc(turned, 1)
                if slot in MIXED_AT:
                    g = MIXED_AT[slot]
                    pe.wait_ge(v_made, TT)
                    pe.wait_ge(masked, 1)
                    if g >= 2:
                        pe.wait_ge(mixed_read, g - 1)
                    pe.wait_ge(exp_made, 4)
                    for t in range(TT):
                        ins = nc.tensor.matmul(side[g % 2][:, t * P:(t + 1) * P], v_norm[:, t, g * P:(g + 1) * P],
                                               mixT[:, g, :], start=True, stop=True)
                    ins.then_inc(mixed_made, 1)

            pe.wait_ge(consts, 2)
            for t in range(TT):
                pe.wait_ge(x_diag_made, t + 1)
                for kt in range(KT):
                    ins = nc.tensor.matmul((acc + side)[kt][:, t * P:(t + 1) * P], x_in[:, t, kt * P:(kt + 1) * P],
                                           x_diag[:, t, :], start=True, stop=True)
                    if t == TT - 1:
                        ins.then_inc(xT_made, 1)

            def sum_mod(kt):
                pe.wait_ge(ada_summed, 2 * kt + 2)
                if kt:
                    pe.wait_ge(h_full, kt)
                for o in range(2):
                    for a in range(2):
                        ins = nc.tensor.matmul(side[3][:, 8 * o + kt:8 * o + kt + 1],
                                               ada_acc[:, kt % 2, a, o * P:(o + 1) * P], ones[:, 0:1],
                                               start=(a == 0), stop=(a == 1))
                ins.then_inc(mod_summed, 1)

            pe.wait_ge(xT_copied, 1)
            sum_mod(0)
            pe.wait_ge(xT_copied, 4)
            pe.wait_ge(xT_taken, 4)

            for k, (kind, j) in enumerate(USED):
                if (kind, j) in EARLIER:
                    continue
                if kind == "fk":
                    hi, lo = weights(k)
                    pe.wait_ge(h_lo, j + 1)
                    for h in range(HEADS - 1):
                        cols = slice(h * P, (h + 1) * P)
                        ins = product((acc + side)[h][:, :], (hi[:, cols], lo[:, cols]), (hT_hi[:, j, :], hT_lo[:, j, :]),
                                      j == 0, j == KT - 1)
                        if h == 0 and j == 0:
                            sum_mod(1)
                        if h == 4 and j + 2 < KT:
                            sum_mod(j + 2)
                    ins.then_inc(unit_used, 1)
                if kind in PANELS:
                    panel(k, kind, j)
                if kind in ("i", "bs", "av", "dv"):
                    token_units(k, kind, j, lambda kt: (hT_hi[:, kt, :], hT_lo[:, kt, :]), SIDE if kind == "bs" else S,
                                x_ready=h2_tile if (kind, j) == ("bs", 2) else None)
                if kind == "br":
                    hi, lo = weights(k)
                    for o in range(2):
                        name = "abcd"[2 * (j % 2) + o]
                        pe.wait_ge(y_made, 1 + FINAL.index((name, 3)))
                        ps = bank(RESULT[kind, j] + o)
                        for kt in range(4):
                            cols = slice((4 * o + kt) * P, (4 * o + kt + 1) * P)
                            ins = product(ps[:, :], (hi[:, cols], lo[:, cols]),
                                          (y_hi[name][:, kt, :], y_lo[name][:, kt, :]), kt == 0, kt == 3)
                    ins.then_inc(unit_used, 1)
                if kind == "w2":
                    pe.wait_ge(m_made, 2 * (j % 4) + 2)
                    token_units(k, kind, j, lambda kt: (m_hi[:, kt, :], m_lo[:, kt, :]), S,
                                tile_made=out_tiles_made if j == 7 else None)
                if kind == "pw":
                    pe.wait_ge(d_lo_made, j + 1)
                    hi, lo = weights(k)
                    for o in range(2):
                        ps = bank(RESULT[kind, j] + o)
                        for a in range(2):
                            cols = slice(a * 256 + o * P, a * 256 + (o + 1) * P)
                            ins = product(ps[:, :], (hi[:, cols], lo[:, cols]), (d_hi[:, a, :], d_lo[:, a, :]),
                                          a == 0, a == 1)
                    ins.then_inc(unit_used, 1)
                if kind == "wo":
                    ktp = j % 8
                    if ktp < 4:
                        pe.wait_ge(mixp_made, 2 * ktp + 2)
                    else:
                        pe.wait_ge(mixh_made, 2 * ktp - 6)
                    token_units(k, kind, j, lambda kt: (mixp_hi[:, kt, :], mixp_lo[:, kt, :]) if kt < KT else
                                (mixh_hi[:, kt - KT, :], mixh_lo[:, kt - KT, :]), S,
                                tile_made=y_tiles_made if j == 15 else None)
                if (kind, j) in LEVEL_AT:
                    level_scores(LEVEL_AT[kind, j])
                n = HEAD_AT.get((kind, j))
                if n is not None:
                    if n < HEADS:
                        transpose_keys(n)
                    if n:
                        head_output(n - 1)
                    if n < HEADS:
                        outer_products(n)
                    if n:
                        head_mean_squares(n - 1)
                if (kind, j) == ("wo", 8):
                    pe.wait_ge(ada_summed, 24)
                    for o in range(2):
                        nc.tensor.matmul(side[1 + o][:, :], ones[:, :], gate_post[:, o * S:(o + 1) * S],
                                         start=True, stop=True).then_inc(gate_summed, 1)
                if (kind, j) == ("bq", 0):
                    pe.wait_ge(lat_made, TT)
                    for t in range(TT):
                        for n, src in enumerate((lat[:, t, :], side_tok[:, t, P:2 * P], side_tok[:, t, 2 * P:3 * P],
                                                 key_twice[:, t, :])):
                            ins = nc.tensor.transpose(side[n][:, t * P:(t + 1) * P], src, ident[:, :])
                    ins.then_inc(idxT_made, 1)
                if kind == "bq" and j:
                    pe.wait_ge(idxT_copied, 4)
                    w = (j + 1) * P
                    for h in range(4):
                        if j > 1:
                            pe.wait_ge(relu_made, 4 * (j - 2) + h + 1)
                        rows = slice((h % 2) * 64, (h % 2 + 1) * 64)
                        nc.tensor.matmul(side[h][:, 0:w], idx_qT[rows, h // 2, j * P:(j + 1) * P], idx_kT[rows, 0:w],
                                         start=True, stop=True).then_inc(dots_made, 1)
                if (kind, j) == ("av", 0):
                    wait_freed(pe, RESULT["bq", 3])
                    pe.wait_ge(up_here, 32)
                    pe.wait_ge(relu_made, 12)
                    for h in range(4):
                        ins = nc.tensor.matmul(side[h][:, :], w_up[:, 0, h, :], lat_q[:, h, :], start=True, stop=True)
                    ins.then_inc(latq_made, 1)
                slot = k - SLOT0
                side_slot(slot)
                if slot == FORGET_AT:
                    pe.wait_ge(exp_made, SPARSE)
                    for t in range(TT):
                        ins = nc.tensor.transpose(side[0][0:4, t * P:(t + 1) * P], forget_tok[:, 4 * t:4 * t + 4], ident[:, :])
                    ins.then_inc(fgt_made, 1)
                if slot == CUM_AT:
                    pe.wait_ge(fgt_sum, 1)
                    for t in range(TT):
                        ins = nc.tensor.transpose(side[1][:, 4 * t:4 * t + 4], forget[:, 0, t * P:(t + 1) * P],
                                                  ident[0:4, 0:4])
                    ins.then_inc(cum_made, 1)


def kernel(**inputs):
    import numpy as _np
    import concourse.bacc as _bacc
    from concourse import mybir as _mybir
    from concourse.bass_utils import run_bass_kernel_spmd as _run

    def panels(w):
        k, n = w.shape
        return w.reshape(k // 128, 128, n // 128, 128).transpose(2, 1, 0, 3).reshape(n // 128, 128, k)

    def strips(w, n):
        k, total = w.shape
        return w.reshape(k // 256, 2, 128, total // n, n).transpose(3, 0, 2, 1, 4).reshape(-1, 128, 2 * n)

    def columns(v):
        return v.reshape(-1, 128).T

    a = {k: _np.asarray(v) for k, v in inputs.items()}
    w = a["w_in"][0]
    sec = {name: w[:, i * 1024:(i + 1) * 1024] for i, name in enumerate(("u", "gp", "q", "f", "i", "gh"))}
    arrays = {
        "x": a["x"][0],
        "ada_w": a["ada_w"][0],
        "par": _np.concatenate([
            columns(a["c"]), columns(a["ada_b"][0, :2048]), columns(a["norm_pre_w"]), columns(a["pool_scale"]),
            columns(a["hgrn_lower_bounds"]), columns(a["hgrn_norm_w"]),
            columns(a["conv_w_2"][0])], axis=1),
        "norm_g": a["norm_g_2"][0],
        "gate_b": a["ada_b"][0, 2048:],
        "post_w": a["norm_post_w"][0],
        "pw": a["pool_w"][0].reshape(4, 2, 128, 256).transpose(0, 2, 1, 3).reshape(4, 128, 512),
        "i": strips(sec["i"], 512),
        "wo": strips(a["w_out"][0], 512),
    }
    for name in ("f", "q", "u", "gp", "gh"):
        arrays[name] = panels(sec[name])
    arrays["fk"] = sec["f"][:, :896].reshape(8, 128, 896)
    arrays["ada"] = a["ada_w"][0][:, :2048].reshape(2, 4, 128, 2, 8, 128).transpose(4, 0, 2, 1, 3, 5)\
        .reshape(16, 128, 1024)
    w = a["w_in_2"][0]
    starts = _np.cumsum([0, 512, 512, 512, 512, 128 + 256 + 64 + 4, 512, 512, 512, 512, 512, 512, 512, 512, 4, 512, 4096])
    names = ("au", "av", "az", "bq", "side", "bz", "cb", "cc", "cx", "cz", "dq", "dk", "dv", "df", "dz", "ga")
    sec = {name: w[:, starts[i]:starts[i + 1]] for i, name in enumerate(names)}
    for name in ("au", "az", "bq", "bz", "cb", "cc", "cx", "cz", "dq", "dk", "dz"):
        arrays[name] = panels(sec[name])
    for name in ("av", "dv"):
        arrays[name] = strips(sec[name], 512)
    arrays["bs"] = strips(_np.concatenate([sec["side"], sec["df"]], axis=1), 456)
    arrays["ga"] = panels(sec["ga"]).reshape(4, 8, 128, 1024).transpose(1, 0, 2, 3).reshape(32, 128, 1024)
    arrays["br"] = a["w_branch_2"][0].reshape(2, 2, 4, 128, 8, 128).transpose(4, 0, 3, 1, 2, 5).reshape(16, 128, 1024)
    arrays["w2"] = strips(a["w_out_2"][0], 512)
    arrays["kv_g"] = a["dsa_kv_g_2"][0]
    arrays["b_f"] = a["fox_b_f_2"].reshape(4, 1)
    arrays["w_uk"] = a["dsa_w_uk_2"][0].transpose(2, 0, 1)
    arrays["w_uv"] = a["dsa_w_uv_2"][0].transpose(1, 0, 2)
    arrays["w_s"] = a["gm_w_s_2"][0].transpose(2, 0, 1)
    arrays["b_s"] = a["gm_b_s_2"][0].reshape(-1)
    arrays["ln_g"], arrays["ln_b"] = a["gm_ln_g_2"][0], a["gm_ln_b_2"][0]
    arrays["final_g"] = a["final_g_2"]
    nc = _bacc.Bacc("TRN2", target_bir_lowering=False, num_devices=1)
    feeds, dram = {}, {}
    for name, v in arrays.items():
        v = _np.ascontiguousarray(v)
        feeds[f"in_{name}"] = v
        dram[name] = nc.dram_tensor(f"in_{name}", v.shape, _mybir.dt.from_np(v.dtype), kind="ExternalInput").ap()
    out = nc.dram_tensor("out", (512, 1024), _mybir.dt.float32, kind="ExternalOutput").ap()
    program(nc, dram, out)
    r = _run(nc, [feeds], core_ids=[0])
    return r.results[0]["out"].reshape(1, 512, 1024)
```
